# Optimizing a Trainium2 kernel written in Bass

```python
import math
import jax, jax.numpy as jnp
from jax import lax
import numpy as np

D_MODEL = 1024
BATCH = 1
SEQ = 512
DEPTH = 2

CHUNK = 64
Q_BLOCK = 128
HEAD_DIM = 64
FOX_HEADS = 8
FOX_W = FOX_HEADS * HEAD_DIM
DIFF_HEADS = 4
DIFF_QK_W = DIFF_HEADS * 2 * HEAD_DIM
DIFF_V_DIM = 2 * HEAD_DIM
DIFF_V_W = DIFF_HEADS * DIFF_V_DIM
SWA_Q_HEADS = 8
SWA_KV_HEADS = 2
SWA_GROUP = SWA_Q_HEADS // SWA_KV_HEADS
SWA_W = SWA_Q_HEADS * HEAD_DIM
SWA_KV_W = SWA_KV_HEADS * HEAD_DIM
WINDOW = 128
WINDOW_CHUNKS = WINDOW // CHUNK
HGRN_HEADS = 4
HGRN_DIM = 128
HGRN_W = HGRN_HEADS * HGRN_DIM
D_FF = -(-8 * D_MODEL // (3 * 256)) * 256
EVEN_IN = 3 * FOX_W + FOX_HEADS + 2 * DIFF_QK_W + DIFF_V_W
EVEN_OUT = FOX_W + DIFF_V_W
ODD_IN = SWA_W + 2 * SWA_KV_W + 4 * HGRN_W
ODD_OUT = SWA_W + HGRN_W
N_EVEN = (DEPTH + 1) // 2
N_ODD = DEPTH // 2
RMS_EPS = 1e-6

kernel_name = "hybrid_fox_diff_swa_hgrn2_trunk"

def rms_norm(x, g):
    xf = x.astype(jnp.float32)
    y = xf * lax.rsqrt(jnp.mean(xf * xf, axis=-1, keepdims=True) + RMS_EPS)
    return (y * g.astype(jnp.float32)).astype(x.dtype)

def partition(t, widths):
    idx = np.cumsum(widths)[:-1].tolist()
    return jnp.split(t, idx, axis=-1)

def split_heads(t, h):
    b, s, w = t.shape
    return t.reshape(b, s, h, w // h).transpose(0, 2, 1, 3)

def merge_heads(t):
    b, h, s, d = t.shape
    return t.transpose(0, 2, 1, 3).reshape(b, s, h * d)

def to_blocks(t, size):
    b, h, s = t.shape[:3]
    t = t.reshape((b, h, s // size, size) + t.shape[3:])
    return jnp.moveaxis(t, 2, 0)

def from_blocks(t):
    nb, b, h, size = t.shape[:4]
    return jnp.moveaxis(t, 0, 2).reshape((b, h, nb * size) + t.shape[4:])

def forgetting_attention(q, k, v, log_f):
    s_len = q.shape[2]
    nb = s_len // Q_BLOCK
    scale = HEAD_DIM ** -0.5
    c = jnp.cumsum(log_f, axis=-1)
    key_pos = jnp.arange(s_len)

    def block(args):
        qb, cb, i = args
        q_pos = i * Q_BLOCK + jnp.arange(Q_BLOCK)
        s = (jnp.einsum('bhqd,bhkd->bhqk', qb, k).astype(jnp.float32) * scale
             + cb[..., :, None] - c[..., None, :])
        s = jnp.where(key_pos[None, :] <= q_pos[:, None], s, -jnp.inf)
        p = jax.nn.softmax(s, axis=-1)
        return jnp.einsum('bhqk,bhkd->bhqd', p.astype(v.dtype), v)

    out = lax.map(block, (to_blocks(q, Q_BLOCK), to_blocks(c, Q_BLOCK), jnp.arange(nb)))
    return from_blocks(out)

def differential_attention(q1, q2, k1, k2, v, lam):
    s_len = q1.shape[2]
    nb = s_len // Q_BLOCK
    scale = HEAD_DIM ** -0.5
    key_chunk = jnp.arange(s_len) // CHUNK

    def block(args):
        q1b, q2b, i = args
        q_chunk = (i * Q_BLOCK + jnp.arange(Q_BLOCK)) // CHUNK
        allowed = key_chunk[None, :] <= q_chunk[:, None]
        s1 = jnp.einsum('bhqd,bhkd->bhqk', q1b, k1).astype(jnp.float32) * scale
        s2 = jnp.einsum('bhqd,bhkd->bhqk', q2b, k2).astype(jnp.float32) * scale
        p1 = jax.nn.softmax(jnp.where(allowed, s1, -jnp.inf), axis=-1)
        p2 = jax.nn.softmax(jnp.where(allowed, s2, -jnp.inf), axis=-1)
        p = p1 - lam * p2
        return jnp.einsum('bhqk,bhkd->bhqd', p.astype(v.dtype), v)

    out = lax.map(block, (to_blocks(q1, Q_BLOCK), to_blocks(q2, Q_BLOCK), jnp.arange(nb)))
    return from_blocks(out)

def swa_sink_attention(q, k, v, sinks):
    b, _, s_len, d = q.shape
    n_c = s_len // CHUNK
    scale = HEAD_DIM ** -0.5
    shifts = list(range(WINDOW_CHUNKS - 1, -1, -1))

    def band(t):
        tc = t.reshape(b, SWA_KV_HEADS, n_c, CHUNK, d)
        parts = [jnp.pad(tc, ((0, 0), (0, 0), (sh, 0), (0, 0), (0, 0)))[:, :, :n_c] for sh in shifts]
        return jnp.concatenate(parts, axis=3)

    kb, vb = band(k), band(v)
    slot_shift = np.repeat(np.array(shifts), CHUNK)
    valid = (jnp.arange(n_c)[:, None] - slot_shift[None, :]) >= 0
    qc = q.reshape(b, SWA_KV_HEADS, SWA_GROUP, n_c, CHUNK, d)
    s = jnp.einsum('bhgcqd,bhckd->bhgcqk', qc, kb).astype(jnp.float32) * scale
    s = jnp.where(valid[:, None, :], s, -jnp.inf)
    sink = jnp.broadcast_to(
        sinks.astype(jnp.float32).reshape(1, SWA_KV_HEADS, SWA_GROUP, 1, 1, 1),
        s.shape[:-1] + (1,))
    p = jax.nn.softmax(jnp.concatenate([s, sink], axis=-1), axis=-1)[..., :-1]
    o = jnp.einsum('bhgcqk,bhckd->bhgcqd', p.astype(v.dtype), vb)
    return o.reshape(b, SWA_Q_HEADS, s_len, d)

def hgrn2_recurrence(q, k, v, log_f):
    b, h, _, dk = q.shape
    dv = v.shape[-1]
    xs = (to_blocks(q, CHUNK), to_blocks(k, CHUNK), to_blocks(v, CHUNK), to_blocks(log_f, CHUNK))
    causal = jnp.tril(jnp.ones((CHUNK, CHUNK), dtype=bool))

    def step(state, inp):
        qc, kc, vc, gc = inp
        bcum = jnp.cumsum(gc, axis=-2)
        inter = jnp.einsum('bhtk,bhkv->bhtv', qc * jnp.exp(bcum), state)
        rel = bcum[:, :, :, None, :] - bcum[:, :, None, :, :]
        decay = jnp.exp(jnp.where(causal[:, :, None], rel, -jnp.inf))
        scores = jnp.einsum('bhtk,bhtsk,bhsk->bhts', qc, decay, kc)
        intra = jnp.einsum('bhts,bhsv->bhtv', scores, vc)
        b_last = bcum[:, :, -1:, :]
        new_state = (jnp.exp(b_last[:, :, 0, :])[..., None] * state
                     + jnp.einsum('bhsk,bhsv->bhkv', kc * jnp.exp(b_last - bcum), vc))
        return new_state, inter + intra

    s0 = jnp.zeros((b, h, dk, dv), jnp.float32)
    _, ys = lax.scan(step, s0, xs)
    return from_blocks(ys)

def even_mixer(h, w_in, b_forget, lq1, lk1, lq2, lk2, diff_norm, w_out, lambda_init):
    proj = h @ w_in
    qa, ka, va, fa, qb, kb, vb = partition(
        proj, [FOX_W, FOX_W, FOX_W, FOX_HEADS, DIFF_QK_W, DIFF_QK_W, DIFF_V_W])
    log_f = jax.nn.log_sigmoid((fa + b_forget).astype(jnp.float32)).transpose(0, 2, 1)
    oa = forgetting_attention(split_heads(qa, FOX_HEADS), split_heads(ka, FOX_HEADS),
                              split_heads(va, FOX_HEADS), log_f)
    qbh, kbh = split_heads(qb, DIFF_HEADS), split_heads(kb, DIFF_HEADS)
    lam = (jnp.exp(jnp.sum(lq1.astype(jnp.float32) * lk1.astype(jnp.float32)))
           - jnp.exp(jnp.sum(lq2.astype(jnp.float32) * lk2.astype(jnp.float32)))
           + lambda_init)
    ob = differential_attention(qbh[..., :HEAD_DIM], qbh[..., HEAD_DIM:],
                                kbh[..., :HEAD_DIM], kbh[..., HEAD_DIM:],
                                split_heads(vb, DIFF_HEADS), lam)
    ob = rms_norm(ob, diff_norm) * (1.0 - lambda_init)
    o = jnp.concatenate([merge_heads(oa), merge_heads(ob).astype(oa.dtype)], axis=-1)
    return (o @ w_out).astype(h.dtype)

def odd_mixer(h, w_in, sinks, lower_bound, hgrn_norm, w_out):
    proj = h @ w_in
    qc, kc, vc, qd, fd, i_d, gd = partition(
        proj, [SWA_W, SWA_KV_W, SWA_KV_W, HGRN_W, HGRN_W, HGRN_W, HGRN_W])
    oc = swa_sink_attention(split_heads(qc, SWA_Q_HEADS), split_heads(kc, SWA_KV_HEADS),
                            split_heads(vc, SWA_KV_HEADS), sinks)
    f = lower_bound + (1.0 - lower_bound) * jax.nn.sigmoid(fd.astype(jnp.float32))
    od = hgrn2_recurrence(split_heads(jax.nn.silu(qd), HGRN_HEADS),
                          split_heads(1.0 - f, HGRN_HEADS),
                          split_heads(i_d, HGRN_HEADS),
                          split_heads(jnp.log(f), HGRN_HEADS))
    od = rms_norm(od.astype(h.dtype), hgrn_norm)
    od = merge_heads(od) * jax.nn.sigmoid(gd)
    o = jnp.concatenate([merge_heads(oc), od.astype(oc.dtype)], axis=-1)
    return (o @ w_out).astype(h.dtype)

def swiglu(h, w_gate, w_up, w_down):
    return (jax.nn.silu(h @ w_gate) * (h @ w_up)) @ w_down

def setup_inputs(seed: int = 0) -> dict:
    key = jax.random.key(seed)
    ks = jax.random.split(key, 20)
    nrm = jax.random.normal
    f32 = jnp.float32
    return {
        "x": nrm(ks[0], (BATCH, SEQ, D_MODEL), f32),
        "ln_mix": 1.0 + 0.02 * nrm(ks[1], (DEPTH, D_MODEL), f32),
        "ln_ffn": 1.0 + 0.02 * nrm(ks[2], (DEPTH, D_MODEL), f32),
        "ln_final": 1.0 + 0.02 * nrm(ks[3], (D_MODEL,), f32),
        "w_in_even": nrm(ks[4], (N_EVEN, D_MODEL, EVEN_IN), f32) * D_MODEL ** -0.5,
        "b_forget": 2.0 + 0.5 * nrm(ks[5], (N_EVEN, FOX_HEADS), f32),
        "lambda_q1": 0.1 * nrm(ks[6], (N_EVEN, HEAD_DIM), f32),
        "lambda_k1": 0.1 * nrm(ks[7], (N_EVEN, HEAD_DIM), f32),
        "lambda_q2": 0.1 * nrm(ks[8], (N_EVEN, HEAD_DIM), f32),
        "lambda_k2": 0.1 * nrm(ks[9], (N_EVEN, HEAD_DIM), f32),
        "diff_norm": 1.0 + 0.02 * nrm(ks[10], (N_EVEN, DIFF_V_DIM), f32),
        "w_out_even": nrm(ks[11], (N_EVEN, EVEN_OUT, D_MODEL), f32) * EVEN_OUT ** -0.5,
        "w_in_odd": nrm(ks[12], (N_ODD, D_MODEL, ODD_IN), f32) * D_MODEL ** -0.5,
        "sinks": 0.5 * nrm(ks[13], (N_ODD, SWA_Q_HEADS), f32),
        "hgrn_gamma": 0.1 * nrm(ks[14], (DEPTH, HGRN_W), f32),
        "hgrn_norm": 1.0 + 0.02 * nrm(ks[15], (N_ODD, HGRN_DIM), f32),
        "w_out_odd": nrm(ks[16], (N_ODD, ODD_OUT, D_MODEL), f32) * ODD_OUT ** -0.5,
        "w_gate": nrm(ks[17], (DEPTH, D_MODEL, D_FF), f32) * D_MODEL ** -0.5,
        "w_up": nrm(ks[18], (DEPTH, D_MODEL, D_FF), f32) * D_MODEL ** -0.5,
        "w_down": nrm(ks[19], (DEPTH, D_FF, D_MODEL), f32) * D_FF ** -0.5,
    }

def reference(x, ln_mix, ln_ffn, ln_final, w_in_even, b_forget, lambda_q1, lambda_k1,
              lambda_q2, lambda_k2, diff_norm, w_out_even, w_in_odd, sinks, hgrn_gamma,
              hgrn_norm, w_out_odd, w_gate, w_up, w_down):
    sm = jax.nn.softmax(hgrn_gamma.astype(jnp.float32), axis=0)
    lower_bounds = jnp.cumsum(sm, axis=0) - sm[0:1]
    for l in range(DEPTH):
        h = rms_norm(x, ln_mix[l])
        j = l // 2
        if l % 2 == 0:
            lambda_init = 0.8 - 0.6 * math.exp(-0.3 * l)
            x = x + even_mixer(h, w_in_even[j], b_forget[j], lambda_q1[j], lambda_k1[j],
                               lambda_q2[j], lambda_k2[j], diff_norm[j], w_out_even[j],
                               lambda_init)
        else:
            x = x + odd_mixer(h, w_in_odd[j], sinks[j], lower_bounds[l], hgrn_norm[j],
                              w_out_odd[j])
        h = rms_norm(x, ln_ffn[l])
        x = x + swiglu(h, w_gate[l], w_up[l], w_down[l]).astype(x.dtype)
    return rms_norm(x, ln_final)


_drawn_inputs = setup_inputs


def setup_inputs(seed=0):
    import zlib

    import numpy as np

    out = dict(_drawn_inputs(seed))
    spreads = {}
    factors = {'ln_ffn': 3.058,
     'ln_final': 2.998,
     'lambda_q1': 3.514,
     'lambda_k2': 8.0,
     'diff_norm': 4.086,
     'sinks': 8.0,
     'hgrn_gamma': 8.0,
     'hgrn_norm': 8.0}
    for name, (base, spread) in spreads.items():
        noise = np.random.default_rng([zlib.crc32(name.encode()), seed]).standard_normal(out[name].shape)
        drawn = base * np.exp(spread * noise) if base else spread * noise
        out[name] = __import__('jax').numpy.asarray(drawn.astype(out[name].dtype))
    for name, factor in factors.items():
        out[name] = (out[name] * factor).astype(out[name].dtype)
    return out
```

```python
from contextlib import ExitStack

import concourse.bass as bass
from concourse import mybir

F32 = mybir.dt.float32
F32R = mybir.dt.float32r
BF16 = mybir.dt.bfloat16
I32 = mybir.dt.int32
ALU = mybir.AluOpType
ACT = mybir.ActivationFunctionType
AX = mybir.AxisListType.X

P = 128
SEQ = 512
D = 1024
DC = D // P
TB = SEQ // P
HD = 64
FF = 2816
FT = FF // P
FH = FT // 2
EPS = 1e-6
LAMBDA_INIT = 0.8 - 0.6
QSCALE = HD ** -0.5
NEG = -1e30
FOX_G = 4
DIFF_G = 4
GROUPS = FOX_G + DIFF_G

LN_MIX, LN_FFN, LN_FIN = 0, 16, 32
DIFFN, HGRNN, BFG, LAMB, SINK, GAM = 40, 41, 42, 43, 47, 55
NSMALL = 63
C_ID, C_FOX, C_DIFF, C_SWA, C_LEV = 0, 128, 256, 384, 640
NLEV = 8
C_FIRST = C_LEV + NLEV * P
NCONST = C_FIRST + P


def constants():
    import numpy as np
    c = np.zeros((P, NCONST), np.float32)
    q = np.arange(P)[:, None]
    s = np.arange(P)[None, :]
    c[:, C_ID:C_ID + P] = q == s
    c[:, C_FOX:C_FOX + P] = np.where(s <= q, 0.0, NEG)
    c[:, C_DIFF:C_DIFF + P] = np.where(s // 64 <= q // 64, 0.0, NEG)
    k = np.arange(2 * P)[None, :] // 64
    c[:, C_SWA:C_SWA + 2 * P] = np.where((k >= q // 64 + 1) & (k <= q // 64 + 2), 0.0, NEG)
    sp, tf = q, s
    for lev in range(NLEV - 1):
        m = 64 >> lev
        on = (sp // (2 * m) == tf // (2 * m)) & (sp % (2 * m) < m) & (tf % (2 * m) >= m)
        c[:, C_LEV + lev * P:C_LEV + (lev + 1) * P] = on
    c[:, C_LEV + (NLEV - 1) * P:C_LEV + NLEV * P] = sp == tf
    c[:, C_FIRST:C_FIRST + P] = tf != 0
    return c


def build(nc, layers, xT, small, const, w_even, w_fa, w_out_e, w_odd, w_out_o, w_gu, w_dn, out):
    with ExitStack() as ctx:
        def sb(name, shape, dt=F32):
            return ctx.enter_context(nc.sbuf_tensor(name, shape, dt))

        def sem(name):
            return ctx.enter_context(nc.semaphore(name))

        def sems(name, n):
            return [sem(f"{name}{i}") for i in range(n)]

        x = sb("x", [P, DC, SEQ])
        xh = sb("xh", [P, DC, SEQ], F32R)
        xl = sb("xl", [P, DC, SEQ], F32R)
        split_acts = sb("split_acts", [P, 2 * FH, SEQ], F32R)
        gh, gl = split_acts[:, 0:FH], split_acts[:, FH:2 * FH]
        oh, ol = split_acts[:, 0:DC], split_acts[:, DC:2 * DC]
        ring_raw = sb("ring_raw", [P, (2 * FH + DC) * P])
        ring_hi = sb("ring_hi", [P, (2 * FH + DC) * P], F32R)
        ring_lo = sb("ring_lo", [P, (2 * FH + DC) * P], F32R)

        def ring(t, s, a, b):
            return t[:, s * FH * P + a:s * FH * P + b]
        fa_raw = sb("fa_raw", [P, DC * 8])
        fa_h = sb("fa_h", [P, DC * 8], F32R)
        fa_l = sb("fa_l", [P, DC * 8], F32R)
        work = sb("work", [P, 24, SEQ])
        rstd = sb("rstd", [P, SEQ])
        mean = sb("mean", [P, SEQ])
        newton = sb("newton", [P, SEQ])
        sq = sb("sq", [P, SEQ])
        sacc = sb("sacc", [P, SEQ])
        sm = sb("sm", [P, NSMALL])
        ident = sb("ident", [P, P])[:]
        level_mask = sb("level_mask", [P, NLEV * P], mybir.dt.uint8)
        not_first = sb("not_first", [P, SEQ])
        score_acc = sb("score_acc", [P, SEQ])
        cstb = sb("cstb", [P, C_LEV], BF16)
        identb = cstb[:, C_ID:C_ID + P]
        ones = sb("ones", [P, P])
        meanw = sb("meanw", [P, P])
        tiny = sb("tiny", [P, 128])

        bank = [ctx.enter_context(nc.psum_tensor(f"bank{i}", [P, SEQ], F32)) for i in range(8)]
        acc = bank[0:3]
        S = bank[3:5]
        PTP = bank[5:7]
        OP = bank[7]

        raw_in, hi_ready, lo_ready = sems("raw_in", 3), sems("hi_ready", 3), sems("lo_ready", 3)
        unit_done, acc_read = sems("unit_done", 3), sems("acc_read", 3)
        x_in, small_in, const_in, fa_in = sem("x_in"), sem("small_in"), sem("const_in"), sem("fa_in")
        const_b = sem("const_b")
        xh_ready, xl_ready = sem("xh_ready"), sem("xl_ready")
        sq_ready, sacc_ready, sacc_zero = sem("sq_ready"), sem("sacc_ready"), sem("sacc_zero")
        stat_ready, mean_ready, ln_ready, y_ready = sem("stat_ready"), sem("mean_ready"), sem("ln_ready"), sem("y_ready")
        nt_ready, rstd_ready = sem("nt_ready"), sem("rstd_ready")
        ones_ready = sem("ones_ready")

        block = ctx.enter_context(nc.Block())

        UNIT8 = DC * P
        R_F = GROUPS
        PH = {}
        r = R_F
        for l in range(layers):
            if l % 2:
                PH["odd_in", l] = r
                r += 8
            PH["mix_out", l] = r
            r += 4
            for half in range(2):
                PH["gu", l, half] = r
                r += FH
                PH["dn", l, half] = r
                r += 4

        def sp_load(sp, s, r, src, n):
            if not (isinstance(r, int) and r == 0):
                sp.wait_ge(lo_ready[s], r)
            sp.dma_start(ring(ring_raw, s, 0, n), src).then_inc(raw_in[s], 16)

        def act_hi(act, s, r, n=UNIT8):
            if not (isinstance(r, int) and r == 0):
                act.wait_ge(unit_done[s], r)
            act.wait_ge(raw_in[s], 16 * (r + 1))
            act.activation(ring(ring_hi, s, 0, n), ring(ring_raw, s, 0, n), ACT.Copy).then_inc(hi_ready[s], 1)

        def dve_lo(v, s, r, n=UNIT8):
            v.wait_ge(hi_ready[s], r + 1)
            v.tensor_tensor(ring(ring_lo, s, 0, n), ring(ring_raw, s, 0, n), ring(ring_hi, s, 0, n).bitcast(F32),
                            ALU.subtract).then_inc(lo_ready[s], 1)

        def pe_chunk(pe, s, c, n, rh, rl, b, last=False):
            w0, w1 = ring(ring_hi, s, c * P, (c + 1) * P), ring(ring_lo, s, c * P, (c + 1) * P)
            pe.matmul(b, w0, rh[:, c], start=(c == 0), stop=False)
            pe.matmul(b, w0, rl[:, c], start=False, stop=False)
            return pe.matmul(b, w1, rh[:, c], start=False, stop=(c == n - 1))

        def pe_unit_wait(pe, s, r):
            pe.wait_ge(lo_ready[s], r + 1)
            if not (isinstance(r, int) and r == 0):
                pe.wait_ge(acc_read[s], r)

        def pe_unit(pe, s, r, n, rh, rl):
            pe_unit_wait(pe, s, r)
            for c in range(n):
                mm = pe_chunk(pe, s, c, n, rh, rl, acc[s][:])
            mm.then_inc(unit_done[s], 1)

        def pe_stat(pe, k):
            pe.wait_ge(sacc_ready, DC * (k + 1))
            pe.wait_ge(mean_ready, k) if k else None
            pe.wait_ge(ones_ready, 3) if not k else None
            pe.matmul(OP[:], meanw[:], sacc[:], start=True, stop=True).then_inc(stat_ready, 1)

        def dve_mean(v, k):
            v.wait_ge(stat_ready, k + 1)
            v.tensor_scalar(mean[:], OP[:], EPS, None, ALU.add).then_inc(mean_ready, 1)

        def act_rsqrt(act, k):
            act.wait_ge(mean_ready, k + 1)
            act.activation(newton[:], mean[:], ACT.Ln).then_inc(ln_ready, 1)
            act.wait_ge(ln_ready, k + 1)
            act.activation(rstd[:], newton[:], ACT.Exp, scale=-0.5).then_inc(y_ready, 1)

        def dve_newton(v, k):
            v.wait_ge(y_ready, k + 1)
            v.scalar_tensor_tensor(newton[:], mean[:], -0.5, rstd[:], ALU.mult, ALU.mult).then_inc(nt_ready, 1)
            v.wait_ge(nt_ready, 2 * k + 1)
            v.tensor_tensor(newton[:], newton[:], rstd[:], ALU.mult).then_inc(nt_ready, 1)
            v.wait_ge(nt_ready, 2 * k + 2)
            v.scalar_tensor_tensor(rstd[:], newton[:], 1.5, rstd[:], ALU.add, ALU.mult).then_inc(rstd_ready, 1)

        def act_xh(act, j, gcol, n, gate):
            act.wait_ge(*gate)
            act.activation(xh[:, j], x[:, j], ACT.Copy, scale=sm[:, gcol:gcol + 1] if isinstance(j, int)
                           else sm[:, bass.ds(gcol, 1)]).then_inc(xh_ready, 1)

        def dve_xl(v, j, gcol, n):
            v.wait_ge(xh_ready, n + 1)
            v.scalar_tensor_tensor(xl[:, j], x[:, j], sm[:, gcol:gcol + 1] if isinstance(j, int) else sm[:, bass.ds(gcol, 1)],
                                   xh[:, j].bitcast(F32), ALU.mult, ALU.subtract).then_inc(xl_ready, 1)

        def pool_sq(g, j, n, k, gate):
            g.wait_ge(*gate)
            if not isinstance(n, int) or n:
                g.wait_ge(sacc_ready, n)
            g.tensor_tensor(sq[:], x[:, j], x[:, j], ALU.mult).then_inc(sq_ready, 1)
            g.wait_ge(sq_ready, n + 1)
            g.tensor_tensor(sacc[:], sacc[:], sq[:], ALU.add).then_inc(sacc_ready, 1)

        def pool_zero(g, k):
            if k:
                g.wait_ge(stat_ready, k)
            g.memset(sacc[:], 0.0).then_inc(sacc_zero, 1)
            g.wait_ge(sacc_zero, k + 1)

        q_cur, k_cur, vT, Vn = work[:, 0], work[:, 1], work[:, 2], work[:, 3]
        PB = [work[:, 4 + i] for i in range(4)]
        PTS = [work[:, 8 + i] for i in range(2)]
        on = work[:, 10]
        CQ = work[:, 11:15].bitcast(BF16).rearrange("p a b -> p (a b)").rearrange("p (h t) -> p h t", h=8)
        CK = work[:, 15:19].bitcast(BF16).rearrange("p a b -> p (a b)").rearrange("p (h t) -> p h t", h=8)
        cq_cur = work[:, 19].bitcast(BF16).rearrange("p (h t) -> p h t", h=2)
        const_stage = work[:, 4:8].rearrange("p a b -> p (a b)")
        z = work[0:8, 20]
        za = work[0:8, 21]
        cum = work[0:8, 22]
        cpart = work[0:8, 23].bitcast(BF16).rearrange("p (a t) -> p a t", a=2)
        cpart2 = work[0:8, 10].bitcast(BF16).rearrange("p (a t) -> p a t", a=2)
        cpartn = [work[0:8, 8 + i].bitcast(BF16).rearrange("p (a t) -> p a t", a=2) for i in range(2)]
        nmax = tiny[:, 0:8]
        rsum = tiny[:, 8:16]
        rinv = tiny[:, 16:24]
        lamt = tiny[:, 24:32]
        dss = tiny[:, 32:36]
        dn = tiny[:, 36:48]
        dscale = tiny[:, 48:49]

        fa_hi, fa_lo, fa_done, fa_read = sem("fa_hi"), sem("fa_lo"), sem("fa_done"), sem("fa_read")
        gate_step, gate_act = sem("gate_step"), sem("gate_act")
        cq_in, cq_ones, cq_staged = sem("cq_in"), sem("cq_ones"), sem("cq_staged")
        lam_prod, lam_sum, lam_exp, lam_ready = sem("lam_prod"), sem("lam_sum"), sem("lam_exp"), sem("lam_ready")
        v_turned, v_nat = sem("v_turned"), sem("v_nat")
        f_scores, f_max, f_exp, f_turned, f_pv = (sem(n) for n in (
            "f_scores", "f_max", "f_exp", "f_turned", "f_pv"))
        f_pts = sems("f_pts", 2)
        d_scores, d_max, d_exp, d_mix, d_turned, d_pts, d_pv = (sem(n) for n in (
            "d_scores", "d_max", "d_exp", "d_mix", "d_turned", "d_pts", "d_pv"))
        rinv_ready, d_step = sem("rinv_ready"), sem("d_step")
        d_sq, d_ln, d_act = sem("d_sq"), sem("d_ln"), sem("d_act")
        on_ready, o_turned, oh_ready, ol_ready = sem("on_ready"), sem("o_turned"), sem("oh_ready"), sem("ol_ready")

        def pe_v_turn(pe, g):
            pe.wait_ge(acc_read[2], g + 1)
            for i in range(TB):
                mm = pe.transpose(acc[2][:, i * P:(i + 1) * P], vT[:, i * P:(i + 1) * P], ident)
            mm.then_inc(v_turned, 1)

        def act_v_nat(act, g, pv, n):
            act.wait_ge(v_turned, g + 1)
            if n is not None:
                act.wait_ge(pv, n)
            act.activation(Vn, acc[2][:], ACT.Copy).then_inc(v_nat, 1)

        def pe_o_turn(pe, g):
            pe.wait_ge(on_ready, g + 2)
            for i in range(TB):
                mm = pe.transpose(S[0][:, i * P:(i + 1) * P], on[:, i * P:(i + 1) * P], ident)
            mm.then_inc(o_turned, 1)

        CR = 2

        def fox_scores(pe, g, n):
            k, m, i = 8 * g + n, n % 2, n // 2
            pe.wait_ge(f_exp, k + 1)
            if n == 0:
                pe.wait_ge(acc_read[1], g + 1)
                pe.wait_ge(acc_read[0], g + 1)
                pe.wait_ge(cq_staged, g + 1)
                pe.wait_ge(ol_ready, g + 1)
            b, w = S[n % 2], P * (i + 1)
            rows = slice(HD * m, HD * m + HD)
            pe.matmul(b[:, 0:w], q_cur[rows, i * P:(i + 1) * P], k_cur[rows, 0:w], start=True, stop=False)
            pe.matmul(b[:, 0:w], cq_cur[0:6, m, i * P:(i + 1) * P],
                      CK[0:6, bass.ds(2 * g + m, 1), 0:w].rearrange("p a t -> p (a t)"), start=False, stop=False)
            pe.matmul(b[:, w - P:w], identb, cstb[:, C_FOX:C_FOX + P], start=False, stop=True).then_inc(f_scores, 1)

        def fox_max(v, g, n):
            v.wait_ge(f_scores, 8 * g + n + 1)
            v.tensor_reduce(nmax[:, n:n + 1], S[n % 2][:, 0:P * (n // 2 + 1)], AX, ALU.max, negate=True).then_inc(f_max, 1)

        def fox_exp(act, g, n):
            k, w = 8 * g + n, P * (n // 2 + 1)
            act.wait_ge(f_max, k + 1)
            act.wait_ge(f_turned, k + 1)
            if n == 0:
                act.wait_ge(rinv_ready, g + 1)
            act.activation(PB[n % 2][:, 0:w], S[n % 2][:, 0:w], ACT.Exp, bias=nmax[:, n:n + 1],
                           accum_out=rsum[:, n:n + 1]).then_inc(f_exp, 1)

        def fox_turn(pe, g, n):
            k = 8 * g + n
            pe.wait_ge(f_exp, k + 1 + CR)
            pe.wait_ge(f_pts[n % 2], 4 * g + n // 2 + 1)
            for j in range(n // 2 + 1):
                mm = pe.transpose(PTP[n % 2][:, j * P:(j + 1) * P], PB[n % 2][:, j * P:(j + 1) * P], ident)
            mm.then_inc(f_turned, 1)

        def fox_pts_wait(e, g, n):
            k = 8 * g + n
            e.wait_ge(f_turned, k + 1 + CR)
            e.wait_ge(f_pv, k + 1)

        def fox_pts_dve(v, g, n):
            fox_pts_wait(v, g, n)
            w = P * (n // 2 + 1)
            v.tensor_copy(PTS[n % 2][:, 0:w], PTP[n % 2][:, 0:w]).then_inc(f_pts[n % 2], 1)

        def fox_pts_act(act, g, n):
            fox_pts_wait(act, g, n)
            w = P * (n // 2 + 1)
            act.activation(PTS[n % 2][:, 0:w], PTP[n % 2][:, 0:w], ACT.Copy).then_inc(f_pts[n % 2], 1)

        def fox_pv(pe, g, n):
            k, m, i = 8 * g + n, n % 2, n // 2
            pe.wait_ge(f_pts[n % 2], 4 * g + n // 2 + 2)
            if n == 0:
                pe.wait_ge(v_nat, g + 1)
                pe.wait_ge(on_ready, g + 1)
            for j in range(i + 1):
                mm = pe.matmul(OP[:, i * P + m * HD:i * P + m * HD + HD], PTS[n % 2][:, j * P:(j + 1) * P],
                               Vn[:, j * P + m * HD:j * P + m * HD + HD], start=(j == 0), stop=(j == i))
            mm.then_inc(f_pv, 1)

        def proj_wait(pe, s, G):
            pe.wait_ge(lo_ready[s], G + 1)
            pe.wait_ge(acc_read[s], G)
            if s == 2:
                pe.wait_ge(v_nat, G)

        def proj_chunks(pe, s, G, c0, c1):
            if c0 == 0:
                proj_wait(pe, s, G)
            for c in range(c0, c1):
                mm = pe_chunk(pe, s, c, DC, xh, xl, acc[s][:])
            if c1 == DC:
                mm.then_inc(unit_done[s], 1)

        def dve_q(v, G):
            v.wait_ge(unit_done[0], G + 1)
            v.scalar_tensor_tensor(q_cur, acc[0][:], QSCALE, rstd[:], ALU.mult, ALU.mult).then_inc(acc_read[0], 1)

        def dve_k(v, G):
            v.wait_ge(unit_done[1], G + 1)
            v.tensor_tensor(k_cur, acc[1][:], rstd[:], ALU.mult).then_inc(acc_read[1], 1)

        def dve_v(v, G):
            v.wait_ge(unit_done[2], G + 1)
            v.tensor_tensor(vT, acc[2][:], rstd[:], ALU.mult).then_inc(acc_read[2], 1)

        def fox_group_pe(pe, g):
            for n in range(8):
                fox_scores(pe, g, n)
                if n == 0:
                    pe_v_turn(pe, g)
                proj_chunks(pe, 0, g + 1, n, n + 1)
                if n >= 1:
                    fox_turn(pe, g, n - 1)
                if n >= 2:
                    fox_pv(pe, g, n - 2)
            proj_chunks(pe, 1, g + 1, 0, 2)
            fox_turn(pe, g, 7)
            fox_pv(pe, g, 6)
            proj_chunks(pe, 1, g + 1, 2, 4)
            fox_pv(pe, g, 7)
            proj_chunks(pe, 1, g + 1, 4, 8)
            pe_o_turn(pe, g)
            proj_chunks(pe, 2, g + 1, 0, 8)

        def fox_group_act(act, g):
            act_v_nat(act, g, f_pv, 8 * g + CR)
            for n in range(8):
                fox_exp(act, g, n)
                if n == 0:
                    act_hi(act, 1, g + 1)
                if n >= 2 and n % 2 == 0:
                    fox_pts_act(act, g, n - 1)
            fox_pts_act(act, g, 7)
            act_hi(act, 2, g + 1)
            act_oh(act, g)
            act_hi(act, 0, g + 2)

        def act_oh(act, g):
            act.wait_ge(o_turned, g + 1)
            act.activation(oh[:, g], S[0][:], ACT.Copy).then_inc(oh_ready, 1)

        def fox_group_dve(v, g):
            fox_max(v, g, 0)
            dve_lo(v, 1, g + 1)
            for n in range(1, 8):
                fox_max(v, g, n)
                if n % 2 == 1:
                    fox_pts_dve(v, g, n - 1)
            v.wait_ge(f_exp, 8 * g + 8 + CR)
            v.reciprocal(rinv, rsum).then_inc(rinv_ready, 1)
            dve_q(v, g + 1)
            dve_lo(v, 2, g + 1)
            v.wait_ge(f_pv, 8 * g + 8 + CR)
            v.wait_ge(rinv_ready, g + 2)
            v.tensor_tensor(on.rearrange("p (n d) -> p n d", d=HD), OP[:].rearrange("p (n d) -> p n d", d=HD),
                            rinv.unsqueeze(2).to_broadcast([P, 8, HD]), ALU.mult).then_inc(on_ready, 1)
            dve_k(v, g + 1)
            v.wait_ge(oh_ready, g + 1)
            v.tensor_tensor(ol[:, g], S[0][:], oh[:, g].bitcast(F32), ALU.subtract).then_inc(ol_ready, 1)
            dve_lo(v, 0, g + 2)
            dve_v(v, g + 1)

        def diff_scores(pe, g, i, last):
            for m in range(2):
                k = 8 * g + 2 * i + m
                pe.wait_ge(d_exp, k + 1)
                if i == 0 and m == 0:
                    pe.wait_ge(acc_read[0], FOX_G + g + 1)
                    pe.wait_ge(acc_read[1], FOX_G + g + 1)
                    pe.wait_ge(ol_ready, FOX_G + g + 1)
                w = P * (i + 1)
                rows = slice(HD * m, HD * m + HD)
                pe.matmul(S[m][:, 0:w], q_cur[rows, i * P:(i + 1) * P], k_cur[rows, 0:w], start=True, stop=False)
                pe.matmul(S[m][:, w - P:w], identb, cstb[:, C_DIFF:C_DIFF + P], start=False,
                          stop=True).then_inc(d_scores, 1)

        def diff_max(v, g, i):
            for m in range(2):
                n = 2 * i + m
                v.wait_ge(d_scores, 8 * g + n + 1)
                v.tensor_reduce(nmax[:, n:n + 1], S[m][:, 0:P * (i + 1)], AX, ALU.max, negate=True).then_inc(d_max, 1)

        def diff_exp(act, g, i):
            for m in range(2):
                n = 2 * i + m
                act.wait_ge(d_max, 8 * g + n + 1)
                act.wait_ge(d_mix, 2 * (4 * g + i) + 1 + m)
                w = P * (i + 1)
                act.activation(PB[m][:, 0:w], S[m][:, 0:w], ACT.Exp, bias=nmax[:, n:n + 1],
                               accum_out=rsum[:, n:n + 1]).then_inc(d_exp, 1)

        def diff_mix(v, g, i):
            t, w, pm = 4 * g + i, P * (i + 1), PB[2 + i % 2]
            v.wait_ge(d_exp, 2 * t + 2 + CR)
            v.reciprocal(rinv[:, 0:2], rsum[:, 2 * i:2 * i + 2]).then_inc(d_step, 1)
            v.wait_ge(d_step, 2 * t + 1)
            v.tensor_scalar(rinv[:, 2:3], rinv[:, 1:2], lamt[:, 7:8], None, ALU.mult).then_inc(d_step, 1)
            v.wait_ge(d_turned, t + 1)
            v.tensor_scalar(pm[:, 0:w], PB[0][:, 0:w], rinv[:, 0:1], None, ALU.mult).then_inc(d_mix, 1)
            v.wait_ge(d_step, 2 * t + 2)
            v.wait_ge(d_mix, 2 * t + 1 + CR)
            v.scalar_tensor_tensor(pm[:, 0:w], PB[1][:, 0:w], rinv[:, 2:3], pm[:, 0:w], ALU.mult,
                                   ALU.add).then_inc(d_mix, 1)

        def diff_turn(pe, g, i):
            t = 4 * g + i
            pe.wait_ge(d_mix, 2 * t + 2 + CR)
            pe.wait_ge(d_pts, t + 1)
            for j in range(i + 1):
                mm = pe.transpose(PTP[i % 2][:, j * P:(j + 1) * P], PB[2 + i % 2][:, j * P:(j + 1) * P], ident)
            mm.then_inc(d_turned, 1)

        def diff_pts(act, g, i):
            t, w = 4 * g + i, P * (i + 1)
            act.wait_ge(d_turned, t + 1 + CR)
            act.wait_ge(d_pv, t + 1)
            act.activation(PTS[i % 2][:, 0:w], PTP[i % 2][:, 0:w], ACT.Copy).then_inc(d_pts, 1)

        def diff_pv(pe, g, i):
            t = 4 * g + i
            pe.wait_ge(d_pts, t + 1 + CR)
            if i == 0:
                pe.wait_ge(v_nat, FOX_G + g + 1)
                pe.wait_ge(on_ready, FOX_G + g + 1)
            for j in range(i + 1):
                mm = pe.matmul(OP[:, i * P:(i + 1) * P], PTS[i % 2][:, j * P:(j + 1) * P],
                               Vn[:, j * P:(j + 1) * P], start=(j == 0), stop=(j == i))
            mm.then_inc(d_pv, 1)

        def diff_group_pe(pe, g, last=False):
            G = FOX_G + g
            for i in range(4):
                diff_scores(pe, g, i, last)
                if i == 0:
                    pe_v_turn(pe, G)
                if not last:
                    proj_chunks(pe, 0, G + 1, 2 * i, 2 * i + 2)
                if i >= 1:
                    diff_turn(pe, g, i - 1)
                if i >= 2:
                    diff_pv(pe, g, i - 2)
            if not last:
                proj_chunks(pe, 1, G + 1, 0, 3)
            diff_turn(pe, g, 3)
            diff_pv(pe, g, 2)
            if not last:
                proj_chunks(pe, 1, G + 1, 3, 6)
            diff_pv(pe, g, 3)
            if not last:
                proj_chunks(pe, 1, G + 1, 6, 8)
                proj_chunks(pe, 2, G + 1, 0, 5)
            pe_o_turn(pe, G)
            if not last:
                proj_chunks(pe, 2, G + 1, 5, 8)

        def row_rms_act(act, g, scratch):
            for i in range(4):
                act.activation(scratch[:, i * P:(i + 1) * P], OP[:, i * P:(i + 1) * P], ACT.Square,
                               accum_out=dss[:, i:i + 1]).then_inc(d_sq, 1)
            act.wait_ge(d_ln, 2 * g + 1)
            act.activation(dn[:, 4:8], dn[:, 0:4], ACT.Ln).then_inc(d_act, 1)
            act.wait_ge(d_act, 2 * g + 1)
            act.activation(dn[:, 4:8], dn[:, 4:8], ACT.Exp, scale=-0.5).then_inc(d_act, 1)

        def row_mean_dve(v, g):
            v.wait_ge(d_sq, 4 * g + 4)
            v.tensor_scalar(dn[:, 0:4], dss, 1.0 / P, EPS, ALU.mult, ALU.add).then_inc(d_ln, 1)

        def row_rms_dve(v, g, on):
            v.wait_ge(d_act, 2 * g + 2)
            v.wait_ge(d_ln, 2 * g + 1)
            v.tensor_tensor(dn[:, 8:12], dn[:, 0:4], dn[:, 4:8], ALU.mult).then_inc(d_ln, 1)
            v.wait_ge(d_ln, 2 * g + 2)
            v.tensor_tensor(dn[:, 8:12], dn[:, 8:12], dn[:, 4:8], ALU.mult).then_inc(d_newton, 1)
            v.wait_ge(d_newton, 3 * g + 1)
            v.tensor_scalar(dn[:, 8:12], dn[:, 8:12], -0.5, 1.5, ALU.mult, ALU.add).then_inc(d_newton, 1)
            v.wait_ge(d_newton, 3 * g + 2)
            v.tensor_tensor(dn[:, 8:12], dn[:, 8:12], dn[:, 4:8], ALU.mult).then_inc(d_newton, 1)
            v.wait_ge(d_newton, 3 * g + 3)
            v.tensor_tensor(on.rearrange("p (n d) -> p n d", d=P), OP[:].rearrange("p (n d) -> p n d", d=P),
                            dn[:, 8:12].unsqueeze(2).to_broadcast([P, 4, P]), ALU.mult).then_inc(on_ready, 1)

        def diff_group_act(act, g, last=False):
            G = FOX_G + g
            act_v_nat(act, G, d_pv, 4 * g + CR)
            for i in range(4):
                diff_exp(act, g, i)
                if i == 0 and not last:
                    act_hi(act, 1, G + 1)
                if i >= 1:
                    diff_pts(act, g, i - 1)
            diff_pts(act, g, 3)
            if not last:
                act_hi(act, 2, G + 1)
            act.wait_ge(d_pv, 4 * g + 4 + CR)
            row_rms_act(act, g, PB[0])
            act.wait_ge(o_turned, G + 1)
            act.activation(oh[:, G], S[0][:], ACT.Copy, scale=dscale).then_inc(oh_ready, 1)
            if not last:
                act_hi(act, 0, G + 2)

        def diff_group_dve(v, g, last=False):
            G = FOX_G + g
            for i in range(4):
                diff_max(v, g, i)
                if i == 0 and not last:
                    dve_lo(v, 1, G + 1)
                diff_mix(v, g, i)
            if not last:
                dve_q(v, G + 1)
                dve_lo(v, 2, G + 1)
            row_mean_dve(v, g)
            if not last:
                dve_k(v, G + 1)
            row_rms_dve(v, g, on)
            v.wait_ge(oh_ready, G + 1)
            v.scalar_tensor_tensor(ol[:, G], S[0][:], dscale, oh[:, G].bitcast(F32), ALU.mult,
                                   ALU.subtract).then_inc(ol_ready, 1)
            if not last:
                dve_lo(v, 0, G + 2)
                dve_v(v, G + 1)

        d_newton = sem("d_newton")

        R0 = PH.get(("odd_in", 1), 0)
        KV = [work[:, 1], work[:, 2]]
        o_state, o_vT, o_Vn = work[:, 3], work[:, 3], work[:, 4]
        oP, oPT, o_on, o_kN = [work[:, 5], work[:, 6]], [work[:, 7], work[:, 8]], work[:, 9], work[:, 9]
        qr, fr, ir, gr = (work[:, 10 + i] for i in range(4))
        hq, sgate, hb, hk = (work[:, 14 + i] for i in range(4))
        dif, zz = [work[:, 18], work[:, 19]], [work[:, 20], work[:, 21]]
        qe, hVn = work[:, 22], work[:, 23]
        LB = [S[1], PTP[1]]
        nsink, sinkx, sinke = tiny[:, 49:57], tiny[:, 57:65], tiny[:, 65:73]
        gmx, gd, ge = tiny[:, 73:77], tiny[:, 77:85], tiny[:, 85:93]
        gsum, grec, gsm, glb, goml, ebl = (tiny[:, 93:97], tiny[:, 97:101], tiny[:, 101:109], tiny[:, 109:113],
                                           tiny[:, 113:117], tiny[:, 117:121])
        s_scores, s_raw_max, s_max, s_exp, s_turned, s_pts, s_pv = (sem(n) for n in (
            "s_scores", "s_raw_max", "s_max", "s_exp", "s_turned", "s_pts", "s_pv"))
        s_sinkx, s_sinke, s_sum, s_rinv = sem("s_sinkx"), sem("s_sinke"), sem("s_sum"), sem("s_rinv")
        k_made, nsink_ready, sv_turned, sv_nat = sem("k_made"), sem("nsink_ready"), sem("sv_turned"), sem("sv_nat")
        lb_step, lb_exp = sem("lb_step"), sem("lb_exp")
        h_sigf, h_sigq, h_sigg, h_f, h_k, h_q, h_lnf, h_b = (sem(n) for n in (
            "h_sigf", "h_sigq", "h_sigg", "h_f", "h_k", "h_q", "h_lnf", "h_b"))
        h_eb, h_qe, h_ebl, h_kexp, h_dif, h_e, h_z, h_zread = (sem(n) for n in (
            "h_eb", "h_qe", "h_ebl", "h_kexp", "h_dif", "h_e", "h_z", "h_zread"))
        h_takes = sem("h_takes")
        h_zhalf, h_sc, h_cp, h_vturned, h_vnat, h_kn, h_u, h_state, h_o, h_gated = (sem(n) for n in (
            "h_zhalf", "h_sc", "h_cp", "h_vturned", "h_vnat", "h_kn", "h_u", "h_state", "h_o", "h_gated"))

        def odd_chunks(pe, s, r, c0, c1):
            if c0 == 0:
                pe_unit_wait(pe, s, r)
            for c in range(c0, c1):
                mm = pe_chunk(pe, s, c, DC, xh, xl, acc[s][:])
            if c1 == DC:
                mm.then_inc(unit_done[s], 1)

        def span(n):
            return (0, P) if n // 2 == 0 else (P * (n // 2 - 1), 2 * P)

        def swa_scores(pe, p, n, kv):
            k, m, i = 8 * p + n, n % 2, n // 2
            pe.wait_ge(s_exp, k + 1)
            if n == 0:
                pe.wait_ge(acc_read[0], R0 + 2 * p + 1)
                pe.wait_ge(ol_ready, 2 * p + GROUPS + 1)
            rows, (k0, w) = slice(HD * m, HD * m + HD), span(n)
            b = S[n % 2]
            pe.matmul(b[:, 0:w], work[rows, 0, i * P:(i + 1) * P], KV[kv][rows, k0:k0 + w],
                      start=True, stop=False)
            pe.matmul(b[:, 0:w], identb, cstb[:, C_SWA + 2 * P - w:C_SWA + 2 * P], start=False,
                      stop=True).then_inc(s_scores, 1)

        def swa_max(v, p, n):
            v.wait_ge(s_scores, 8 * p + n + 1)
            v.tensor_reduce(nmax[:, n:n + 1], S[n % 2][:, 0:span(n)[1]], AX, ALU.max, negate=True).then_inc(s_raw_max, 1)
            v.wait_ge(s_raw_max, 8 * p + n + 1)
            v.tensor_tensor(nmax[:, n:n + 1], nmax[:, n:n + 1], nsink[:, bass.ds(2 * p + n % 2, 1)],
                            ALU.min).then_inc(s_max, 1)

        def swa_exp(act, p, n):
            k, w = 8 * p + n, span(n)[1]
            act.wait_ge(s_max, k + 1)
            act.wait_ge(s_turned, k + 1)
            if n == 0:
                act.wait_ge(s_rinv, p + 1)
            act.activation(oP[n % 2][:, 0:w], S[n % 2][:, 0:w], ACT.Exp, bias=nmax[:, n:n + 1],
                           accum_out=rsum[:, n:n + 1]).then_inc(s_exp, 1)

        def swa_turn(pe, p, n):
            k = 8 * p + n
            pe.wait_ge(s_exp, k + 1 + CR)
            pe.wait_ge(s_pts, k + 1)
            if n == 0:
                pe.wait_ge(h_state, 3 * p + 1)
            if n == 1:
                pe.wait_ge(h_cp, 8 * p + CR)
            for j in range(span(n)[1] // P):
                mm = pe.transpose(PTP[n % 2][:, j * P:(j + 1) * P], oP[n % 2][:, j * P:(j + 1) * P], ident)
            mm.then_inc(s_turned, 1)

        def swa_pts(act, p, n):
            k, w = 8 * p + n, span(n)[1]
            act.wait_ge(s_turned, k + 1 + CR)
            act.wait_ge(s_pv, k + 1)
            act.activation(oPT[n % 2][:, 0:w], PTP[n % 2][:, 0:w], ACT.Copy).then_inc(s_pts, 1)

        def swa_pv(pe, p, n, kv):
            k, m, i = 8 * p + n, n % 2, n // 2
            k0, w = span(n)
            pe.wait_ge(s_pts, k + 1 + CR)
            if n == 0:
                pe.wait_ge(on_ready, 2 * p + GROUPS + 1)
            for j in range(w // P):
                mm = pe.matmul(OP[:, i * P + m * HD:i * P + m * HD + HD], oPT[n % 2][:, j * P:(j + 1) * P],
                               o_Vn[:, k0 + j * P + HD * kv:k0 + j * P + HD * kv + HD],
                               start=(j == 0), stop=(j == w // P - 1))
            mm.then_inc(s_pv, 1)

        def piece(a, L):
            return a.rearrange("p (n h m) -> p n h m", h=2, m=64 >> L)

        def head_start_act(act, p):
            act.wait_ge(acc_read[2], GROUPS + 2 + p + 1)
            act.activation(fr, fr, ACT.Sigmoid).then_inc(h_sigf, 1)
            act.wait_ge(acc_read[0], R0 + 2 * p + 2)
            act.wait_ge(h_z, 8 * p + CR)
            act.activation(dif[0], qr, ACT.Sigmoid).then_inc(h_sigq, 1)
            act.wait_ge(acc_read[1], R0 + 2 * p + 2)
            act.wait_ge(ol_ready, 2 * p + GROUPS + 1)
            act.activation(sgate, gr, ACT.Sigmoid).then_inc(h_sigg, 1)

        def head_f_dve(v, p):
            v.wait_ge(h_sigf, p + 1)
            v.tensor_scalar(fr, fr, goml[:, bass.ds(p, 1)], glb[:, bass.ds(p, 1)], ALU.mult, ALU.add).then_inc(h_f, 1)
            v.wait_ge(h_f, p + 1)
            v.tensor_scalar(hk, fr, -1.0, 1.0, ALU.mult, ALU.add).then_inc(h_k, 1)
            v.wait_ge(h_sigq, p + 1)
            v.tensor_tensor(hq, qr, dif[0], ALU.mult).then_inc(h_q, 1)

        def head_ln_act(act, p):
            act.wait_ge(h_k, p + 1)
            act.activation(fr, fr, ACT.Ln).then_inc(h_lnf, 1)

        def head_scan_dve(v, p):
            v.wait_ge(h_lnf, p + 1)
            v.tensor_tensor_scan(hb, not_first[:], fr, 0.0, ALU.mult, ALU.add).then_inc(h_b, 1)

        def head_decays_act(act, p):
            act.wait_ge(h_b, p + 1)
            act.wait_ge(h_o, p + 1)
            act.activation(qe, hb, ACT.Exp).then_inc(h_eb, 1)
            act.activation(ebl, hb[:, P - 1::P], ACT.Exp).then_inc(h_ebl, 1)
            act.wait_ge(h_z, 8 * p + 1)
            for i in range(TB):
                act.activation(dif[1][:, i * P:(i + 1) * P], hb[:, i * P:(i + 1) * P], ACT.Exp, scale=-1.0,
                               bias=hb[:, (i + 1) * P - 1:(i + 1) * P]).then_inc(h_kexp, 1)

        def head_kdec_pool(g, p):
            g.wait_ge(h_kexp, TB * p + TB)
            g.wait_ge(h_zread, 8 * p + 1)
            g.tensor_tensor(zz[1], hk, dif[1], ALU.mult).then_inc(h_z, 1)

        def level_dif_dve(v, p, L):
            b, o = piece(hb, L), piece(dif[L % 2], L)
            n, m = SEQ // (128 >> L), 64 >> L
            ref = b[:, :, 0, m - 1:m].to_broadcast([P, n, m])
            v.wait_ge(h_z, 8 * p + L + 2)
            v.wait_ge(h_b, p + 1)
            v.tensor_tensor(o[:, :, 0], ref, b[:, :, 0], ALU.subtract).then_inc(h_dif, 1)
            v.tensor_tensor(o[:, :, 1], b[:, :, 1], ref, ALU.subtract).then_inc(h_dif, 1)

        def level_exp_act(act, p, L):
            act.wait_ge(h_dif, 14 * p + 2 * L + 2)
            act.activation(dif[L % 2], dif[L % 2], ACT.Exp).then_inc(h_e, 1)

        def level_z_pool(g, p, L):
            e, o = piece(dif[L % 2], L), piece(zz[L % 2], L)
            g.wait_ge(h_e, 7 * p + L + 1)
            g.wait_ge(h_q, p + 1)
            g.wait_ge(h_zread, 8 * p + L + 2)
            g.tensor_tensor(o[:, :, 0], piece(hk, L)[:, :, 0], e[:, :, 0], ALU.mult).then_inc(h_zhalf, 1)
            g.wait_ge(h_zhalf, 7 * p + L + 1)
            g.tensor_tensor(o[:, :, 1], piece(hq, L)[:, :, 1], e[:, :, 1], ALU.mult).then_inc(h_z, 1)

        def level_scores_pe(pe, p, L):
            pe.wait_ge(h_cp, 8 * p + L + 1)
            if L < NLEV - 1:
                pe.wait_ge(h_z, 8 * p + L + 2 + CR)
                a = c = zz[L % 2]
            else:
                pe.wait_ge(h_k, p + 1)
                pe.wait_ge(h_q, p + 1)
                a, c = hk, hq
            for i in range(TB):
                mm = pe.matmul(LB[L % 2][:, i * P:(i + 1) * P], a[:, i * P:(i + 1) * P], c[:, i * P:(i + 1) * P],
                               start=True, stop=True)
            mm.then_inc(h_sc if L == NLEV - 1 else h_zread, 1)

        def level_take_dve(v, p, L):
            if L < NLEV - 1:
                v.wait_ge(h_zread, 8 * p + L + 2 + CR)
            else:
                v.wait_ge(h_sc, p + 1)
            if L == 0:
                v.wait_ge(h_o, p + 1)
            else:
                v.wait_ge(h_cp, 8 * p + L + CR)
            v.sem_inc(h_takes, 1)
            v.copy_predicated(score_acc[:].rearrange("p (n t) -> p n t", t=P),
                              level_mask[:, L * P:(L + 1) * P].unsqueeze(1).to_broadcast([P, TB, P]),
                              LB[L % 2][:].rearrange("p (n t) -> p n t", t=P)).then_inc(h_cp, 1)

        def head_turns_pe(pe, p):
            pe.wait_ge(acc_read[1], R0 + 2 * p + 1)
            pe.wait_ge(s_pts, 8 * p + 8 + CR)
            for i in range(TB):
                mm = pe.transpose(PTP[0][:, i * P:(i + 1) * P], ir[:, i * P:(i + 1) * P], ident)
            mm.then_inc(h_vturned, 1)
            pe.wait_ge(h_z, 8 * p + 1 + CR)
            for i in range(TB):
                mm = pe.transpose(PTP[1][:, i * P:(i + 1) * P], zz[1][:, i * P:(i + 1) * P], ident)
            mm.then_inc(h_zread, 1)

        def head_nat_act(act, p):
            act.wait_ge(h_vturned, p + 1)
            act.activation(hVn, PTP[0][:], ACT.Copy).then_inc(h_vnat, 1)
            act.wait_ge(h_zread, 8 * p + 1 + CR)
            act.wait_ge(o_turned, GROUPS + 2 * p + 1)
            act.activation(o_kN, PTP[1][:], ACT.Copy).then_inc(h_kn, 1)

        def head_state_pe(pe, p):
            pe.wait_ge(h_vnat, p + 1)
            pe.wait_ge(h_kn, p + 1)
            for i in range(TB - 1):
                mm = pe.matmul(PTP[0][:, i * P:(i + 1) * P], o_kN[:, i * P:(i + 1) * P], hVn[:, i * P:(i + 1) * P],
                               start=True, stop=True)
            mm.then_inc(h_u, 1)

        def head_state_dve(v, p):
            v.wait_ge(h_u, p + 1)
            v.wait_ge(h_ebl, p + 1)
            v.wait_ge(h_o, p + 1)
            v.tensor_copy(o_state[:, 0:P], PTP[0][:, 0:P]).then_inc(h_state, 1)
            for i in range(1, TB - 1):
                v.wait_ge(h_state, 3 * p + i + 1)
                v.scalar_tensor_tensor(o_state[:, i * P:(i + 1) * P], o_state[:, (i - 1) * P:i * P], ebl[:, i:i + 1],
                                       PTP[0][:, i * P:(i + 1) * P], ALU.mult, ALU.add).then_inc(h_state, 1)

        def head_out_pe(pe, p):
            pe.wait_ge(h_cp, 8 * p + 8 + CR)
            pe.wait_ge(h_state, 3 * p + 4)
            pe.wait_ge(h_qe, p + 1)
            pe.wait_ge(on_ready, 2 * p + GROUPS + 2)
            for i in range(TB):
                t = slice(i * P, (i + 1) * P)
                if i:
                    pe.matmul(OP[:, t], qe[:, t], o_state[:, (i - 1) * P:i * P], start=True, stop=False)
                mm = pe.matmul(OP[:, t], score_acc[:, t], hVn[:, t], start=(i == 0), stop=True)
            mm.then_inc(h_o, 1)

        def out_turn_pe(pe, n, src):
            pe.wait_ge(on_ready, n + 2)
            for i in range(TB):
                mm = pe.transpose(S[0][:, i * P:(i + 1) * P], src[:, i * P:(i + 1) * P], ident)
            mm.then_inc(o_turned, 1)

        def body_pe(pe, p, kv, last=False):
            def chunks(s, r, c0, c1):
                if not last:
                    odd_chunks(pe, s, r, c0, c1)
            rq, ri, rf = R0 + 2 + 2 * p, R0 + 2 + 2 * p, GROUPS + 3 + p
            for n in range(8):
                swa_scores(pe, p, n, kv)
                chunks(0, rq, n, n + 1)
                if n >= 1:
                    swa_turn(pe, p, n - 1)
                if n >= 2:
                    swa_pv(pe, p, n - 2, kv)
            chunks(1, ri, 0, 2)
            swa_turn(pe, p, 7)
            swa_pv(pe, p, 6, kv)
            chunks(1, ri, 2, 4)
            swa_pv(pe, p, 7, kv)
            head_turns_pe(pe, p)
            chunks(1, ri, 4, 8)
            out_turn_pe(pe, GROUPS + 2 * p, o_on)
            chunks(2, rf, 0, 2)
            head_state_pe(pe, p)
            plan = [(2, rf, 2, 4), (2, rf, 4, 6), (2, rf, 6, 8), (0, rq + 1, 0, 3), (0, rq + 1, 3, 6), (0, rq + 1, 6, 8),
                    (1, ri + 1, 0, 2), (1, ri + 1, 2, 4)]
            for L in range(NLEV):
                level_scores_pe(pe, p, L)
                chunks(*plan[L])
            head_out_pe(pe, p)
            chunks(1, ri + 1, 4, 8)
            out_turn_pe(pe, GROUPS + 2 * p + 1, o_on)

        def body_act(act, p, last=False):
            def hi(s, r):
                if not last:
                    act_hi(act, s, r)
            rq, ri, rf = R0 + 2 + 2 * p, R0 + 2 + 2 * p, GROUPS + 3 + p
            head_start_act(act, p)
            head_ln_act(act, p)
            swa_exp(act, p, 0)
            hi(1, ri)
            swa_exp(act, p, 1)
            swa_pts(act, p, 0)
            for n in range(2, 8):
                swa_exp(act, p, n)
                swa_pts(act, p, n - 1)
            head_decays_act(act, p)
            swa_pts(act, p, 7)
            act.wait_ge(s_sinkx, p + 1)
            act.activation(sinke, sinkx, ACT.Exp).then_inc(s_sinke, 1)
            hi(2, rf)
            act.wait_ge(o_turned, GROUPS + 2 * p + 1)
            act.activation(oh[:, p], S[0][:], ACT.Copy).then_inc(oh_ready, 1)
            head_nat_act(act, p)
            for L in range(NLEV - 1):
                level_exp_act(act, p, L)
                if L == 1:
                    hi(0, rq + 1)
                if L == 4:
                    hi(1, ri + 1)
            act.wait_ge(h_o, p + 2)
            row_rms_act(act, DIFF_G + p, oPT[0])
            hi(0, rq + 2)
            act.wait_ge(h_gated, p + 1)
            act.activation(oh[:, p + 4], oPT[1], ACT.Copy).then_inc(oh_ready, 1)

        def body_dve(v, p, last=False):
            def lo(s, r):
                if not last:
                    dve_lo(v, s, r)

            def take(dst, s, r, scale=None, waits=()):
                if last:
                    return
                v.wait_ge(unit_done[s], r + 1)
                for w in waits:
                    v.wait_ge(*w)
                if scale is None:
                    v.tensor_tensor(dst, acc[s][:], rstd[:], ALU.mult).then_inc(acc_read[s], 1)
                else:
                    v.scalar_tensor_tensor(dst, acc[s][:], scale, rstd[:], ALU.mult, ALU.mult).then_inc(acc_read[s], 1)
            rq, ri, rf = R0 + 2 + 2 * p, R0 + 2 + 2 * p, GROUPS + 3 + p
            head_f_dve(v, p)
            swa_max(v, p, 0)
            swa_max(v, p, 1)
            head_scan_dve(v, p)
            lo(1, ri)
            for n in range(2, 8):
                swa_max(v, p, n)
            v.wait_ge(s_max, 8 * p + 8)
            v.tensor_tensor(sinkx.rearrange("p (i m) -> p i m", m=2), nmax.rearrange("p (i m) -> p i m", m=2),
                            sm[:, bass.ds(SINK + 2 * p, 2)].unsqueeze(1).to_broadcast([P, 4, 2]), ALU.add).then_inc(s_sinkx, 1)
            take(work[:, 0], 0, rq, QSCALE)
            v.wait_ge(h_eb, p + 1)
            v.wait_ge(h_q, p + 1)
            v.tensor_tensor(qe, qe, hq, ALU.mult).then_inc(h_qe, 1)
            v.wait_ge(s_sinke, p + 1)
            v.wait_ge(s_exp, 8 * p + 8 + CR)
            v.tensor_tensor(rsum, rsum, sinke, ALU.add).then_inc(s_sum, 1)
            v.wait_ge(s_sum, p + 1)
            v.reciprocal(rinv, rsum).then_inc(s_rinv, 1)
            v.wait_ge(s_pv, 8 * p + 8 + CR)
            v.wait_ge(s_rinv, p + 2)
            v.wait_ge(o_turned, GROUPS + 2 * p)
            v.tensor_tensor(o_on.rearrange("p (n d) -> p n d", d=HD), OP[:].rearrange("p (n d) -> p n d", d=HD),
                            rinv.unsqueeze(2).to_broadcast([P, 8, HD]), ALU.mult).then_inc(on_ready, 1)
            level_dif_dve(v, p, 0)
            lo(2, rf)
            level_dif_dve(v, p, 1)
            take(ir, 1, ri, waits=[(h_vturned, p + 1)])
            v.wait_ge(oh_ready, GROUPS + 2 * p + 1)
            v.tensor_tensor(ol[:, p], S[0][:], oh[:, p].bitcast(F32), ALU.subtract).then_inc(ol_ready, 1)
            head_state_dve(v, p)
            for L in range(NLEV):
                level_take_dve(v, p, L)
                if L + 2 < NLEV - 1:
                    level_dif_dve(v, p, L + 2)
                if L == 1:
                    lo(0, rq + 1)
                if L == 3:
                    take(fr, 2, rf)
                if L == 4:
                    lo(1, ri + 1)
                if L == 6:
                    take(qr, 0, rq + 1)
            row_mean_dve(v, DIFF_G + p)
            row_rms_dve(v, DIFF_G + p, o_on)
            lo(0, rq + 2)
            v.wait_ge(o_turned, GROUPS + 2 * p + 2)
            v.wait_ge(h_sigg, p + 1)
            v.scalar_tensor_tensor(oPT[1], S[0][:], sm[:, HGRNN:HGRNN + 1], sgate, ALU.mult, ALU.mult).then_inc(h_gated, 1)
            take(gr, 1, ri + 1)
            v.wait_ge(oh_ready, GROUPS + 2 * p + 2)
            v.wait_ge(h_gated, p + 1)
            v.tensor_tensor(ol[:, p + 4], oPT[1], oh[:, p + 4].bitcast(F32), ALU.subtract).then_inc(ol_ready, 1)

        def body_pool(g, p):
            head_kdec_pool(g, p)
            for L in range(NLEV - 1):
                level_z_pool(g, p, L)

        ODD_FIRST = ((2, GROUPS), (0, R0), (2, GROUPS + 1), (1, R0), (2, GROUPS + 2), (0, R0 + 1), (1, R0 + 1))

        def odd_pe(pe, l):
            for n, (s, r) in enumerate(ODD_FIRST):
                pe_unit(pe, s, r, DC, xh, xl)
                if n == 3:
                    pe.wait_ge(acc_read[2], GROUPS + 2)
                    for i in range(TB):
                        mm = pe.transpose(PTP[0][:, i * P:(i + 1) * P], o_vT[:, i * P:(i + 1) * P], ident)
                    mm.then_inc(sv_turned, 1)
            pe.wait_ge(sv_nat, 1)
            with pe.Fori(0, 2) as p:
                body_pe(pe, p, 0)
            body_pe(pe, 2, 1)
            body_pe(pe, 3, 1, last=True)

        def odd_act(act, l):
            for n, (s, r) in enumerate(ODD_FIRST):
                if n:
                    act_hi(act, s, r)
                if n == 4:
                    act.wait_ge(sv_turned, 1)
                    act.activation(o_Vn, PTP[0][:], ACT.Copy).then_inc(sv_nat, 1)
            act.wait_ge(lb_step, 3)
            act.activation(ge, gd, ACT.Exp).then_inc(lb_exp, 1)
            act_hi(act, 0, R0 + 2)
            with act.Fori(0, 3) as p:
                body_act(act, p)
            body_act(act, 3, last=True)

        def odd_dve(v, l):
            def take(dst, s, r, scale=None):
                v.wait_ge(unit_done[s], r + 1)
                if scale is None:
                    v.tensor_tensor(dst, acc[s][:], rstd[:], ALU.mult).then_inc(acc_read[s], 1)
                else:
                    v.scalar_tensor_tensor(dst, acc[s][:], scale, rstd[:], ALU.mult, ALU.mult).then_inc(acc_read[s], 1)
            v.tensor_scalar(nsink, sm[:, SINK:SINK + 8], -1.0, None, ALU.mult).then_inc(nsink_ready, 1)
            g0, g1 = sm[:, GAM:GAM + 4], sm[:, GAM + 4:GAM + 8]
            v.tensor_tensor(gmx, g0, g1, ALU.max).then_inc(lb_step, 1)
            v.wait_ge(lb_step, 1)
            v.tensor_tensor(gd[:, 0:4], g0, gmx, ALU.subtract).then_inc(lb_step, 1)
            v.tensor_tensor(gd[:, 4:8], g1, gmx, ALU.subtract).then_inc(lb_step, 1)
            dve_lo(v, 0, R0)
            v.wait_ge(unit_done[2], GROUPS + 1)
            for n, (h, half) in enumerate(((0, 0), (0, 1), (1, 0), (1, 1))):
                src, dst = slice(HD * h, HD * h + HD), slice(HD * half, HD * half + HD)
                v.tensor_tensor(KV[h][dst, :], acc[2][src, :], rstd[src, :], ALU.mult).then_inc(
                    acc_read[2] if n == 3 else k_made, 1)
            dve_lo(v, 2, GROUPS + 1)
            take(work[:, 0], 0, R0, QSCALE)
            dve_lo(v, 1, R0)
            take(o_vT, 2, GROUPS + 1)
            dve_lo(v, 2, GROUPS + 2)
            take(ir, 1, R0)
            dve_lo(v, 0, R0 + 1)
            take(fr, 2, GROUPS + 2)
            dve_lo(v, 1, R0 + 1)
            take(qr, 0, R0 + 1)
            v.wait_ge(lb_exp, 1)
            v.tensor_tensor(gsum, ge[:, 0:4], ge[:, 4:8], ALU.add).then_inc(lb_step, 1)
            v.wait_ge(lb_step, 4)
            v.reciprocal(grec, gsum).then_inc(lb_step, 1)
            v.wait_ge(lb_step, 5)
            v.tensor_tensor(gsm[:, 0:4], ge[:, 0:4], grec, ALU.mult).then_inc(lb_step, 1)
            v.tensor_tensor(gsm[:, 4:8], ge[:, 4:8], grec, ALU.mult).then_inc(lb_step, 1)
            v.wait_ge(lb_step, 7)
            v.tensor_tensor(glb, gsm[:, 0:4], gsm[:, 4:8], ALU.add).then_inc(lb_step, 1)
            v.wait_ge(lb_step, 8)
            v.tensor_tensor(glb, glb, gsm[:, 0:4], ALU.subtract).then_inc(lb_step, 1)
            v.wait_ge(lb_step, 9)
            v.tensor_scalar(goml, glb, -1.0, 1.0, ALU.mult, ALU.add).then_inc(lb_step, 1)
            v.wait_ge(lb_step, 10)
            v.wait_ge(nsink_ready, 1)
            dve_lo(v, 0, R0 + 2)
            take(gr, 1, R0 + 1)
            with v.Fori(0, 3) as p:
                body_dve(v, p)
            body_dve(v, 3, last=True)

        def odd_pool(g, l):
            with g.Fori(0, 4) as p:
                body_pool(g, p)

        gs, us, sg, gg = (work[:, i] for i in range(4))
        silu_ready, g_ready, gh_ready, gl_ready = sem("silu_ready"), sem("g_ready"), sem("gh_ready"), sem("gl_ready")
        out_sent, y_out = sem("out_sent"), sem("y_out")

        def F_act(act):
            for l in range(layers):
                if l % 2:
                    odd_act(act, l)
                k = 2 * l + 1
                r0 = PH["mix_out", l]
                with act.Fori(0, 3) as i:
                    out_pair_act(act, 2 * i, r0 + i, LN_FFN + DC * l, DC * k, True)
                out_pair_act(act, 6, r0 + 3, LN_FFN + DC * l, DC * k, False)
                act_hi(act, 0, PH["gu", l, 0])
                act_xh(act, 7, LN_FFN + DC * l + 7, 0, (acc_read[1], r0 + 4))
                act_rsqrt(act, k)
                for half in range(2):
                    r0 = PH["gu", l, half]
                    n0 = FT * l + FH * half
                    with act.Fori(0, FH - 1) as i:
                        gu_pair_act(act, i, r0 + i, n0 + i)
                        act_hi(act, 0, r0 + i + 1)
                        gu_gh_act(act, i, n0 + i)
                    gu_pair_act(act, FH - 1, r0 + FH - 1, n0 + FH - 1)
                    act_hi(act, 0, PH["dn", l, half], FH * P)
                    gu_gh_act(act, FH - 1, n0 + FH - 1)
                    r0 = PH["dn", l, half]
                    final = l == layers - 1 and half == 1
                    nextg = LN_MIX + DC * (l + 1)
                    if half == 0 or final:
                        with act.Fori(0, 3) as i:
                            act_hi(act, 1, r0 + i, FH * P)
                            act_hi(act, 0, r0 + i + 1, FH * P)
                        act_hi(act, 1, r0 + 3, FH * P)
                        if not final:
                            act_hi(act, 0, r0 + 4)
                        else:
                            act_rsqrt(act, 2 * layers)
                    else:
                        with act.Fori(0, 3) as i:
                            act_hi(act, 1, r0 + i, FH * P)
                            act_xh(act, 2 * i, nextg + 2 * i, 0, (acc_read[0], r0 + i + 1))
                            act_hi(act, 0, r0 + i + 1, FH * P)
                            act_xh(act, 2 * i + 1, nextg + 2 * i + 1, 0, (acc_read[1], r0 + i + 1))
                        act_hi(act, 1, r0 + 3, FH * P)
                        act_xh(act, 6, nextg + 6, 0, (acc_read[0], r0 + 4))
                        act_hi(act, 2, GROUPS)
                        act_xh(act, 7, nextg + 7, 0, (acc_read[1], r0 + 4))
                        act_rsqrt(act, 2 * l + 2)

        def out_pair_act(act, j, r, gcol, n, ahead):
            act_hi(act, 1, r)
            act_xh(act, j, gcol + j, 0, (acc_read[0], r + 1))
            if ahead:
                act_hi(act, 0, r + 1)
                act_xh(act, j + 1, gcol + j + 1, 0, (acc_read[1], r + 1))

        def gu_pair_act(act, t, r, n):
            act_hi(act, 1, r)
            act.wait_ge(acc_read[0], r + 1)
            act.activation(sg, gs, ACT.Silu).then_inc(silu_ready, 1)

        def gu_gh_act(act, t, n):
            act.wait_ge(g_ready, n + 1)
            act.activation(gh[:, t], gg, ACT.Copy).then_inc(gh_ready, 1)

        def x_add(v, s, j, r):
            v.wait_ge(unit_done[s], r + 1)
            v.tensor_tensor(x[:, j], acc[s][:], x[:, j], ALU.add).then_inc(acc_read[s], 1)

        def x_tile_split(v, s, j, r, gcol, n):
            x_add(v, s, j, r)
            v.wait_ge(acc_read[s], r + 1)
            dve_xl(v, j, gcol + j, n)

        def gate_dve(v, r):
            dve_lo(v, 1, r)
            v.wait_ge(unit_done[0], r + 1)
            v.tensor_tensor(gs, acc[0][:], rstd[:], ALU.mult).then_inc(acc_read[0], 1)

        def up_dve(v, t, r, n):
            v.wait_ge(unit_done[1], r + 1)
            v.tensor_tensor(us, acc[1][:], rstd[:], ALU.mult).then_inc(acc_read[1], 1)
            v.wait_ge(silu_ready, n + 1)
            v.wait_ge(acc_read[1], r + 1)
            v.tensor_tensor(gg, sg, us, ALU.mult).then_inc(g_ready, 1)
            v.wait_ge(gh_ready, n + 1)
            v.wait_ge(g_ready, n + 1)
            v.tensor_tensor(gl[:, t], gg, gh[:, t].bitcast(F32), ALU.subtract).then_inc(gl_ready, 1)

        def F_dve(v):
            for l in range(layers):
                if l % 2:
                    odd_dve(v, l)
                k = 2 * l + 1
                r0 = PH["mix_out", l]
                gc = LN_FFN + DC * l
                with v.Fori(0, 3) as i:
                    dve_lo(v, 1, r0 + i)
                    x_tile_split(v, 0, 2 * i, r0 + i, gc, DC * k + 2 * i)
                    dve_lo(v, 0, r0 + i + 1)
                    x_tile_split(v, 1, 2 * i + 1, r0 + i, gc, DC * k + 2 * i + 1)
                dve_lo(v, 1, r0 + 3)
                x_tile_split(v, 0, 6, r0 + 3, gc, DC * k + 6)
                dve_lo(v, 0, PH["gu", l, 0])
                x_tile_split(v, 1, 7, r0 + 3, gc, DC * k + 7)
                dve_mean(v, k)
                dve_newton(v, k)
                v.wait_ge(rstd_ready, k + 1)
                for half in range(2):
                    r0 = PH["gu", l, half]
                    n0 = FT * l + FH * half
                    with v.Fori(0, FH - 1) as i:
                        gate_dve(v, r0 + i)
                        dve_lo(v, 0, r0 + i + 1)
                        up_dve(v, i, r0 + i, n0 + i)
                    rd = PH["dn", l, half]
                    gate_dve(v, r0 + FH - 1)
                    dve_lo(v, 0, rd, FH * P)
                    up_dve(v, FH - 1, r0 + FH - 1, n0 + FH - 1)
                    final = l == layers - 1 and half == 1
                    nextg = LN_MIX + DC * (l + 1)
                    kn = 2 * l + 2
                    if half == 0 or final:
                        with v.Fori(0, 3) as i:
                            dve_lo(v, 1, rd + i, FH * P)
                            x_add(v, 0, 2 * i, rd + i)
                            dve_lo(v, 0, rd + i + 1, FH * P)
                            x_add(v, 1, 2 * i + 1, rd + i)
                        dve_lo(v, 1, rd + 3, FH * P)
                        x_add(v, 0, 6, rd + 3)
                        if not final:
                            dve_lo(v, 0, rd + 4)
                        x_add(v, 1, 7, rd + 3)
                    else:
                        with v.Fori(0, 3) as i:
                            dve_lo(v, 1, rd + i, FH * P)
                            x_tile_split(v, 0, 2 * i, rd + i, nextg, DC * kn + 2 * i)
                            dve_lo(v, 0, rd + i + 1, FH * P)
                            x_tile_split(v, 1, 2 * i + 1, rd + i, nextg, DC * kn + 2 * i + 1)
                        dve_lo(v, 1, rd + 3, FH * P)
                        x_tile_split(v, 0, 6, rd + 3, nextg, DC * kn + 6)
                        dve_lo(v, 2, GROUPS)
                        x_tile_split(v, 1, 7, rd + 3, nextg, DC * kn + 7)
                        dve_mean(v, kn)
                        dve_newton(v, kn)
                        v.wait_ge(rstd_ready, kn + 1)

        def F_pe(pe):
            for l in range(layers):
                if l % 2:
                    odd_pe(pe, l)
                k = 2 * l + 1
                r0 = PH["mix_out", l]
                pe.wait_ge(ol_ready, (DC if l == 0 else DC + DC) + 1)
                with pe.Fori(0, 4) as i:
                    for s in range(2):
                        pe_unit(pe, s, r0 + i, DC, oh, ol)
                pe_stat(pe, k)
                for half in range(2):
                    r0 = PH["gu", l, half]
                    n0 = FT * l + FH * half
                    if half == 0:
                        pe.wait_ge(xl_ready, DC * (k + 1))
                    with pe.Fori(0, FH) as i:
                        for s in range(2):
                            pe_unit(pe, s, r0 + i, DC, xh, xl)
                    pe.wait_ge(gl_ready, n0 + FH)
                    with pe.Fori(0, 4) as i:
                        for s in range(2):
                            pe_unit(pe, s, PH["dn", l, half] + i, FH, gh, gl)
                pe_stat(pe, 2 * l + 2)
                if l < layers - 1:
                    pe.wait_ge(xl_ready, DC * (k + 2))

        def F_sp(sp):
            for l in range(layers):
                if l % 2:
                    r0 = PH["odd_in", l]
                    for n, (s, r) in enumerate(((2, GROUPS), (0, r0), (2, GROUPS + 1), (1, r0), (2, GROUPS + 2),
                                                (0, r0 + 1), (1, r0 + 1))):
                        sp_load(sp, s, r, w_odd[n], UNIT8)
                    with sp.Fori(0, 3) as p:
                        for n, (s, r) in enumerate(((0, r0 + 2 + 2 * p), (1, r0 + 2 + 2 * p), (2, GROUPS + 3 + p),
                                                    (0, r0 + 3 + 2 * p), (1, r0 + 3 + 2 * p))):
                            sp_load(sp, s, r, w_odd[7 + 5 * p + n], UNIT8)
                r0 = PH["mix_out", l]
                w = w_out_o if l % 2 else w_out_e
                with sp.Fori(0, 4) as i:
                    for s in range(2):
                        sp_load(sp, s, r0 + i, w[2 * i + s], UNIT8)
                for half in range(2):
                    r0 = PH["gu", l, half]
                    with sp.Fori(0, FH) as i:
                        for s in range(2):
                            sp_load(sp, s, r0 + i, w_gu[l, FH * half + i, s], UNIT8)
                    r0 = PH["dn", l, half]
                    with sp.Fori(0, 4) as i:
                        for s in range(2):
                            sp_load(sp, s, r0 + i, w_dn[l, half, 2 * i + s], FH * P)

        def square_tile(g, s, j, r, n, k):
            pool_sq(g, j, n, k, (acc_read[s], r + 1))

        def F_pool(g):
            for l in range(layers):
                if l % 2:
                    odd_pool(g, l)
                k = 2 * l + 1
                for kk, r0 in ((k, PH["mix_out", l]), (k + 1, PH["dn", l, 1])):
                    pool_zero(g, kk)
                    with g.Fori(0, 4) as i:
                        for s in range(2):
                            square_tile(g, s, 2 * i + s, r0 + i, DC * kk + 2 * i + s, kk)

        @block.sync
        def _(sp):
            sp.dma_start(sm[:], small).then_inc(small_in, 16)
            sp.dma_start(x[:, 0:4], xT[:, 0:4]).then_inc(x_in, 16)
            sp_load(sp, 0, 0, w_even[0], UNIT8)
            sp.dma_start(x[:, 4:8], xT[:, 4:8]).then_inc(x_in, 16)
            sp.dma_start(fa_raw[:], w_fa).then_inc(fa_in, 16)
            sp_load(sp, 1, 0, w_even[1], UNIT8)
            sp_load(sp, 2, 0, w_even[2], UNIT8)
            sp.dma_start(const_stage[:, 0:NCONST], const).then_inc(const_in, 16)
            sp.dma_start(ident, const[:, C_ID:C_ID + P]).then_inc(const_in, 16)
            sp.wait_ge(gate_step, 9)
            sp.wait_ge(cq_ones, 2)
            for a, src in enumerate((cpart[:, 0], cpart[:, 1], cpart2[:, 0])):
                sp.dma_start(CQ[a:a + 1], src).then_inc(cq_in, 16)
            for a, src in enumerate((cpartn[0][:, 0], cpartn[0][:, 1], cpartn[1][:, 0])):
                sp.dma_start(CK[3 + a:4 + a], src).then_inc(cq_in, 16)
            with sp.Fori(1, GROUPS) as G:
                for s in range(3):
                    sp_load(sp, s, G, w_even[3 * G + s], UNIT8)
            F_sp(sp)
            for j in range(DC):
                sp.wait_ge(y_out, j + 1)
                sp.dma_start(out[:, j], x[:, j]).then_inc(out_sent, 16)
            sp.wait_ge(out_sent, 16 * DC)

        @block.gpsimd
        def _(g):
            g.memset(ones[:], 1.0).then_inc(ones_ready, 1)
            g.memset(meanw[:], 1.0 / D).then_inc(ones_ready, 1)
            g.memset(score_acc[:], 0.0).then_inc(ones_ready, 1)
            g.memset(work[0:6, 11:19], 0.0).then_inc(cq_ones, 1)
            g.wait_ge(cq_ones, 1)
            g.memset(work[0:6, 11:19].bitcast(BF16), 1.0).then_inc(cq_ones, 1)
            pool_zero(g, 0)
            for j in range(DC):
                pool_sq(g, j, j, 0, (x_in, 32))
            g.wait_ge(cq_in, 16 * 6)
            g.tensor_copy(cq_cur[0:6], CQ[0:6, 0:2]).then_inc(cq_staged, 1)
            with g.Fori(1, FOX_G) as G:
                g.wait_ge(f_scores, 8 * G)
                g.tensor_copy(cq_cur[0:6], CQ[0:6, bass.ds(2 * G, 2)]).then_inc(cq_staged, 1)
            F_pool(g)

        @block.scalar
        def _(act):
            act.wait_ge(small_in, 16)
            for j in range(DC):
                act_xh(act, j, LN_MIX + j, j, (x_in, 32))
            act_hi(act, 0, 0)
            act.wait_ge(fa_in, 16)
            act.activation(fa_h[:], fa_raw[:], ACT.Copy).then_inc(fa_hi, 1)
            act_rsqrt(act, 0)
            act_hi(act, 1, 0)
            act_hi(act, 2, 0)
            act.wait_ge(const_in, 32)
            act.activation(cstb[:], const_stage[:, 0:C_LEV], ACT.Copy).then_inc(const_b, 1)
            act.activation(level_mask[:], const_stage[:, C_LEV:C_FIRST], ACT.Copy).then_inc(const_b, 1)
            for i in range(TB):
                act.activation(not_first[:, i * P:(i + 1) * P], const_stage[:, C_FIRST:NCONST], ACT.Copy).then_inc(const_b, 1)
            act.wait_ge(gate_step, 2)
            act.activation(za, z, ACT.Abs).then_inc(gate_act, 1)
            act.wait_ge(gate_act, 1)
            act.activation(za, za, ACT.Exp, scale=-1.0).then_inc(gate_act, 1)
            act.wait_ge(gate_act, 2)
            act.activation(za, za, ACT.Ln, bias=1.0).then_inc(gate_act, 1)
            act.wait_ge(lam_sum, 1)
            act.activation(lamt[:, 2:4], OP[:, 0:2], ACT.Exp).then_inc(lam_exp, 1)
            act_hi(act, 0, 1)
            with act.Fori(0, FOX_G) as g:
                fox_group_act(act, g)
            with act.Fori(0, DIFF_G - 1) as g:
                diff_group_act(act, g)
            diff_group_act(act, DIFF_G - 1, last=True)
            F_act(act)

        @block.vector
        def _(v):
            for s in (f_exp, f_turned, f_pv, d_exp, d_mix, d_turned, d_pts, d_pv):
                v.sem_inc(s, CR)
            for s in (s_exp, s_turned, s_pts, s_pv, h_cp, h_z, h_zread):
                v.sem_inc(s, CR)
            for s in (ol_ready, on_ready, rinv_ready, *f_pts, s_rinv, h_o, h_state):
                v.sem_inc(s, 1)
            v.wait_ge(small_in, 16)
            v.wait_ge(x_in, 32)
            for j in range(DC):
                dve_xl(v, j, LN_MIX + j, j)
            dve_lo(v, 0, 0)
            v.wait_ge(fa_hi, 1)
            v.tensor_tensor(fa_l[:], fa_raw[:], fa_h[:].bitcast(F32), ALU.subtract).then_inc(fa_lo, 1)
            dve_mean(v, 0)
            dve_newton(v, 0)
            v.wait_ge(rstd_ready, 1)
            dve_lo(v, 1, 0)
            v.wait_ge(fa_done, 1)
            v.tensor_tensor(z, acc[2][0:8, :], rstd[0:8, :], ALU.mult).then_inc(gate_step, 1)
            v.wait_ge(gate_step, 1)
            v.tensor_scalar(z, z, sm[0:8, BFG:BFG + 1], None, ALU.add).then_inc(gate_step, 1)
            v.tensor_tensor(lamt[0:HD, 0:2], sm[0:HD, LAMB:LAMB + 2], sm[0:HD, LAMB + 2:LAMB + 4],
                            ALU.mult).then_inc(lam_prod, 1)
            dve_lo(v, 2, 0)
            dve_q(v, 0)
            v.wait_ge(gate_act, 3)
            v.scalar_tensor_tensor(z, z, 0.0, za, ALU.min, ALU.subtract).then_inc(gate_step, 1)
            v.wait_ge(gate_step, 3)
            v.wait_ge(ones_ready, 3)
            v.tensor_tensor_scan(cum, z, z, 0.0, ALU.add, ALU.bypass).then_inc(gate_step, 1)
            v.wait_ge(gate_step, 4)
            v.tensor_copy(cpart[:, 0], cum).then_inc(gate_step, 1)
            v.wait_ge(gate_step, 5)
            v.tensor_tensor(z, cum, cpart[:, 0], ALU.subtract).then_inc(gate_step, 1)
            v.wait_ge(gate_step, 6)
            v.tensor_copy(cpart[:, 1], z).then_inc(gate_step, 1)
            v.wait_ge(gate_step, 7)
            v.tensor_tensor(cpart2[:, 0], z, cpart[:, 1], ALU.subtract).then_inc(gate_step, 1)
            v.wait_ge(gate_step, 8)
            v.tensor_scalar(cpartn[0], cpart, -1.0, None, ALU.mult)
            v.tensor_scalar(cpartn[1][:, 0], cpart2[:, 0], -1.0, None, ALU.mult).then_inc(gate_step, 1)
            dve_k(v, 0)
            v.wait_ge(lam_exp, 1)
            v.tensor_tensor(lamt[:, 4:5], lamt[:, 3:4], lamt[:, 2:3], ALU.subtract).then_inc(lam_ready, 1)
            v.wait_ge(lam_ready, 1)
            v.tensor_scalar(lamt[:, 7:8], lamt[:, 4:5], -LAMBDA_INIT, None, ALU.add).then_inc(lam_ready, 1)
            v.tensor_scalar(dscale, sm[:, DIFFN:DIFFN + 1], 1.0 - LAMBDA_INIT, None, ALU.mult).then_inc(lam_ready, 1)
            dve_v(v, 0)
            dve_lo(v, 0, 1)
            v.wait_ge(cq_in, 16 * 6)
            with v.Fori(0, FOX_G) as g:
                fox_group_dve(v, g)
            v.wait_ge(lam_ready, 3)
            with v.Fori(0, DIFF_G - 1) as g:
                diff_group_dve(v, g)
            diff_group_dve(v, DIFF_G - 1, last=True)
            F_dve(v)
            k = 2 * layers
            dve_mean(v, k)
            dve_newton(v, k)
            v.wait_ge(rstd_ready, k + 1)
            for j in range(DC):
                v.scalar_tensor_tensor(x[:, j], x[:, j], sm[:, LN_FIN + j:LN_FIN + j + 1], rstd[:],
                                       ALU.mult, ALU.mult).then_inc(y_out, 1)

        @block.tensor
        def _(pe):
            pe.wait_ge(xl_ready, DC)
            pe_unit(pe, 0, 0, DC, xh, xl)
            pe_stat(pe, 0)
            pe.wait_ge(fa_lo, 1)
            for c in range(DC):
                a, b = fa_h[:, 8 * c:8 * c + 8], fa_l[:, 8 * c:8 * c + 8]
                pe.matmul(acc[2][0:8, :], a, xh[:, c], start=(c == 0), stop=False)
                pe.matmul(acc[2][0:8, :], a, xl[:, c], start=False, stop=False)
                mm = pe.matmul(acc[2][0:8, :], b, xh[:, c], start=False, stop=(c == DC - 1))
            mm.then_inc(fa_done, 1)
            pe_unit(pe, 1, 0, DC, xh, xl)
            pe.wait_ge(lam_prod, 1)
            pe.wait_ge(mean_ready, 1)
            pe.matmul(OP[:, 0:2], ones[0:HD, :], lamt[0:HD, 0:2], start=True, stop=True).then_inc(lam_sum, 1)
            pe_unit(pe, 2, 0, DC, xh, xl)
            pe.wait_ge(const_b, 2 + TB)
            pe.wait_ge(cq_in, 16 * 6)
            with pe.Fori(0, FOX_G) as g:
                fox_group_pe(pe, g)
            with pe.Fori(0, DIFF_G - 1) as g:
                diff_group_pe(pe, g)
            diff_group_pe(pe, DIFF_G - 1, last=True)
            F_pe(pe)


def kernel(**inputs):
    import numpy as np
    import concourse.bacc as _bacc
    from concourse import mybir as _mybir
    from concourse.bass_utils import run_bass_kernel_spmd as _run
    layers = LAYERS

    a = {n: np.asarray(v) for n, v in inputs.items()}

    def tiles(w, cols, width=P):
        k = w.shape[0] // P
        return np.ascontiguousarray(np.stack([
            w[:, c:c + width].reshape(k, P, width).transpose(1, 0, 2).reshape(P, k * width) for c in cols]))

    def cols(v):
        return v.reshape(-1, P).T

    w = a["w_in_even"][0]
    starts = []
    for g in range(FOX_G):
        starts += [g * P, 512 + g * P, 1024 + g * P]
    for g in range(DIFF_G):
        starts += [1544 + g * P, 2056 + g * P, 2568 + g * P]
    small = np.zeros((P, NSMALL), np.float32)
    small[:, LN_MIX:LN_MIX + 16] = cols(a["ln_mix"])
    small[:, LN_FFN:LN_FFN + 16] = cols(a["ln_ffn"])
    small[:, LN_FIN:LN_FIN + 8] = cols(a["ln_final"])
    small[:, DIFFN:DIFFN + 1] = cols(a["diff_norm"])
    small[:, HGRNN:HGRNN + 1] = cols(a["hgrn_norm"])
    small[0:8, BFG] = a["b_forget"][0]
    for n, name in enumerate(("lambda_q1", "lambda_q2", "lambda_k1", "lambda_k2")):
        small[0:HD, LAMB + n] = a[name][0]
    small[:, SINK:SINK + 8] = a["sinks"]
    small[:, GAM:GAM + 8] = cols(a["hgrn_gamma"])
    def hgrn(h):
        return [768 + 512 * b + P * h for b in (2, 1, 0, 3)]
    odd_cols = [512, 0, 640, *hgrn(0)]
    for p in range(3):
        odd_cols += [P * (p + 1), *hgrn(p + 1)]
    gate, up, down = a["w_gate"], a["w_up"], a["w_down"]
    fcols = [t * P for t in range(FT)]
    ocols = [j * P for j in range(DC)]
    arrays = {
        "xT": np.ascontiguousarray(a["x"][0].T.reshape(DC, P, SEQ).transpose(1, 0, 2)),
        "small": small,
        "const": constants(),
        "w_even": tiles(w, starts),
        "w_fa": tiles(w, [1536], 8)[0],
        "w_out_e": tiles(a["w_out_even"][0], ocols),
        "w_odd": tiles(a["w_in_odd"][0], odd_cols),
        "w_out_o": tiles(a["w_out_odd"][0], ocols),
        "w_gu": np.stack([np.stack([tiles(gate[l], fcols), tiles(up[l], fcols)], 1) for l in range(2)]),
        "w_dn": np.stack([np.stack([tiles(down[l, h * FH * P:(h + 1) * FH * P], ocols) for h in range(2)])
                          for l in range(2)]),
    }
    nc = _bacc.Bacc("TRN2", target_bir_lowering=False, num_devices=1)
    args = [nc.dram_tensor(f"in_{n}", v.shape, _mybir.dt.from_np(v.dtype), kind="ExternalInput").ap()
            for n, v in arrays.items()]
    out = nc.dram_tensor("out", (P, DC, SEQ), F32, kind="ExternalOutput").ap()
    build(nc, layers, *args, out)
    r = _run(nc, [{f"in_{n}": v for n, v in arrays.items()}], core_ids=[0])
    y = r.results[0]["out"]
    return np.ascontiguousarray(y.transpose(2, 1, 0).reshape(1, SEQ, D))


LAYERS = 2
```

```python
from contextlib import ExitStack

import concourse.bass as bass
from concourse import mybir

F32 = mybir.dt.float32
F32R = mybir.dt.float32r
BF16 = mybir.dt.bfloat16
I32 = mybir.dt.int32
ALU = mybir.AluOpType
ACT = mybir.ActivationFunctionType
AX = mybir.AxisListType.X

P = 128
SEQ = 512
D = 1024
DC = D // P
TB = SEQ // P
HD = 64
FF = 2816
FT = FF // P
FH = FT // 2
EPS = 1e-6
LAMBDA_INIT = 0.8 - 0.6
QSCALE = HD ** -0.5
NEG = -1e30
FOX_G = 4
DIFF_G = 4
GROUPS = FOX_G + DIFF_G
OUT_EARLY = 5

LN_MIX, LN_FFN, LN_FIN = 0, 16, 32
DIFFN, HGRNN, BFG, LAMB, SINK, GAM = 40, 41, 42, 43, 47, 55
NSMALL = 63
C_ID, C_FOX, C_DIFF, C_SWA, C_LEV = 0, 128, 256, 384, 640
NLEV = 8
C_FIRST = C_LEV + NLEV * P
NCONST = C_FIRST + P


def constants():
    import numpy as np
    c = np.zeros((P, NCONST), np.float32)
    q = np.arange(P)[:, None]
    s = np.arange(P)[None, :]
    c[:, C_ID:C_ID + P] = q == s
    c[:, C_FOX:C_FOX + P] = np.where(s <= q, 0.0, NEG)
    c[:, C_DIFF:C_DIFF + P] = np.where(s // 64 <= q // 64, 0.0, NEG)
    k = np.arange(2 * P)[None, :] // 64
    c[:, C_SWA:C_SWA + 2 * P] = np.where((k >= q // 64 + 1) & (k <= q // 64 + 2), 0.0, NEG)
    sp, tf = q, s
    for lev in range(NLEV - 1):
        m = 64 >> lev
        on = (sp // (2 * m) == tf // (2 * m)) & (sp % (2 * m) < m) & (tf % (2 * m) >= m)
        c[:, C_LEV + lev * P:C_LEV + (lev + 1) * P] = on
    c[:, C_LEV + (NLEV - 1) * P:C_LEV + NLEV * P] = sp == tf
    c[:, C_FIRST:C_FIRST + P] = tf != 0
    return c


def build(nc, layers, xT, small, const, w_even, w_fa, w_out_e, w_odd, w_out_o, w_gu, w_dn, out):
    with ExitStack() as ctx:
        def sb(name, shape, dt=F32):
            return ctx.enter_context(nc.sbuf_tensor(name, shape, dt))

        def sem(name):
            return ctx.enter_context(nc.semaphore(name))

        def sems(name, n):
            return [sem(f"{name}{i}") for i in range(n)]

        x = sb("x", [P, DC, SEQ])
        xh = sb("xh", [P, DC, SEQ], F32R)
        xl = sb("xl", [P, DC, SEQ], F32R)
        split_acts = sb("split_acts", [P, 2 * FH, SEQ], F32R)
        gh, gl = split_acts[:, 0:FH], split_acts[:, FH:2 * FH]
        oh, ol = split_acts[:, 0:DC], split_acts[:, DC:2 * DC]
        ring_raw = sb("ring_raw", [P, (2 * FH + DC) * P])
        ring_hi = sb("ring_hi", [P, (2 * FH + DC) * P], F32R)
        ring_lo = sb("ring_lo", [P, (2 * FH + DC) * P], F32R)

        def ring(t, s, a, b):
            return t[:, s * FH * P + a:s * FH * P + b]
        fa_raw = sb("fa_raw", [P, DC * 8])
        fa_h = sb("fa_h", [P, DC * 8], F32R)
        fa_l = sb("fa_l", [P, DC * 8], F32R)
        work = sb("work", [P, 24, SEQ])
        rstd = sb("rstd", [P, SEQ])
        mean = sb("mean", [P, SEQ])
        newton = sb("newton", [P, SEQ])
        sq = sb("sq", [P, SEQ])
        sacc = sb("sacc", [P, SEQ])
        sm = sb("sm", [P, NSMALL])
        ident = sb("ident", [P, P])[:]
        level_mask = sb("level_mask", [P, NLEV * P], mybir.dt.uint8)
        not_first = sb("not_first", [P, SEQ])
        score_acc = sb("score_acc", [P, SEQ])
        cstb = sb("cstb", [P, C_LEV], BF16)
        identb = cstb[:, C_ID:C_ID + P]
        ones = sb("ones", [P, P])
        meanw = sb("meanw", [P, P])
        tiny = sb("tiny", [P, 128])

        bank = [ctx.enter_context(nc.psum_tensor(f"bank{i}", [P, SEQ], F32)) for i in range(8)]
        acc = bank[0:3]
        S = bank[3:5]
        PTP = bank[5:7]
        OP = bank[7]

        raw_in, hi_ready, lo_ready = sems("raw_in", 3), sems("hi_ready", 3), sems("lo_ready", 3)
        unit_done, acc_read = sems("unit_done", 3), sems("acc_read", 3)
        x_in, x_sq = sems("x_in", DC // 2), sems("x_sq", 2)
        small_in, const_in, fa_in = sem("small_in"), sem("const_in"), sem("fa_in")
        const_b = sem("const_b")
        xh_ready, xl_ready = sem("xh_ready"), sem("xl_ready")
        sq_ready, sacc_ready, sacc_zero = sem("sq_ready"), sem("sacc_ready"), sem("sacc_zero")
        stat_ready, mean_ready, ln_ready, y_ready = sem("stat_ready"), sem("mean_ready"), sem("ln_ready"), sem("y_ready")
        nt_ready, rstd_ready = sem("nt_ready"), sem("rstd_ready")
        ones_ready = sem("ones_ready")

        block = ctx.enter_context(nc.Block())

        UNIT8 = DC * P
        R_F = GROUPS
        PH = {}
        r = R_F
        for l in range(layers):
            if l % 2:
                PH["odd_in", l] = r
                r += 8
            PH["mix_out", l] = r
            r += 4
            for half in range(2):
                PH["gu", l, half] = r
                r += FH
                PH["dn", l, half] = r
                r += 4

        def act_table(act, func):
            act.activation(table_warm, ones[:, 0:1], func)

        def sp_load(sp, s, r, src, n):
            if not (isinstance(r, int) and r == 0):
                sp.wait_ge(lo_ready[s], r)
            sp.dma_start(ring(ring_raw, s, 0, n), src).then_inc(raw_in[s], 16)

        def act_hi(act, s, r, n=UNIT8):
            if not (isinstance(r, int) and r == 0):
                act.wait_ge(unit_done[s], r)
            act.wait_ge(raw_in[s], 16 * (r + 1))
            act.activation(ring(ring_hi, s, 0, n), ring(ring_raw, s, 0, n), ACT.Copy).then_inc(hi_ready[s], 1)

        def dve_lo(v, s, r, n=UNIT8):
            v.wait_ge(hi_ready[s], r + 1)
            v.tensor_tensor(ring(ring_lo, s, 0, n), ring(ring_raw, s, 0, n), ring(ring_hi, s, 0, n).bitcast(F32),
                            ALU.subtract).then_inc(lo_ready[s], 1)

        def pe_chunk(pe, s, c, n, rh, rl, b, last=False):
            w0, w1 = ring(ring_hi, s, c * P, (c + 1) * P), ring(ring_lo, s, c * P, (c + 1) * P)
            pe.matmul(b, w0, rh[:, c], start=(c == 0), stop=False)
            pe.matmul(b, w0, rl[:, c], start=False, stop=False)
            return pe.matmul(b, w1, rh[:, c], start=False, stop=(c == n - 1))

        def pe_unit_wait(pe, s, r):
            pe.wait_ge(lo_ready[s], r + 1)
            if not (isinstance(r, int) and r == 0):
                pe.wait_ge(acc_read[s], r)

        def pe_unit(pe, s, r, n, rh, rl):
            pe_unit_wait(pe, s, r)
            for c in range(n):
                mm = pe_chunk(pe, s, c, n, rh, rl, acc[s][:])
            mm.then_inc(unit_done[s], 1)

        def pe_chunks(pe, s, c0, c1, n, rh, rl):
            for c in range(c0, c1):
                mm = pe_chunk(pe, s, c, n, rh, rl, acc[s][:])
            if c1 == n:
                mm.then_inc(unit_done[s], 1)

        def pe_unit_first(pe, s, r, k):
            pe_unit_wait(pe, s, r)
            for c in range(DC):
                pe.wait_ge(xl_ready, DC * k + c + 1)
                if c == 5:
                    pe_stat(pe, k)
                pe_chunks(pe, s, c, c + 1, DC, xh, xl)

        def out_early(pe, l, c0, c1):
            if c0 == 0:
                pe_unit_wait(pe, 0, PH["mix_out", l])
            pe_chunks(pe, 0, c0, c1, DC, oh, ol)

        def pe_stat(pe, k):
            pe.wait_ge(sacc_ready, DC * (k + 1))
            pe.wait_ge(mean_ready, k)
            pe.matmul(OP[:], meanw[:], sacc[:], start=True, stop=True).then_inc(stat_ready, 1)

        def x_square(c):
            return work[:, (0, 1, 2, 3, 8, 9, 10, 20)[c]]

        def pe_stat_first(pe, c):
            pe.wait_ge(x_sq[c % 2], c // 2 + 1)
            mm = pe.matmul(OP[:], meanw[:], x_square(c), start=(c == 0), stop=(c == DC - 1))
            if c == DC - 1:
                mm.then_inc(stat_ready, 1)

        def dve_mean(v, k):
            v.wait_ge(stat_ready, k + 1)
            v.tensor_scalar(mean[:], OP[:], EPS, None, ALU.add).then_inc(mean_ready, 1)

        def act_rsqrt(act, k):
            act.wait_ge(mean_ready, k + 1)
            act.activation(newton[:], mean[:], ACT.Ln).then_inc(ln_ready, 1)
            act.wait_ge(ln_ready, k + 1)
            act.activation(rstd[:], newton[:], ACT.Exp, scale=-0.5).then_inc(y_ready, 1)

        def dve_newton(v, k):
            v.wait_ge(y_ready, k + 1)
            v.scalar_tensor_tensor(newton[:], mean[:], -0.5, rstd[:], ALU.mult, ALU.mult).then_inc(nt_ready, 1)
            v.wait_ge(nt_ready, 2 * k + 1)
            v.tensor_tensor(newton[:], newton[:], rstd[:], ALU.mult).then_inc(nt_ready, 1)
            v.wait_ge(nt_ready, 2 * k + 2)
            v.scalar_tensor_tensor(rstd[:], newton[:], 1.5, rstd[:], ALU.add, ALU.mult).then_inc(rstd_ready, 1)

        def act_xh(act, j, gcol, n, gate):
            act.wait_ge(*gate)
            act.activation(xh[:, j], x[:, j], ACT.Copy, scale=sm[:, gcol:gcol + 1] if isinstance(j, int)
                           else sm[:, bass.ds(gcol, 1)]).then_inc(xh_ready, 1)

        def dve_xl(v, j, gcol, n):
            v.wait_ge(xh_ready, n + 1)
            v.scalar_tensor_tensor(xl[:, j], x[:, j], sm[:, gcol:gcol + 1] if isinstance(j, int) else sm[:, bass.ds(gcol, 1)],
                                   xh[:, j].bitcast(F32), ALU.mult, ALU.subtract).then_inc(xl_ready, 1)

        def pool_sq(g, j, n, k, gate):
            g.wait_ge(*gate)
            g.wait_ge(sacc_ready, n)
            g.tensor_tensor(sq[:], x[:, j], x[:, j], ALU.mult).then_inc(sq_ready, 1)
            g.wait_ge(sq_ready, n + 1)
            g.tensor_tensor(sacc[:], sacc[:], sq[:], ALU.add).then_inc(sacc_ready, 1)

        def pool_zero(g, k):
            g.wait_ge(stat_ready, k)
            g.memset(sacc[:], 0.0).then_inc(sacc_zero, 1)
            g.wait_ge(sacc_zero, k)

        q_cur, k_cur, vT, Vn = work[:, 0], work[:, 1], work[:, 2], work[:, 3]
        PB = [work[:, 4 + i] for i in range(4)]
        PTS = [work[:, 8 + i] for i in range(2)]
        on = work[:, 10]
        CQ = work[:, 11:15].bitcast(BF16).rearrange("p a b -> p (a b)").rearrange("p (h t) -> p h t", h=8)
        CK = work[:, 15:19].bitcast(BF16).rearrange("p a b -> p (a b)").rearrange("p (h t) -> p h t", h=8)
        cq_cur = work[:, 19].bitcast(BF16).rearrange("p (h t) -> p h t", h=2)
        const_stage = work[:, 4:8].rearrange("p a b -> p (a b)")
        z = work[0:8, 20]
        za = work[0:8, 21]
        cum = work[0:8, 22]
        cpart = work[0:8, 23].bitcast(BF16).rearrange("p (a t) -> p a t", a=2)
        cpart2 = work[0:8, 10].bitcast(BF16).rearrange("p (a t) -> p a t", a=2)
        cpartn = [work[0:8, 8 + i].bitcast(BF16).rearrange("p (a t) -> p a t", a=2) for i in range(2)]
        nmax = tiny[:, 0:8]
        rsum = tiny[:, 8:16]
        rinv = tiny[:, 16:24]
        lamt = tiny[:, 24:32]
        dss = tiny[:, 32:36]
        dn = tiny[:, 36:48]
        dscale = tiny[:, 48:49]
        table_warm = tiny[:, 121:122]

        fa_hi, fa_lo, fa_done, fa_read = sem("fa_hi"), sem("fa_lo"), sem("fa_done"), sem("fa_read")
        gate_step, gate_act = sem("gate_step"), sem("gate_act")
        cq_in, cq_ones, cq_staged = sem("cq_in"), sem("cq_ones"), sem("cq_staged")
        lam_prod, lam_sum, lam_exp, lam_ready = sem("lam_prod"), sem("lam_sum"), sem("lam_exp"), sem("lam_ready")
        v_turned, v_nat = sem("v_turned"), sem("v_nat")
        f_scores, f_max, f_exp, f_turned, f_pv = (sem(n) for n in (
            "f_scores", "f_max", "f_exp", "f_turned", "f_pv"))
        f_pts = sems("f_pts", 2)
        d_scores, d_max, d_exp, d_mix, d_turned, d_pts, d_pv = (sem(n) for n in (
            "d_scores", "d_max", "d_exp", "d_mix", "d_turned", "d_pts", "d_pv"))
        rinv_ready, d_step = sem("rinv_ready"), sem("d_step")
        d_sq, d_ln, d_act = sem("d_sq"), sem("d_ln"), sem("d_act")
        on_ready, o_turned, oh_ready, ol_ready = sem("on_ready"), sem("o_turned"), sem("oh_ready"), sem("ol_ready")

        def pe_v_turn(pe, g):
            pe.wait_ge(acc_read[2], g + 1)
            for i in range(TB):
                mm = pe.transpose(acc[2][:, i * P:(i + 1) * P], vT[:, i * P:(i + 1) * P], ident)
            mm.then_inc(v_turned, 1)

        def act_v_nat(act, g, pv, n):
            act.wait_ge(v_turned, g + 1)
            if n is not None:
                act.wait_ge(pv, n)
            act.activation(Vn, acc[2][:], ACT.Copy).then_inc(v_nat, 1)

        def out_turn_pe(pe, n, src):
            pe.wait_ge(on_ready, n + 2)
            for i in range(TB):
                mm = pe.transpose(S[0][:, i * P:(i + 1) * P], src[:, i * P:(i + 1) * P], ident)
            mm.then_inc(o_turned, 1)

        CR = 2

        def fox_scores(pe, g, n):
            k, m, i = 8 * g + n, n % 2, n // 2
            pe.wait_ge(f_exp, k + 1)
            if n == 0:
                pe.wait_ge(acc_read[1], g + 1)
                pe.wait_ge(acc_read[0], g + 1)
                pe.wait_ge(cq_staged, g + 1)
                pe.wait_ge(ol_ready, g + 1)
            b, w = S[n % 2], P * (i + 1)
            rows = slice(HD * m, HD * m + HD)
            pe.matmul(b[:, 0:w], q_cur[rows, i * P:(i + 1) * P], k_cur[rows, 0:w], start=True, stop=False)
            pe.matmul(b[:, 0:w], cq_cur[0:6, m, i * P:(i + 1) * P],
                      CK[0:6, bass.ds(2 * g + m, 1), 0:w].rearrange("p a t -> p (a t)"), start=False, stop=False)
            pe.matmul(b[:, w - P:w], identb, cstb[:, C_FOX:C_FOX + P], start=False, stop=True).then_inc(f_scores, 1)

        def fox_max(v, g, n):
            v.wait_ge(f_scores, 8 * g + n + 1)
            v.tensor_reduce(nmax[:, n:n + 1], S[n % 2][:, 0:P * (n // 2 + 1)], AX, ALU.max, negate=True).then_inc(f_max, 1)

        def fox_exp(act, g, n):
            k, w = 8 * g + n, P * (n // 2 + 1)
            act.wait_ge(f_max, k + 1)
            act.wait_ge(f_turned, k + 1)
            if n == 0:
                act.wait_ge(rinv_ready, g + 1)
            act.activation(PB[n % 2][:, 0:w], S[n % 2][:, 0:w], ACT.Exp, bias=nmax[:, n:n + 1],
                           accum_out=rsum[:, n:n + 1]).then_inc(f_exp, 1)

        def fox_turn(pe, g, n):
            k = 8 * g + n
            pe.wait_ge(f_exp, k + 1 + CR)
            pe.wait_ge(f_pts[n % 2], 4 * g + n // 2 + 1)
            for j in range(n // 2 + 1):
                mm = pe.transpose(PTP[n % 2][:, j * P:(j + 1) * P], PB[n % 2][:, j * P:(j + 1) * P], ident)
            mm.then_inc(f_turned, 1)

        def fox_pts_wait(e, g, n):
            k = 8 * g + n
            e.wait_ge(f_turned, k + 1 + CR)
            e.wait_ge(f_pv, k + 1)

        def fox_pts_dve(v, g, n):
            fox_pts_wait(v, g, n)
            w = P * (n // 2 + 1)
            v.tensor_copy(PTS[n % 2][:, 0:w], PTP[n % 2][:, 0:w]).then_inc(f_pts[n % 2], 1)

        def fox_pts_act(act, g, n):
            fox_pts_wait(act, g, n)
            w = P * (n // 2 + 1)
            act.activation(PTS[n % 2][:, 0:w], PTP[n % 2][:, 0:w], ACT.Copy).then_inc(f_pts[n % 2], 1)

        def fox_pv(pe, g, n):
            k, m, i = 8 * g + n, n % 2, n // 2
            pe.wait_ge(f_pts[n % 2], 4 * g + n // 2 + 2)
            if n == 0:
                pe.wait_ge(v_nat, g + 1)
                pe.wait_ge(on_ready, g + 1)
            for j in range(i + 1):
                mm = pe.matmul(OP[:, i * P + m * HD:i * P + m * HD + HD], PTS[n % 2][:, j * P:(j + 1) * P],
                               Vn[:, j * P + m * HD:j * P + m * HD + HD], start=(j == 0), stop=(j == i))
            mm.then_inc(f_pv, 1)

        def proj_wait(pe, s, G):
            pe.wait_ge(lo_ready[s], G + 1)
            pe.wait_ge(acc_read[s], G)
            if s == 2:
                pe.wait_ge(v_nat, G)

        def proj_chunks(pe, s, G, c0, c1):
            if c0 == 0:
                proj_wait(pe, s, G)
            for c in range(c0, c1):
                mm = pe_chunk(pe, s, c, DC, xh, xl, acc[s][:])
            if c1 == DC:
                mm.then_inc(unit_done[s], 1)

        def dve_q(v, G):
            v.wait_ge(unit_done[0], G + 1)
            v.scalar_tensor_tensor(q_cur, acc[0][:], QSCALE, rstd[:], ALU.mult, ALU.mult).then_inc(acc_read[0], 1)

        def dve_k(v, G):
            v.wait_ge(unit_done[1], G + 1)
            v.tensor_tensor(k_cur, acc[1][:], rstd[:], ALU.mult).then_inc(acc_read[1], 1)

        def dve_v(v, G):
            v.wait_ge(unit_done[2], G + 1)
            v.tensor_tensor(vT, acc[2][:], rstd[:], ALU.mult).then_inc(acc_read[2], 1)

        def fox_group_pe(pe, g):
            proj_chunks(pe, 0, g + 1, 0, 1)
            for n in range(8):
                fox_scores(pe, g, n)
                if n == 1:
                    pe_v_turn(pe, g)
                if n < 7:
                    proj_chunks(pe, 0, g + 1, n + 1, n + 2)
                else:
                    proj_chunks(pe, 1, g + 1, 0, 1)
                if n >= 1:
                    fox_turn(pe, g, n - 1)
                if n >= 2:
                    fox_pv(pe, g, n - 2)
            proj_chunks(pe, 1, g + 1, 1, 3)
            fox_turn(pe, g, 7)
            fox_pv(pe, g, 6)
            proj_chunks(pe, 1, g + 1, 3, 5)
            fox_pv(pe, g, 7)
            proj_chunks(pe, 1, g + 1, 5, 8)
            proj_chunks(pe, 2, g + 1, 0, 1)
            out_turn_pe(pe, g, on)
            proj_chunks(pe, 2, g + 1, 1, 8)

        def fox_group_act(act, g):
            for n in range(8):
                fox_exp(act, g, n)
                if n == 0:
                    act_hi(act, 1, g + 1)
                if n == 1:
                    act_v_nat(act, g, f_pv, 8 * g + CR)
                if n >= 2 and n % 2 == 0:
                    fox_pts_act(act, g, n - 1)
            fox_pts_act(act, g, 7)
            act_hi(act, 2, g + 1)
            act_hi(act, 0, g + 2)
            act_oh(act, g)

        def act_oh(act, g):
            act.wait_ge(o_turned, g + 1)
            act.activation(oh[:, g], S[0][:], ACT.Copy).then_inc(oh_ready, 1)

        def fox_group_dve(v, g):
            fox_max(v, g, 0)
            dve_lo(v, 1, g + 1)
            for n in range(1, 8):
                fox_max(v, g, n)
                if n % 2 == 1:
                    fox_pts_dve(v, g, n - 1)
            v.wait_ge(f_exp, 8 * g + 8 + CR)
            v.reciprocal(rinv, rsum).then_inc(rinv_ready, 1)
            dve_q(v, g + 1)
            dve_lo(v, 2, g + 1)
            v.wait_ge(f_pv, 8 * g + 8 + CR)
            v.wait_ge(rinv_ready, g + 2)
            v.tensor_tensor(on.rearrange("p (n d) -> p n d", d=HD), OP[:].rearrange("p (n d) -> p n d", d=HD),
                            rinv.unsqueeze(2).to_broadcast([P, 8, HD]), ALU.mult).then_inc(on_ready, 1)
            dve_k(v, g + 1)
            dve_lo(v, 0, g + 2)
            v.wait_ge(oh_ready, g + 1)
            v.tensor_tensor(ol[:, g], S[0][:], oh[:, g].bitcast(F32), ALU.subtract).then_inc(ol_ready, 1)
            dve_v(v, g + 1)

        def diff_scores(pe, g, i, last):
            for m in range(2):
                k = 8 * g + 2 * i + m
                pe.wait_ge(d_exp, k + 1)
                if i == 0 and m == 0:
                    pe.wait_ge(acc_read[0], FOX_G + g + 1)
                    pe.wait_ge(acc_read[1], FOX_G + g + 1)
                    pe.wait_ge(ol_ready, FOX_G + g + 1)
                w = P * (i + 1)
                rows = slice(HD * m, HD * m + HD)
                pe.matmul(S[m][:, 0:w], q_cur[rows, i * P:(i + 1) * P], k_cur[rows, 0:w], start=True, stop=False)
                pe.matmul(S[m][:, w - P:w], identb, cstb[:, C_DIFF:C_DIFF + P], start=False,
                          stop=True).then_inc(d_scores, 1)

        def diff_max(v, g, i):
            for m in range(2):
                n = 2 * i + m
                v.wait_ge(d_scores, 8 * g + n + 1)
                v.tensor_reduce(nmax[:, n:n + 1], S[m][:, 0:P * (i + 1)], AX, ALU.max, negate=True).then_inc(d_max, 1)

        def diff_exp(act, g, i):
            for m in range(2):
                n = 2 * i + m
                act.wait_ge(d_max, 8 * g + n + 1)
                act.wait_ge(d_mix, 2 * (4 * g + i) + 1 + m)
                w = P * (i + 1)
                act.activation(PB[m][:, 0:w], S[m][:, 0:w], ACT.Exp, bias=nmax[:, n:n + 1],
                               accum_out=rsum[:, n:n + 1]).then_inc(d_exp, 1)

        def diff_mix(v, g, i):
            t, w, pm = 4 * g + i, P * (i + 1), PB[2 + i % 2]
            v.wait_ge(d_exp, 2 * t + 2 + CR)
            v.reciprocal(rinv[:, 0:2], rsum[:, 2 * i:2 * i + 2]).then_inc(d_step, 1)
            v.wait_ge(d_step, 2 * t + 1)
            v.tensor_scalar(rinv[:, 2:3], rinv[:, 1:2], lamt[:, 7:8], None, ALU.mult).then_inc(d_step, 1)
            v.wait_ge(d_turned, t + 1)
            v.tensor_scalar(pm[:, 0:w], PB[0][:, 0:w], rinv[:, 0:1], None, ALU.mult).then_inc(d_mix, 1)
            v.wait_ge(d_step, 2 * t + 2)
            v.wait_ge(d_mix, 2 * t + 1 + CR)
            v.scalar_tensor_tensor(pm[:, 0:w], PB[1][:, 0:w], rinv[:, 2:3], pm[:, 0:w], ALU.mult,
                                   ALU.add).then_inc(d_mix, 1)

        def diff_turn(pe, g, i):
            t = 4 * g + i
            pe.wait_ge(d_mix, 2 * t + 2 + CR)
            pe.wait_ge(d_pts, t + 1)
            for j in range(i + 1):
                mm = pe.transpose(PTP[i % 2][:, j * P:(j + 1) * P], PB[2 + i % 2][:, j * P:(j + 1) * P], ident)
            mm.then_inc(d_turned, 1)

        def diff_pts(act, g, i):
            t, w = 4 * g + i, P * (i + 1)
            act.wait_ge(d_turned, t + 1 + CR)
            act.wait_ge(d_pv, t + 1)
            act.activation(PTS[i % 2][:, 0:w], PTP[i % 2][:, 0:w], ACT.Copy).then_inc(d_pts, 1)

        def diff_pv(pe, g, i):
            t = 4 * g + i
            pe.wait_ge(d_pts, t + 1 + CR)
            if i == 0:
                pe.wait_ge(v_nat, FOX_G + g + 1)
                pe.wait_ge(on_ready, FOX_G + g + 1)
            for j in range(i + 1):
                mm = pe.matmul(OP[:, i * P:(i + 1) * P], PTS[i % 2][:, j * P:(j + 1) * P],
                               Vn[:, j * P:(j + 1) * P], start=(j == 0), stop=(j == i))
            mm.then_inc(d_pv, 1)

        def diff_group_pe(pe, g, last=False):
            G = FOX_G + g

            def chunks(s, c0, c1, early=None):
                if not last:
                    proj_chunks(pe, s, G + 1, c0, c1)
                elif early:
                    out_early(pe, 0, *early)
            chunks(0, 0, 1)
            for i in range(4):
                diff_scores(pe, g, i, last)
                if i == 1:
                    pe_v_turn(pe, G)
                chunks(0, *((1, 3), (3, 5), (5, 7), (7, 8))[i], early=((0, 1), (1, 2), (2, 3), (3, 4))[i])
                if i >= 1:
                    diff_turn(pe, g, i - 1)
                if i >= 2:
                    diff_pv(pe, g, i - 2)
            chunks(1, 0, 4, early=(4, OUT_EARLY))
            diff_turn(pe, g, 3)
            diff_pv(pe, g, 2)
            chunks(1, 4, 6)
            diff_pv(pe, g, 3)
            chunks(1, 6, 8)
            if not last:
                chunks(2, 0, 6)
                out_turn_pe(pe, G, on)
                chunks(2, 6, 8)

        def row_rms_act(act, g, scratch):
            for i in range(4):
                act.activation(scratch[:, i * P:(i + 1) * P], OP[:, i * P:(i + 1) * P], ACT.Square,
                               accum_out=dss[:, i:i + 1]).then_inc(d_sq, 1)
            act.wait_ge(d_ln, 2 * g + 1)
            act.activation(dn[:, 4:8], dn[:, 0:4], ACT.Ln).then_inc(d_act, 1)
            act.wait_ge(d_act, 2 * g + 1)
            act.activation(dn[:, 4:8], dn[:, 4:8], ACT.Exp, scale=-0.5).then_inc(d_act, 1)

        def row_mean_dve(v, g):
            v.wait_ge(d_sq, 4 * g + 4)
            v.tensor_scalar(dn[:, 0:4], dss, 1.0 / P, EPS, ALU.mult, ALU.add).then_inc(d_ln, 1)

        def row_rms_dve(v, g, on):
            v.wait_ge(d_act, 2 * g + 2)
            v.wait_ge(d_ln, 2 * g + 1)
            v.tensor_tensor(dn[:, 8:12], dn[:, 0:4], dn[:, 4:8], ALU.mult).then_inc(d_ln, 1)
            v.wait_ge(d_ln, 2 * g + 2)
            v.tensor_tensor(dn[:, 8:12], dn[:, 8:12], dn[:, 4:8], ALU.mult).then_inc(d_newton, 1)
            v.wait_ge(d_newton, 3 * g + 1)
            v.tensor_scalar(dn[:, 8:12], dn[:, 8:12], -0.5, 1.5, ALU.mult, ALU.add).then_inc(d_newton, 1)
            v.wait_ge(d_newton, 3 * g + 2)
            v.tensor_tensor(dn[:, 8:12], dn[:, 8:12], dn[:, 4:8], ALU.mult).then_inc(d_newton, 1)
            v.wait_ge(d_newton, 3 * g + 3)
            v.tensor_tensor(on.rearrange("p (n d) -> p n d", d=P), OP[:].rearrange("p (n d) -> p n d", d=P),
                            dn[:, 8:12].unsqueeze(2).to_broadcast([P, 4, P]), ALU.mult).then_inc(on_ready, 1)

        def diff_group_act(act, g, last=False):
            G = FOX_G + g
            for i in range(4):
                diff_exp(act, g, i)
                if i == 1:
                    act_v_nat(act, G, d_pv, 4 * g + CR)
                    act_hi(act, 1, G + 1)
                if i >= 1:
                    diff_pts(act, g, i - 1)
            diff_pts(act, g, 3)
            if not last:
                act_hi(act, 2, G + 1)
                act_hi(act, 0, G + 2)
            act_table(act, ACT.Ln)
            act.wait_ge(d_pv, 4 * g + 4 + CR)
            row_rms_act(act, g, PB[0])
            act.wait_ge(o_turned, G + 1)
            act.activation(oh[:, G], S[0][:], ACT.Copy, scale=dscale).then_inc(oh_ready, 1)

        def diff_group_dve(v, g, last=False):
            G = FOX_G + g
            for i in range(4):
                diff_max(v, g, i)
                diff_mix(v, g, i)
                if i == 1:
                    dve_lo(v, 1, G + 1)
            if not last:
                dve_q(v, G + 1)
                dve_lo(v, 2, G + 1)
                dve_lo(v, 0, G + 2)
            row_mean_dve(v, g)
            if not last:
                dve_k(v, G + 1)
            row_rms_dve(v, g, on)
            v.wait_ge(oh_ready, G + 1)
            v.scalar_tensor_tensor(ol[:, G], S[0][:], dscale, oh[:, G].bitcast(F32), ALU.mult,
                                   ALU.subtract).then_inc(ol_ready, 1)
            if not last:
                dve_v(v, G + 1)

        d_newton = sem("d_newton")

        R0 = PH.get(("odd_in", 1), 0)
        KV = [work[:, 1], work[:, 2]]
        o_state, o_vT, o_Vn = work[:, 3], work[:, 3], work[:, 4]
        oP, oPT, o_on, o_kN = [work[:, 5], work[:, 6]], [work[:, 7], work[:, 8]], work[:, 9], work[:, 9]
        qr, fr, ir, gr = (work[:, 10 + i] for i in range(4))
        hq, sgate, hb, hk = (work[:, 14 + i] for i in range(4))
        dif, zz = [work[:, 18], work[:, 19]], [work[:, 20], work[:, 21]]
        qe, hVn = work[:, 22], work[:, 23]
        sigq = mean[:]
        LB = [S[1], PTP[1]]
        nsink, sinkx, sinke = tiny[:, 49:57], tiny[:, 57:65], tiny[:, 65:73]
        gmx, gd, ge = tiny[:, 73:77], tiny[:, 77:85], tiny[:, 85:93]
        gsum, grec, gsm, glb, goml, ebl = (tiny[:, 93:97], tiny[:, 97:101], tiny[:, 101:109], tiny[:, 109:113],
                                           tiny[:, 113:117], tiny[:, 117:121])
        s_scores, s_raw_max, s_max, s_exp, s_turned, s_pts, s_pv = (sem(n) for n in (
            "s_scores", "s_raw_max", "s_max", "s_exp", "s_turned", "s_pts", "s_pv"))
        s_sinkx, s_sinke, s_sum, s_rinv = sem("s_sinkx"), sem("s_sinke"), sem("s_sum"), sem("s_rinv")
        k_made, nsink_ready, sv_turned, sv_nat = sem("k_made"), sem("nsink_ready"), sem("sv_turned"), sem("sv_nat")
        lb_step, lb_exp = sem("lb_step"), sem("lb_exp")
        h_sigf, h_sigq, h_sigg, h_gate, h_f, h_k, h_q, h_lnf, h_b = (sem(n) for n in (
            "h_sigf", "h_sigq", "h_sigg", "h_gate", "h_f", "h_k", "h_q", "h_lnf", "h_b"))
        h_eb, h_qe, h_ebl, h_kexp, h_dif, h_e, h_z, h_zread = (sem(n) for n in (
            "h_eb", "h_qe", "h_ebl", "h_kexp", "h_dif", "h_e", "h_z", "h_zread"))
        h_takes = sem("h_takes")
        h_zhalf, h_sc, h_cp, h_vturned, h_vnat, h_kn, h_u, h_state, h_o, h_gated = (sem(n) for n in (
            "h_zhalf", "h_sc", "h_cp", "h_vturned", "h_vnat", "h_kn", "h_u", "h_state", "h_o", "h_gated"))

        def odd_chunks(pe, s, r, c0, c1):
            if c0 == 0:
                pe_unit_wait(pe, s, r)
            for c in range(c0, c1):
                mm = pe_chunk(pe, s, c, DC, xh, xl, acc[s][:])
            if c1 == DC:
                mm.then_inc(unit_done[s], 1)

        def span(n):
            return (0, P) if n // 2 == 0 else (P * (n // 2 - 1), 2 * P)

        def swa_scores(pe, p, n, kv):
            k, m, i = 8 * p + n, n % 2, n // 2
            pe.wait_ge(s_exp, k + 1)
            if n == 0:
                pe.wait_ge(acc_read[0], R0 + 2 * p + 1)
                pe.wait_ge(h_gated, p + 1)
            rows, (k0, w) = slice(HD * m, HD * m + HD), span(n)
            b = S[n % 2]
            pe.matmul(b[:, 0:w], work[rows, 0, i * P:(i + 1) * P], KV[kv][rows, k0:k0 + w],
                      start=True, stop=False)
            pe.matmul(b[:, 0:w], identb, cstb[:, C_SWA + 2 * P - w:C_SWA + 2 * P], start=False,
                      stop=True).then_inc(s_scores, 1)

        def swa_max(v, p, n):
            v.wait_ge(s_scores, 8 * p + n + 1)
            v.tensor_reduce(nmax[:, n:n + 1], S[n % 2][:, 0:span(n)[1]], AX, ALU.max, negate=True).then_inc(s_raw_max, 1)
            v.wait_ge(s_raw_max, 8 * p + n + 1)
            v.tensor_tensor(nmax[:, n:n + 1], nmax[:, n:n + 1], nsink[:, bass.ds(2 * p + n % 2, 1)],
                            ALU.min).then_inc(s_max, 1)

        def swa_exp(act, p, n):
            k, w = 8 * p + n, span(n)[1]
            act.wait_ge(s_max, k + 1)
            act.wait_ge(s_turned, k + 1)
            if n == 0:
                act.wait_ge(s_rinv, p + 1)
            act.activation(oP[n % 2][:, 0:w], S[n % 2][:, 0:w], ACT.Exp, bias=nmax[:, n:n + 1],
                           accum_out=rsum[:, n:n + 1]).then_inc(s_exp, 1)

        def swa_turn(pe, p, n):
            k = 8 * p + n
            pe.wait_ge(s_exp, k + 1 + CR)
            pe.wait_ge(s_pts, k + 1)
            if n == 0:
                pe.wait_ge(h_state, 3 * p + 1)
            if n == 1:
                pe.wait_ge(h_cp, 8 * p + CR)
            for j in range(span(n)[1] // P):
                mm = pe.transpose(PTP[n % 2][:, j * P:(j + 1) * P], oP[n % 2][:, j * P:(j + 1) * P], ident)
            mm.then_inc(s_turned, 1)

        def swa_pts(act, p, n):
            k, w = 8 * p + n, span(n)[1]
            act.wait_ge(s_turned, k + 1 + CR)
            act.wait_ge(s_pv, k + 1)
            act.activation(oPT[n % 2][:, 0:w], PTP[n % 2][:, 0:w], ACT.Copy).then_inc(s_pts, 1)

        def swa_pv(pe, p, n, kv):
            k, m, i = 8 * p + n, n % 2, n // 2
            k0, w = span(n)
            pe.wait_ge(s_pts, k + 1 + CR)
            if n == 0:
                pe.wait_ge(on_ready, 2 * p + GROUPS + 1)
            for j in range(w // P):
                mm = pe.matmul(OP[:, i * P + m * HD:i * P + m * HD + HD], oPT[n % 2][:, j * P:(j + 1) * P],
                               o_Vn[:, k0 + j * P + HD * kv:k0 + j * P + HD * kv + HD],
                               start=(j == 0), stop=(j == w // P - 1))
            mm.then_inc(s_pv, 1)

        def piece(a, L):
            return a.rearrange("p (n h m) -> p n h m", h=2, m=64 >> L)

        def head_sigmoids_act(act, h):
            act.wait_ge(acc_read[1], R0 + 2 * h + 1)
            act.activation(fr, fr, ACT.Sigmoid).then_inc(h_sigf, 1)
            act.wait_ge(acc_read[2], GROUPS + 2 + h + 1)
            act.activation(sigq, qr, ACT.Sigmoid).then_inc(h_sigq, 1)
            act.wait_ge(acc_read[0], R0 + 2 * h + 2)
            act.activation(gr, gr, ACT.Sigmoid).then_inc(h_sigg, 1)

        def head_f_dve(v, h):
            v.wait_ge(h_sigf, h + 1)
            v.tensor_scalar(fr, fr, goml[:, bass.ds(h, 1)], glb[:, bass.ds(h, 1)], ALU.mult, ALU.add).then_inc(h_f, 1)

        def head_ln_act(act, h):
            act.wait_ge(h_f, h + 1)
            act.activation(newton[:], fr, ACT.Ln).then_inc(h_lnf, 1)

        def head_q_dve(v, h):
            v.wait_ge(h_sigq, h + 1)
            v.tensor_tensor(hq, qr, sigq, ALU.mult).then_inc(h_q, 1)

        def head_gate_dve(v, h):
            v.wait_ge(h_sigg, h + 1)
            v.wait_ge(h_gated, h + 1)
            v.tensor_copy(sgate, gr).then_inc(h_gate, 1)

        def head_k_dve(v, p):
            v.wait_ge(h_f, p + 1)
            v.tensor_scalar(hk, fr, -1.0, 1.0, ALU.mult, ALU.add).then_inc(h_k, 1)

        def head_scan_dve(v, p):
            v.wait_ge(h_lnf, p + 1)
            v.tensor_tensor_scan(hb, not_first[:], newton[:], 0.0, ALU.mult, ALU.add).then_inc(h_b, 1)

        def head_decays_act(act, p):
            act.wait_ge(h_b, p + 1)
            act.wait_ge(h_o, p + 1)
            act.activation(qe, hb, ACT.Exp).then_inc(h_eb, 1)
            act.activation(ebl, hb[:, P - 1::P], ACT.Exp).then_inc(h_ebl, 1)
            act.wait_ge(h_z, 8 * p + 1)
            for i in range(TB):
                act.activation(dif[1][:, i * P:(i + 1) * P], hb[:, i * P:(i + 1) * P], ACT.Exp, scale=-1.0,
                               bias=hb[:, (i + 1) * P - 1:(i + 1) * P]).then_inc(h_kexp, 1)

        def head_kdec_pool(g, p):
            g.wait_ge(h_kexp, TB * p + TB)
            g.wait_ge(h_zread, 8 * p + 1)
            g.tensor_tensor(zz[1], hk, dif[1], ALU.mult).then_inc(h_z, 1)

        def level_dif_dve(v, p, L):
            b, o = piece(hb, L), piece(dif[L % 2], L)
            n, m = SEQ // (128 >> L), 64 >> L
            ref = b[:, :, 0, m - 1:m].to_broadcast([P, n, m])
            v.wait_ge(h_z, 8 * p + L + 2)
            v.wait_ge(h_b, p + 1)
            v.tensor_tensor(o[:, :, 0], ref, b[:, :, 0], ALU.subtract).then_inc(h_dif, 1)
            v.tensor_tensor(o[:, :, 1], b[:, :, 1], ref, ALU.subtract).then_inc(h_dif, 1)

        def level_exp_act(act, p, L):
            act.wait_ge(h_dif, 14 * p + 2 * L + 2)
            act.activation(dif[L % 2], dif[L % 2], ACT.Exp).then_inc(h_e, 1)

        def level_z_pool(g, p, L):
            e, o = piece(dif[L % 2], L), piece(zz[L % 2], L)
            g.wait_ge(h_e, 7 * p + L + 1)
            g.wait_ge(h_q, p + 1)
            g.wait_ge(h_zread, 8 * p + L + 2)
            g.tensor_tensor(o[:, :, 0], piece(hk, L)[:, :, 0], e[:, :, 0], ALU.mult).then_inc(h_zhalf, 1)
            g.wait_ge(h_zhalf, 7 * p + L + 1)
            g.tensor_tensor(o[:, :, 1], piece(hq, L)[:, :, 1], e[:, :, 1], ALU.mult).then_inc(h_z, 1)

        def level_scores_pe(pe, p, L):
            pe.wait_ge(h_cp, 8 * p + L + 1)
            if L < NLEV - 1:
                pe.wait_ge(h_z, 8 * p + L + 2 + CR)
                a = c = zz[L % 2]
            else:
                pe.wait_ge(h_k, p + 1)
                pe.wait_ge(h_q, p + 1)
                a, c = hk, hq
            for i in range(TB):
                mm = pe.matmul(LB[L % 2][:, i * P:(i + 1) * P], a[:, i * P:(i + 1) * P], c[:, i * P:(i + 1) * P],
                               start=True, stop=True)
            mm.then_inc(h_sc if L == NLEV - 1 else h_zread, 1)

        def level_take_dve(v, p, L):
            if L < NLEV - 1:
                v.wait_ge(h_zread, 8 * p + L + 2 + CR)
            else:
                v.wait_ge(h_sc, p + 1)
            if L == 0:
                v.wait_ge(h_o, p + 1)
            else:
                v.wait_ge(h_cp, 8 * p + L + CR)
            v.sem_inc(h_takes, 1)
            v.copy_predicated(score_acc[:].rearrange("p (n t) -> p n t", t=P),
                              level_mask[:, L * P:(L + 1) * P].unsqueeze(1).to_broadcast([P, TB, P]),
                              LB[L % 2][:].rearrange("p (n t) -> p n t", t=P)).then_inc(h_cp, 1)

        def head_turns_pe(pe, p):
            pe.wait_ge(acc_read[1], R0 + 2 * p + 2)
            pe.wait_ge(s_pts, 8 * p + 8 + CR)
            for i in range(TB):
                mm = pe.transpose(PTP[0][:, i * P:(i + 1) * P], ir[:, i * P:(i + 1) * P], ident)
            mm.then_inc(h_vturned, 1)
            pe.wait_ge(h_z, 8 * p + 1 + CR)
            for i in range(TB):
                mm = pe.transpose(PTP[1][:, i * P:(i + 1) * P], zz[1][:, i * P:(i + 1) * P], ident)
            mm.then_inc(h_zread, 1)

        def head_state_pe(pe, p):
            pe.wait_ge(h_vnat, p + 1)
            pe.wait_ge(h_kn, p + 1)
            for i in range(TB - 1):
                mm = pe.matmul(PTP[0][:, i * P:(i + 1) * P], o_kN[:, i * P:(i + 1) * P], hVn[:, i * P:(i + 1) * P],
                               start=True, stop=True)
            mm.then_inc(h_u, 1)

        def head_state_dve(v, p):
            v.wait_ge(h_u, p + 1)
            v.wait_ge(h_ebl, p + 1)
            v.wait_ge(h_o, p + 1)
            v.tensor_copy(o_state[:, 0:P], PTP[0][:, 0:P]).then_inc(h_state, 1)
            for i in range(1, TB - 1):
                v.wait_ge(h_state, 3 * p + i + 1)
                v.scalar_tensor_tensor(o_state[:, i * P:(i + 1) * P], o_state[:, (i - 1) * P:i * P], ebl[:, i:i + 1],
                                       PTP[0][:, i * P:(i + 1) * P], ALU.mult, ALU.add).then_inc(h_state, 1)

        def head_out_pe(pe, p):
            pe.wait_ge(h_cp, 8 * p + 8 + CR)
            pe.wait_ge(h_state, 3 * p + 4)
            pe.wait_ge(h_qe, p + 1)
            pe.wait_ge(on_ready, 2 * p + GROUPS + 2)
            for i in range(TB):
                t = slice(i * P, (i + 1) * P)
                if i:
                    pe.matmul(OP[:, t], qe[:, t], o_state[:, (i - 1) * P:i * P], start=True, stop=False)
                mm = pe.matmul(OP[:, t], score_acc[:, t], hVn[:, t], start=(i == 0), stop=True)
            mm.then_inc(h_o, 1)

        def body_pe(pe, p, kv, last=False):
            def chunks(s, r, c0, c1, early=None):
                if not last:
                    odd_chunks(pe, s, r, c0, c1)
                elif early:
                    out_early(pe, 1, *early)
            rq, ri, rf = R0 + 2 + 2 * p, R0 + 2 + 2 * p, GROUPS + 3 + p
            for n in range(8):
                if n == 0:
                    chunks(0, rq, 0, 1, early=(0, 1))
                swa_scores(pe, p, n, kv)
                if n >= 1:
                    chunks(0, rq, n, n + 1, early=(1, 2) if n == 1 else None)
                if n >= 1:
                    swa_turn(pe, p, n - 1)
                if n >= 2:
                    swa_pv(pe, p, n - 2, kv)
            chunks(1, ri, 0, 2)
            swa_turn(pe, p, 7)
            swa_pv(pe, p, 6, kv)
            chunks(1, ri, 2, 4)
            swa_pv(pe, p, 7, kv)
            head_turns_pe(pe, p)
            chunks(1, ri, 4, 8)
            out_turn_pe(pe, GROUPS + 2 * p, o_on)
            chunks(2, rf, 0, 2, early=(2, 3))
            head_state_pe(pe, p)
            plan = [(2, rf, 2, 4), (2, rf, 4, 6), (2, rf, 6, 8), (0, rq + 1, 0, 3), (0, rq + 1, 3, 6), (0, rq + 1, 6, 8),
                    (1, ri + 1, 0, 1), (1, ri + 1, 1, 2)]
            for L in range(NLEV):
                level_scores_pe(pe, p, L)
                if last and L == 2:
                    pe.wait_ge(ol_ready, GROUPS + 2 * p + 2)
                chunks(*plan[L], early=(L + 1, L + 2) if L in (2, 3) else None)
            head_out_pe(pe, p)
            chunks(1, ri + 1, 2, 8)
            if not last:
                out_turn_pe(pe, GROUPS + 2 * p + 1, o_on)

        def body_act(act, p, last=False):
            def hi(s, r):
                if not last:
                    act_hi(act, s, r)
            rq, ri, rf = R0 + 2 + 2 * p, R0 + 2 + 2 * p, GROUPS + 3 + p
            swa_exp(act, p, 0)
            act_hi(act, 1, ri)
            swa_exp(act, p, 1)
            swa_pts(act, p, 0)
            for n in range(2, 8):
                swa_exp(act, p, n)
                swa_pts(act, p, n - 1)
                if n == 3:
                    head_decays_act(act, p)
            level_exp_act(act, p, 0)
            swa_pts(act, p, 7)
            act.wait_ge(s_sinkx, p + 1)
            act.activation(sinke, sinkx, ACT.Exp).then_inc(s_sinke, 1)
            hi(2, rf)
            act.wait_ge(h_vturned, p + 1)
            act.activation(hVn, PTP[0][:], ACT.Copy).then_inc(h_vnat, 1)
            act.wait_ge(o_turned, GROUPS + 2 * p + 1)
            act.activation(oh[:, p], S[0][:], ACT.Copy).then_inc(oh_ready, 1)
            act.wait_ge(h_zread, 8 * p + 1 + CR)
            act.activation(o_kN, PTP[1][:], ACT.Copy).then_inc(h_kn, 1)
            for L in range(1, NLEV - 1):
                level_exp_act(act, p, L)
                if L == 1:
                    hi(0, rq + 1)
                if L == 4:
                    hi(1, ri + 1)
            if not last:
                head_sigmoids_act(act, p + 1)
                head_ln_act(act, p + 1)
                hi(0, rq + 2)
            else:
                act_table(act, ACT.Ln)
            act.wait_ge(h_o, p + 2)
            row_rms_act(act, DIFF_G + p, oPT[0])
            act.wait_ge(h_gated, p + 2)
            act.activation(oh[:, p + 4], oPT[1], ACT.Copy).then_inc(oh_ready, 1)

        def body_dve(v, p, last=False):
            def lo(s, r):
                if not last:
                    dve_lo(v, s, r)

            def take(dst, s, r, scale=None, waits=()):
                if last:
                    return
                v.wait_ge(unit_done[s], r + 1)
                for w in waits:
                    v.wait_ge(*w)
                if scale is None:
                    v.tensor_tensor(dst, acc[s][:], rstd[:], ALU.mult).then_inc(acc_read[s], 1)
                else:
                    v.scalar_tensor_tensor(dst, acc[s][:], scale, rstd[:], ALU.mult, ALU.mult).then_inc(acc_read[s], 1)
            rq, ri, rf = R0 + 2 + 2 * p, R0 + 2 + 2 * p, GROUPS + 3 + p
            swa_max(v, p, 0)
            swa_max(v, p, 1)
            head_k_dve(v, p)
            head_scan_dve(v, p)
            dve_lo(v, 1, ri)
            for n in range(2, 8):
                swa_max(v, p, n)
                if n == 5:
                    level_dif_dve(v, p, 0)
            v.wait_ge(s_max, 8 * p + 8)
            v.tensor_tensor(sinkx.rearrange("p (i m) -> p i m", m=2), nmax.rearrange("p (i m) -> p i m", m=2),
                            sm[:, bass.ds(SINK + 2 * p, 2)].unsqueeze(1).to_broadcast([P, 4, 2]), ALU.add).then_inc(s_sinkx, 1)
            take(work[:, 0], 0, rq, QSCALE)
            v.wait_ge(h_eb, p + 1)
            v.wait_ge(h_q, p + 1)
            v.tensor_tensor(qe, qe, hq, ALU.mult).then_inc(h_qe, 1)
            v.wait_ge(s_sinke, p + 1)
            v.wait_ge(s_exp, 8 * p + 8 + CR)
            v.tensor_tensor(rsum, rsum, sinke, ALU.add).then_inc(s_sum, 1)
            v.wait_ge(s_sum, p + 1)
            v.reciprocal(rinv, rsum).then_inc(s_rinv, 1)
            v.wait_ge(s_pv, 8 * p + 8 + CR)
            v.wait_ge(s_rinv, p + 2)
            v.wait_ge(o_turned, GROUPS + 2 * p)
            v.tensor_tensor(o_on.rearrange("p (n d) -> p n d", d=HD), OP[:].rearrange("p (n d) -> p n d", d=HD),
                            rinv.unsqueeze(2).to_broadcast([P, 8, HD]), ALU.mult).then_inc(on_ready, 1)
            lo(2, rf)
            level_dif_dve(v, p, 1)
            take(fr, 1, ri)
            v.wait_ge(oh_ready, GROUPS + 2 * p + 1)
            v.tensor_tensor(ol[:, p], S[0][:], oh[:, p].bitcast(F32), ALU.subtract).then_inc(ol_ready, 1)
            head_state_dve(v, p)
            for L in range(NLEV):
                if L + 2 < NLEV - 1:
                    level_dif_dve(v, p, L + 2)
                level_take_dve(v, p, L)
                if L == 1:
                    lo(0, rq + 1)
                if L == 2:
                    take(qr, 2, rf)
                if L == 4:
                    lo(1, ri + 1)
                if L == 5:
                    take(gr, 0, rq + 1)
            if not last:
                head_f_dve(v, p + 1)
                head_q_dve(v, p + 1)
            lo(0, rq + 2)
            row_mean_dve(v, DIFF_G + p)
            row_rms_dve(v, DIFF_G + p, o_on)
            v.wait_ge(o_turned, GROUPS + 2 * p + 2)
            v.wait_ge(h_gate, p + 1)
            v.scalar_tensor_tensor(oPT[1], S[0][:], sm[:, HGRNN:HGRNN + 1], sgate, ALU.mult, ALU.mult).then_inc(h_gated, 1)
            if not last:
                head_gate_dve(v, p + 1)
            take(ir, 1, ri + 1, waits=[(h_vturned, p + 1)])
            v.wait_ge(oh_ready, GROUPS + 2 * p + 2)
            v.wait_ge(h_gated, p + 2)
            v.tensor_tensor(ol[:, p + 4], oPT[1], oh[:, p + 4].bitcast(F32), ALU.subtract).then_inc(ol_ready, 1)

        def body_pool(g, p):
            head_kdec_pool(g, p)
            for L in range(NLEV - 1):
                level_z_pool(g, p, L)

        ODD_FIRST = ((2, GROUPS), (0, R0), (2, GROUPS + 1), (1, R0), (2, GROUPS + 2), (0, R0 + 1), (1, R0 + 1))

        def odd_pe(pe, l):
            for n, (s, r) in enumerate(ODD_FIRST):
                if n == 0:
                    pe_unit_first(pe, s, r, 2 * l)
                else:
                    pe_unit(pe, s, r, DC, xh, xl)
                if n == 3:
                    pe.wait_ge(acc_read[2], GROUPS + 2)
                    for i in range(TB):
                        mm = pe.transpose(PTP[0][:, i * P:(i + 1) * P], o_vT[:, i * P:(i + 1) * P], ident)
                    mm.then_inc(sv_turned, 1)
            pe.wait_ge(sv_nat, 1)
            with pe.Fori(0, 2) as p:
                body_pe(pe, p, 0)
            body_pe(pe, 2, 1)
            body_pe(pe, 3, 1, last=True)

        def odd_act(act, l):
            for n, (s, r) in enumerate(ODD_FIRST):
                if n >= 2:
                    act_hi(act, s, r)
                if n == 4:
                    act.wait_ge(sv_turned, 1)
                    act.activation(o_Vn, PTP[0][:], ACT.Copy).then_inc(sv_nat, 1)
            act.wait_ge(lb_step, 3)
            act.activation(ge, gd, ACT.Exp).then_inc(lb_exp, 1)
            head_sigmoids_act(act, 0)
            head_ln_act(act, 0)
            act_hi(act, 0, R0 + 2)
            act_table(act, ACT.Exp)
            with act.Fori(0, 3) as p:
                body_act(act, p)
            body_act(act, 3, last=True)

        def odd_dve(v, l):
            def take(dst, s, r, scale=None):
                v.wait_ge(unit_done[s], r + 1)
                if scale is None:
                    v.tensor_tensor(dst, acc[s][:], rstd[:], ALU.mult).then_inc(acc_read[s], 1)
                else:
                    v.scalar_tensor_tensor(dst, acc[s][:], scale, rstd[:], ALU.mult, ALU.mult).then_inc(acc_read[s], 1)
            v.tensor_scalar(nsink, sm[:, SINK:SINK + 8], -1.0, None, ALU.mult).then_inc(nsink_ready, 1)
            g0, g1 = sm[:, GAM:GAM + 4], sm[:, GAM + 4:GAM + 8]
            v.tensor_tensor(gmx, g0, g1, ALU.max).then_inc(lb_step, 1)
            v.wait_ge(lb_step, 1)
            v.tensor_tensor(gd[:, 0:4], g0, gmx, ALU.subtract).then_inc(lb_step, 1)
            v.tensor_tensor(gd[:, 4:8], g1, gmx, ALU.subtract).then_inc(lb_step, 1)
            v.wait_ge(unit_done[2], GROUPS + 1)
            for n, (h, half) in enumerate(((0, 0), (0, 1), (1, 0), (1, 1))):
                src, dst = slice(HD * h, HD * h + HD), slice(HD * half, HD * half + HD)
                v.tensor_tensor(KV[h][dst, :], acc[2][src, :], rstd[src, :], ALU.mult).then_inc(
                    acc_read[2] if n == 3 else k_made, 1)
            dve_lo(v, 2, GROUPS + 1)
            take(work[:, 0], 0, R0, QSCALE)
            dve_lo(v, 1, R0)
            take(o_vT, 2, GROUPS + 1)
            dve_lo(v, 2, GROUPS + 2)
            take(fr, 1, R0)
            dve_lo(v, 0, R0 + 1)
            take(qr, 2, GROUPS + 2)
            dve_lo(v, 1, R0 + 1)
            v.wait_ge(lb_exp, 1)
            v.tensor_tensor(gsum, ge[:, 0:4], ge[:, 4:8], ALU.add).then_inc(lb_step, 1)
            v.wait_ge(lb_step, 4)
            v.reciprocal(grec, gsum).then_inc(lb_step, 1)
            v.wait_ge(lb_step, 5)
            v.tensor_tensor(gsm[:, 0:4], ge[:, 0:4], grec, ALU.mult).then_inc(lb_step, 1)
            v.tensor_tensor(gsm[:, 4:8], ge[:, 4:8], grec, ALU.mult).then_inc(lb_step, 1)
            v.wait_ge(lb_step, 7)
            v.tensor_tensor(glb, gsm[:, 0:4], gsm[:, 4:8], ALU.add).then_inc(lb_step, 1)
            v.wait_ge(lb_step, 8)
            v.tensor_tensor(glb, glb, gsm[:, 0:4], ALU.subtract).then_inc(lb_step, 1)
            v.wait_ge(lb_step, 9)
            v.tensor_scalar(goml, glb, -1.0, 1.0, ALU.mult, ALU.add).then_inc(lb_step, 1)
            v.wait_ge(lb_step, 10)
            v.wait_ge(nsink_ready, 1)
            take(gr, 0, R0 + 1)
            head_f_dve(v, 0)
            dve_lo(v, 0, R0 + 2)
            head_q_dve(v, 0)
            head_gate_dve(v, 0)
            take(ir, 1, R0 + 1)
            with v.Fori(0, 3) as p:
                body_dve(v, p)
            body_dve(v, 3, last=True)

        def odd_pool(g, l):
            with g.Fori(0, 4) as p:
                body_pool(g, p)

        gs, us, sg, gg = (work[:, i] for i in range(4))
        silu_ready, g_ready, gh_ready, gl_ready = sem("silu_ready"), sem("g_ready"), sem("gh_ready"), sem("gl_ready")
        sq_last, last_sq = us, sem("last_sq")
        out_sent, y_out = sem("out_sent"), sem("y_out")

        def F_act(act):
            for l in range(layers):
                if l % 2:
                    odd_act(act, l)
                k = 2 * l + 1
                out_pairs_act(act, PH["mix_out", l], UNIT8, LN_FFN + DC * l)
                act_hi(act, 0, PH["gu", l, 0])
                act_table(act, ACT.Ln)
                act_xh(act, 7, LN_FFN + DC * l + 7, 0, (acc_read[1], PH["mix_out", l] + 4))
                act_hi(act, 1, PH["gu", l, 0])
                act_rsqrt(act, k)
                for half in range(2):
                    r0 = PH["gu", l, half]
                    n0 = FT * l + FH * half
                    act_table(act, ACT.Silu)
                    with act.Fori(0, FH - 1) as i:
                        gu_silu_act(act, r0 + i)
                        act_hi(act, 0, r0 + i + 1)
                        act_hi(act, 1, r0 + i + 1)
                        gu_gh_act(act, i, n0 + i)
                    rd = PH["dn", l, half]
                    gu_silu_act(act, r0 + FH - 1)
                    act_hi(act, 0, rd, FH * P)
                    act_hi(act, 1, rd, FH * P)
                    gu_gh_act(act, FH - 1, n0 + FH - 1)
                    if half == 0 or l == layers - 1:
                        with act.Fori(0, 3) as i:
                            act_hi(act, 0, rd + i + 1, FH * P)
                            act_hi(act, 1, rd + i + 1, FH * P)
                    if half == 0:
                        act_hi(act, 0, rd + 4)
                        act_hi(act, 1, rd + 4)
                    elif l == layers - 1:
                        act_table(act, ACT.Ln)
                        act.wait_ge(acc_read[1], rd + 4)
                        act.activation(sq_last, x[:, DC - 1], ACT.Square).then_inc(last_sq, 1)
                        act_rsqrt(act, 2 * layers)
                    else:
                        gcol = LN_MIX + DC * (l + 1)
                        out_pairs_act(act, rd, FH * P, gcol)
                        act_hi(act, 2, GROUPS)
                        act_table(act, ACT.Ln)
                        act_xh(act, 7, gcol + 7, 0, (acc_read[1], rd + 4))
                        act_hi(act, 0, R0)
                        act_rsqrt(act, 2 * l + 2)

        def out_pairs_act(act, r, n, gcol):
            with act.Fori(0, 3) as i:
                act_hi(act, 0, r + i + 1, n)
                act_xh(act, 2 * i, gcol + 2 * i, 0, (acc_read[0], r + i + 1))
                act_hi(act, 1, r + i + 1, n)
                act_xh(act, 2 * i + 1, gcol + 2 * i + 1, 0, (acc_read[1], r + i + 1))
            act_xh(act, 6, gcol + 6, 0, (acc_read[0], r + 4))

        def gu_silu_act(act, r):
            act.wait_ge(acc_read[0], r + 1)
            act.activation(sg, gs, ACT.Silu).then_inc(silu_ready, 1)

        def gu_gh_act(act, t, n):
            act.wait_ge(g_ready, n + 1)
            act.activation(gh[:, t], gg, ACT.Copy).then_inc(gh_ready, 1)

        def x_add(v, s, j, r):
            v.wait_ge(unit_done[s], r + 1)
            v.tensor_tensor(x[:, j], acc[s][:], x[:, j], ALU.add).then_inc(acc_read[s], 1)

        def x_tile_split(v, s, j, r, gcol, n):
            x_add(v, s, j, r)
            v.wait_ge(acc_read[s], r + 1)
            dve_xl(v, j, gcol + j, n)

        def gate_up_dve(v, t, r, n, width):
            v.wait_ge(unit_done[0], r + 1)
            v.tensor_tensor(gs, acc[0][:], rstd[:], ALU.mult).then_inc(acc_read[0], 1)
            dve_lo(v, 0, r + 1, width)
            v.wait_ge(unit_done[1], r + 1)
            v.tensor_tensor(us, acc[1][:], rstd[:], ALU.mult).then_inc(acc_read[1], 1)
            v.wait_ge(silu_ready, n + 1)
            v.wait_ge(acc_read[1], r + 1)
            v.tensor_tensor(gg, sg, us, ALU.mult).then_inc(g_ready, 1)
            dve_lo(v, 1, r + 1, width)
            v.wait_ge(gh_ready, n + 1)
            v.wait_ge(g_ready, n + 1)
            v.tensor_tensor(gl[:, t], gg, gh[:, t].bitcast(F32), ALU.subtract).then_inc(gl_ready, 1)

        def out_pairs_dve(v, r, n, gcol, k):
            with v.Fori(0, 3) as i:
                for s in range(2):
                    x_add(v, s, 2 * i + s, r + i)
                    dve_lo(v, s, r + i + 1, n)
                    v.wait_ge(acc_read[s], r + i + 1)
                    dve_xl(v, 2 * i + s, gcol + 2 * i + s, DC * k + 2 * i + s)
            x_tile_split(v, 0, 6, r + 3, gcol, DC * k + 6)

        def F_dve(v):
            for l in range(layers):
                if l % 2:
                    odd_dve(v, l)
                k = 2 * l + 1
                r0 = PH["mix_out", l]
                gcol = LN_FFN + DC * l
                out_pairs_dve(v, r0, UNIT8, gcol, k)
                dve_lo(v, 0, PH["gu", l, 0])
                x_tile_split(v, 1, 7, r0 + 3, gcol, DC * k + 7)
                dve_lo(v, 1, PH["gu", l, 0])
                dve_mean(v, k)
                dve_newton(v, k)
                v.wait_ge(rstd_ready, k + 1)
                for half in range(2):
                    r0 = PH["gu", l, half]
                    n0 = FT * l + FH * half
                    with v.Fori(0, FH - 1) as i:
                        gate_up_dve(v, i, r0 + i, n0 + i, UNIT8)
                    gate_up_dve(v, FH - 1, r0 + FH - 1, n0 + FH - 1, FH * P)
                    rd = PH["dn", l, half]
                    if half == 0 or l == layers - 1:
                        with v.Fori(0, 3) as i:
                            x_add(v, 0, 2 * i, rd + i)
                            dve_lo(v, 0, rd + i + 1, FH * P)
                            x_add(v, 1, 2 * i + 1, rd + i)
                            dve_lo(v, 1, rd + i + 1, FH * P)
                        x_add(v, 0, 6, rd + 3)
                        if half == 0:
                            dve_lo(v, 0, rd + 4)
                        x_add(v, 1, 7, rd + 3)
                        if half == 0:
                            dve_lo(v, 1, rd + 4)
                    else:
                        gcol = LN_MIX + DC * (l + 1)
                        kn = 2 * l + 2
                        out_pairs_dve(v, rd, FH * P, gcol, kn)
                        dve_lo(v, 2, GROUPS)
                        x_tile_split(v, 1, 7, rd + 3, gcol, DC * kn + 7)
                        dve_lo(v, 0, R0)
                        dve_mean(v, kn)
                        dve_newton(v, kn)
                        v.wait_ge(rstd_ready, kn + 1)

        def F_pe(pe):
            for l in range(layers):
                if l % 2:
                    odd_pe(pe, l)
                k = 2 * l + 1
                r0 = PH["mix_out", l]
                heads = DC * (l + 1)
                pe.wait_ge(ol_ready, heads)
                pe_chunks(pe, 0, OUT_EARLY, DC - 1, DC, oh, ol)
                pe_unit_wait(pe, 1, r0)
                pe_chunks(pe, 1, 0, 5, DC, oh, ol)
                out_turn_pe(pe, heads - 1, o_on if l % 2 else on)
                pe_chunks(pe, 1, 5, DC - 1, DC, oh, ol)
                pe.wait_ge(ol_ready, heads + 1)
                for s in range(2):
                    pe_chunks(pe, s, DC - 1, DC, DC, oh, ol)
                with pe.Fori(1, 4) as i:
                    for s in range(2):
                        pe_unit(pe, s, r0 + i, DC, oh, ol)
                for half in range(2):
                    r0 = PH["gu", l, half]
                    n0 = FT * l + FH * half
                    if half == 0:
                        pe_unit_first(pe, 0, r0, k)
                    else:
                        pe_unit(pe, 0, r0, DC, xh, xl)
                    pe_unit(pe, 1, r0, DC, xh, xl)
                    with pe.Fori(1, FH) as i:
                        for s in range(2):
                            pe_unit(pe, s, r0 + i, DC, xh, xl)
                    r0 = PH["dn", l, half]
                    pe.wait_ge(gl_ready, n0 + FH - 1)
                    pe_unit_wait(pe, 0, r0)
                    pe_chunks(pe, 0, 0, FH - 1, FH, gh, gl)
                    pe.wait_ge(gl_ready, n0 + FH)
                    pe_chunks(pe, 0, FH - 1, FH, FH, gh, gl)
                    pe_unit(pe, 1, r0, FH, gh, gl)
                    with pe.Fori(1, 4) as i:
                        for s in range(2):
                            pe_unit(pe, s, r0 + i, FH, gh, gl)
            k = 2 * layers
            pe.wait_ge(sacc_ready, DC * (k + 1) - 1)
            pe.wait_ge(mean_ready, k)
            pe.matmul(OP[:], meanw[:], sacc[:], start=True, stop=False)
            pe.wait_ge(last_sq, 1)
            pe.matmul(OP[:], meanw[:], sq_last, start=False, stop=True).then_inc(stat_ready, 1)

        def F_sp(sp):
            for l in range(layers):
                if l % 2:
                    r0 = PH["odd_in", l]
                    for n, (s, r) in enumerate(((2, GROUPS), (0, r0), (2, GROUPS + 1), (1, r0), (2, GROUPS + 2),
                                                (0, r0 + 1), (1, r0 + 1))):
                        sp_load(sp, s, r, w_odd[n], UNIT8)
                    with sp.Fori(0, 3) as p:
                        for n, (s, r) in enumerate(((0, r0 + 2 + 2 * p), (1, r0 + 2 + 2 * p), (2, GROUPS + 3 + p),
                                                    (0, r0 + 3 + 2 * p), (1, r0 + 3 + 2 * p))):
                            sp_load(sp, s, r, w_odd[7 + 5 * p + n], UNIT8)
                r0 = PH["mix_out", l]
                w = w_out_o if l % 2 else w_out_e
                with sp.Fori(0, 4) as i:
                    for s in range(2):
                        sp_load(sp, s, r0 + i, w[2 * i + s], UNIT8)
                for half in range(2):
                    r0 = PH["gu", l, half]
                    with sp.Fori(0, FH) as i:
                        for s in range(2):
                            sp_load(sp, s, r0 + i, w_gu[l, FH * half + i, s], UNIT8)
                    r0 = PH["dn", l, half]
                    with sp.Fori(0, 4) as i:
                        for s in range(2):
                            sp_load(sp, s, r0 + i, w_dn[l, half, 2 * i + s], FH * P)

        def square_tile(g, s, j, r, n, k):
            pool_sq(g, j, n, k, (acc_read[s], r + 1))

        def F_pool(g):
            for l in range(layers):
                if l % 2:
                    odd_pool(g, l)
                k = 2 * l + 1
                for kk, r0 in ((k, PH["mix_out", l]), (k + 1, PH["dn", l, 1])):
                    pool_zero(g, kk)
                    with g.Fori(0, 3) as i:
                        for s in range(2):
                            square_tile(g, s, 2 * i + s, r0 + i, DC * kk + 2 * i + s, kk)
                    square_tile(g, 0, 6, r0 + 3, DC * kk + 6, kk)
                    if kk < 2 * layers:
                        square_tile(g, 1, 7, r0 + 3, DC * kk + 7, kk)

        @block.sync
        def _(sp):
            sp.dma_start(sm[:], small).then_inc(small_in, 16)
            sp.dma_start(x[:, 0:2], xT[:, 0:2]).then_inc(x_in[0], 16)
            sp_load(sp, 0, 0, w_even[0], UNIT8)
            for j in range(1, DC // 2):
                sp.dma_start(x[:, 2 * j:2 * j + 2], xT[:, 2 * j:2 * j + 2]).then_inc(x_in[j], 16)
            sp.dma_start(fa_raw[:], w_fa).then_inc(fa_in, 16)
            sp_load(sp, 1, 0, w_even[1], UNIT8)
            sp_load(sp, 2, 0, w_even[2], UNIT8)
            sp.dma_start(const_stage[:, 0:NCONST], const).then_inc(const_in, 16)
            sp.dma_start(ident, const[:, C_ID:C_ID + P]).then_inc(const_in, 16)
            sp.wait_ge(cq_ones, 1)
            for a, (part, minus) in enumerate(((cpart[:, 0], cpartn[0][:, 0]), (cpart[:, 1], cpartn[0][:, 1]),
                                               (cpart2[:, 0], cpartn[1][:, 0]))):
                sp.wait_ge(gate_step, (5, 8, 10)[a])
                sp.dma_start(CQ[a:a + 1], part).then_inc(cq_in, 16)
                sp.wait_ge(gate_step, (6, 9, 11)[a])
                sp.dma_start(CK[3 + a:4 + a], minus).then_inc(cq_in, 16)
            with sp.Fori(1, GROUPS) as G:
                for s in range(3):
                    sp_load(sp, s, G, w_even[3 * G + s], UNIT8)
            F_sp(sp)
            for j in range(DC):
                sp.wait_ge(y_out, j + 1)
                sp.dma_start(out[:, j], x[:, j]).then_inc(out_sent, 16)
            sp.wait_ge(out_sent, 16 * DC)

        @block.gpsimd
        def _(g):
            g.memset(ones[:], 1.0).then_inc(ones_ready, 1)
            g.memset(meanw[:], 1.0 / D).then_inc(ones_ready, 1)
            for j in range(0, DC, 2):
                g.wait_ge(x_in[j // 2], 16)
                g.tensor_tensor(x_square(j), x[:, j], x[:, j], ALU.mult).then_inc(x_sq[0], 1)
            g.memset(score_acc[:], 0.0).then_inc(ones_ready, 1)
            g.memset(work[0:6, 11:19].bitcast(BF16), 1.0).then_inc(cq_ones, 1)
            g.sem_inc(sq_ready, DC)
            g.sem_inc(sacc_ready, DC)
            with g.Fori(1, FOX_G) as G:
                g.wait_ge(f_scores, 8 * G)
                g.tensor_copy(cq_cur[0:6], CQ[0:6, bass.ds(2 * G, 2)]).then_inc(cq_staged, 1)
            F_pool(g)

        @block.scalar
        def _(act):
            act.wait_ge(small_in, 16)
            for j in range(DC):
                act_xh(act, j, LN_MIX + j, j, (x_in[j // 2], 16))
                if j % 2:
                    act.activation(x_square(j), x[:, j], ACT.Square).then_inc(x_sq[1], 1)
                if j == 1:
                    act_hi(act, 0, 0)
            act.wait_ge(fa_in, 16)
            act.activation(fa_h[:], fa_raw[:], ACT.Copy).then_inc(fa_hi, 1)
            act_hi(act, 1, 0)
            act_hi(act, 2, 0)
            act_rsqrt(act, 0)
            act.wait_ge(const_in, 32)
            act.activation(cstb[:], const_stage[:, 0:C_LEV], ACT.Copy).then_inc(const_b, 1)
            act.activation(level_mask[:], const_stage[:, C_LEV:C_FIRST], ACT.Copy).then_inc(const_b, 1)
            for i in range(TB):
                act.activation(not_first[:, i * P:(i + 1) * P], const_stage[:, C_FIRST:NCONST], ACT.Copy).then_inc(const_b, 1)
            act.wait_ge(gate_step, 2)
            act.activation(za, z, ACT.Abs).then_inc(gate_act, 1)
            act.wait_ge(gate_act, 1)
            act.activation(za, za, ACT.Exp, scale=-1.0).then_inc(gate_act, 1)
            act.wait_ge(gate_act, 2)
            act.activation(za, za, ACT.Ln, bias=1.0).then_inc(gate_act, 1)
            act.wait_ge(lam_sum, 1)
            act.activation(lamt[:, 2:4], OP[:, 0:2], ACT.Exp).then_inc(lam_exp, 1)
            act_hi(act, 0, 1)
            with act.Fori(0, FOX_G) as g:
                fox_group_act(act, g)
            with act.Fori(0, DIFF_G - 1) as g:
                diff_group_act(act, g)
            diff_group_act(act, DIFF_G - 1, last=True)
            F_act(act)

        @block.vector
        def _(v):
            for s in (f_exp, f_turned, f_pv, d_exp, d_mix, d_turned, d_pts, d_pv):
                v.sem_inc(s, CR)
            for s in (s_exp, s_turned, s_pts, s_pv, h_cp, h_z, h_zread):
                v.sem_inc(s, CR)
            for s in (ol_ready, on_ready, rinv_ready, *f_pts, s_rinv, h_o, h_state, h_gated):
                v.sem_inc(s, 1)
            v.wait_ge(small_in, 16)
            for j in range(DC):
                v.wait_ge(x_in[j // 2], 16)
                dve_xl(v, j, LN_MIX + j, j)
                if j == 1:
                    dve_lo(v, 0, 0)
            v.wait_ge(fa_hi, 1)
            v.tensor_tensor(fa_l[:], fa_raw[:], fa_h[:].bitcast(F32), ALU.subtract).then_inc(fa_lo, 1)
            v.tensor_tensor(lamt[0:HD, 0:2], sm[0:HD, LAMB:LAMB + 2], sm[0:HD, LAMB + 2:LAMB + 4],
                            ALU.mult).then_inc(lam_prod, 1)
            dve_lo(v, 1, 0)
            dve_mean(v, 0)
            dve_lo(v, 2, 0)
            dve_newton(v, 0)
            v.wait_ge(rstd_ready, 1)
            v.wait_ge(fa_done, 1)
            v.tensor_tensor(z, acc[2][0:8, :], rstd[0:8, :], ALU.mult).then_inc(gate_step, 1)
            v.wait_ge(gate_step, 1)
            v.tensor_scalar(z, z, sm[0:8, BFG:BFG + 1], None, ALU.add).then_inc(gate_step, 1)
            dve_q(v, 0)
            dve_k(v, 0)
            v.wait_ge(gate_act, 3)
            v.scalar_tensor_tensor(z, z, 0.0, za, ALU.min, ALU.subtract).then_inc(gate_step, 1)
            v.wait_ge(gate_step, 3)
            v.tensor_tensor_scan(cum, z, z, 0.0, ALU.add, ALU.bypass).then_inc(gate_step, 1)
            v.wait_ge(gate_step, 4)
            v.tensor_copy(cpart[:, 0], cum).then_inc(gate_step, 1)
            v.wait_ge(gate_step, 5)
            v.tensor_scalar(cpartn[0][:, 0], cpart[:, 0], -1.0, None, ALU.mult).then_inc(gate_step, 1)
            v.tensor_tensor(z, cum, cpart[:, 0], ALU.subtract).then_inc(gate_step, 1)
            v.wait_ge(gate_step, 7)
            v.tensor_copy(cpart[:, 1], z).then_inc(gate_step, 1)
            v.wait_ge(gate_step, 8)
            v.tensor_scalar(cpartn[0][:, 1], cpart[:, 1], -1.0, None, ALU.mult).then_inc(gate_step, 1)
            v.tensor_tensor(cpart2[:, 0], z, cpart[:, 1], ALU.subtract).then_inc(gate_step, 1)
            v.wait_ge(gate_step, 10)
            v.tensor_scalar(cpartn[1][:, 0], cpart2[:, 0], -1.0, None, ALU.mult).then_inc(gate_step, 1)
            dve_v(v, 0)
            v.wait_ge(lam_exp, 1)
            v.tensor_tensor(lamt[:, 4:5], lamt[:, 3:4], lamt[:, 2:3], ALU.subtract).then_inc(lam_ready, 1)
            v.wait_ge(lam_ready, 1)
            v.tensor_scalar(lamt[:, 7:8], lamt[:, 4:5], -LAMBDA_INIT, None, ALU.add).then_inc(lam_ready, 1)
            v.tensor_scalar(dscale, sm[:, DIFFN:DIFFN + 1], 1.0 - LAMBDA_INIT, None, ALU.mult).then_inc(lam_ready, 1)
            dve_lo(v, 0, 1)
            v.wait_ge(cq_in, 16 * 6)
            v.tensor_copy(cq_cur[0:6], CQ[0:6, 0:2]).then_inc(cq_staged, 1)
            with v.Fori(0, FOX_G) as g:
                fox_group_dve(v, g)
            v.wait_ge(lam_ready, 3)
            with v.Fori(0, DIFF_G - 1) as g:
                diff_group_dve(v, g)
            diff_group_dve(v, DIFF_G - 1, last=True)
            F_dve(v)
            k = 2 * layers
            dve_mean(v, k)
            dve_newton(v, k)
            v.wait_ge(rstd_ready, k + 1)
            for j in range(DC):
                v.scalar_tensor_tensor(x[:, j], x[:, j], sm[:, LN_FIN + j:LN_FIN + j + 1], rstd[:],
                                       ALU.mult, ALU.mult).then_inc(y_out, 1)

        @block.tensor
        def _(pe):
            pe.wait_ge(ones_ready, 2)
            pe_stat_first(pe, 0)
            pe_stat_first(pe, 1)
            pe_unit_wait(pe, 0, 0)
            for c in range(DC):
                if c + 2 < DC:
                    pe_stat_first(pe, c + 2)
                pe.wait_ge(xl_ready, c + 1)
                pe_chunks(pe, 0, c, c + 1, DC, xh, xl)
            pe.wait_ge(fa_lo, 1)
            for c in range(DC):
                a, b = fa_h[:, 8 * c:8 * c + 8], fa_l[:, 8 * c:8 * c + 8]
                pe.matmul(acc[2][0:8, :], a, xh[:, c], start=(c == 0), stop=False)
                pe.matmul(acc[2][0:8, :], a, xl[:, c], start=False, stop=False)
                mm = pe.matmul(acc[2][0:8, :], b, xh[:, c], start=False, stop=(c == DC - 1))
            mm.then_inc(fa_done, 1)
            pe_unit(pe, 1, 0, DC, xh, xl)
            pe.wait_ge(lam_prod, 1)
            pe.wait_ge(mean_ready, 1)
            pe.matmul(OP[:, 0:2], ones[0:HD, :], lamt[0:HD, 0:2], start=True, stop=True).then_inc(lam_sum, 1)
            pe.wait_ge(gate_step, 1)
            pe_unit(pe, 2, 0, DC, xh, xl)
            pe.wait_ge(const_b, 2 + TB)
            pe.wait_ge(cq_in, 16 * 6)
            with pe.Fori(0, FOX_G) as g:
                fox_group_pe(pe, g)
            with pe.Fori(0, DIFF_G - 1) as g:
                diff_group_pe(pe, g)
            diff_group_pe(pe, DIFF_G - 1, last=True)
            F_pe(pe)


def kernel(**inputs):
    import numpy as np
    import concourse.bacc as _bacc
    from concourse import mybir as _mybir
    from concourse.bass_utils import run_bass_kernel_spmd as _run
    layers = LAYERS

    a = {n: np.asarray(v) for n, v in inputs.items()}

    def tiles(w, cols, width=P):
        k = w.shape[0] // P
        return np.ascontiguousarray(np.stack([
            w[:, c:c + width].reshape(k, P, width).transpose(1, 0, 2).reshape(P, k * width) for c in cols]))

    def cols(v):
        return v.reshape(-1, P).T

    w = a["w_in_even"][0]
    starts = []
    for g in range(FOX_G):
        starts += [g * P, 512 + g * P, 1024 + g * P]
    for g in range(DIFF_G):
        starts += [1544 + g * P, 2056 + g * P, 2568 + g * P]
    small = np.zeros((P, NSMALL), np.float32)
    small[:, LN_MIX:LN_MIX + 16] = cols(a["ln_mix"])
    small[:, LN_FFN:LN_FFN + 16] = cols(a["ln_ffn"])
    small[:, LN_FIN:LN_FIN + 8] = cols(a["ln_final"])
    small[:, DIFFN:DIFFN + 1] = cols(a["diff_norm"])
    small[:, HGRNN:HGRNN + 1] = cols(a["hgrn_norm"])
    small[0:8, BFG] = a["b_forget"][0]
    for n, name in enumerate(("lambda_q1", "lambda_q2", "lambda_k1", "lambda_k2")):
        small[0:HD, LAMB + n] = a[name][0]
    small[:, SINK:SINK + 8] = a["sinks"]
    small[:, GAM:GAM + 8] = cols(a["hgrn_gamma"])
    def hgrn(h):
        return [768 + 512 * b + P * h for b in (1, 0, 3, 2)]
    odd_cols = [512, 0, 640, *hgrn(0)]
    for p in range(3):
        odd_cols += [P * (p + 1), *hgrn(p + 1)]
    gate, up, down = a["w_gate"], a["w_up"], a["w_down"]
    fcols = [t * P for t in range(FT)]
    ocols = [j * P for j in range(DC)]
    arrays = {
        "xT": np.ascontiguousarray(a["x"][0].T.reshape(DC, P, SEQ).transpose(1, 0, 2)),
        "small": small,
        "const": constants(),
        "w_even": tiles(w, starts),
        "w_fa": tiles(w, [1536], 8)[0],
        "w_out_e": tiles(a["w_out_even"][0], ocols),
        "w_odd": tiles(a["w_in_odd"][0], odd_cols),
        "w_out_o": tiles(a["w_out_odd"][0], ocols),
        "w_gu": np.stack([np.stack([tiles(gate[l], fcols), tiles(up[l], fcols)], 1) for l in range(2)]),
        "w_dn": np.stack([np.stack([tiles(down[l, h * FH * P:(h + 1) * FH * P], ocols) for h in range(2)])
                          for l in range(2)]),
    }
    nc = _bacc.Bacc("TRN2", target_bir_lowering=False, num_devices=1)
    args = [nc.dram_tensor(f"in_{n}", v.shape, _mybir.dt.from_np(v.dtype), kind="ExternalInput").ap()
            for n, v in arrays.items()]
    out = nc.dram_tensor("out", (P, DC, SEQ), F32, kind="ExternalOutput").ap()
    build(nc, layers, *args, out)
    r = _run(nc, [{f"in_{n}": v for n, v in arrays.items()}], core_ids=[0])
    y = r.results[0]["out"]
    return np.ascontiguousarray(y.transpose(2, 1, 0).reshape(1, SEQ, D))


LAYERS = 2
```

```python
from contextlib import ExitStack

import concourse.bass as bass
from concourse import mybir

F32 = mybir.dt.float32
F32R = mybir.dt.float32r
BF16 = mybir.dt.bfloat16
ALU = mybir.AluOpType
ACT = mybir.ActivationFunctionType
AX = mybir.AxisListType.X

P = 128
SEQ = 512
D = 1024
DC = D // P
TB = SEQ // P
HD = 64
FF = 2816
FT = FF // P
FH = FT // 2
EPS = 1e-6
LAMBDA_INIT = 0.8 - 0.6
QSCALE = HD ** -0.5
NEG = -1e30
FOX_G = 4
DIFF_G = 4
GROUPS = FOX_G + DIFF_G

LN_MIX, LN_FFN, LN_FIN = 0, 16, 32
DIFFN, HGRNN, BFG, LAMB, SINK, GAM = 40, 41, 42, 43, 47, 55
NSMALL = 63
C_ID, C_FOX, C_DIFF, C_SWA, C_LEV = 0, 128, 256, 384, 640
NLEV = 8
C_FIRST = C_LEV + NLEV * P
NCONST = C_FIRST + P


def constants():
    import numpy as np
    c = np.zeros((P, NCONST), np.float32)
    q = np.arange(P)[:, None]
    s = np.arange(P)[None, :]
    c[:, C_ID:C_ID + P] = q == s
    c[:, C_FOX:C_FOX + P] = np.where(s <= q, 0.0, NEG)
    c[:, C_DIFF:C_DIFF + P] = np.where(s // 64 <= q // 64, 0.0, NEG)
    k = np.arange(2 * P)[None, :] // 64
    c[:, C_SWA:C_SWA + 2 * P] = np.where((k >= q // 64 + 1) & (k <= q // 64 + 2), 0.0, NEG)
    sp, tf = q, s
    for lev in range(NLEV - 1):
        m = 64 >> lev
        on = (sp // (2 * m) == tf // (2 * m)) & (sp % (2 * m) < m) & (tf % (2 * m) >= m)
        c[:, C_LEV + lev * P:C_LEV + (lev + 1) * P] = on
    c[:, C_LEV + (NLEV - 1) * P:C_LEV + NLEV * P] = sp == tf
    c[:, C_FIRST:C_FIRST + P] = tf != 0
    return c


def build(nc, layers, xT, small, const, w_even, w_fa, w_out_e, w_odd, w_out_o, w_gu, w_dn, out):
    with ExitStack() as ctx:
        def sb(name, shape, dt=F32):
            return ctx.enter_context(nc.sbuf_tensor(name, shape, dt))

        def sem(name):
            return ctx.enter_context(nc.semaphore(name))

        def sems(name, n):
            return [sem(f"{name}{i}") for i in range(n)]

        x = sb("x", [P, DC, SEQ])
        xh = sb("xh", [P, DC, SEQ], F32R)
        xl = sb("xl", [P, DC, SEQ], F32R)
        split_acts = sb("split_acts", [P, 2 * FH, SEQ], F32R)
        gh, gl = split_acts[:, 0:FH], split_acts[:, FH:2 * FH]
        oh, ol = split_acts[:, 0:DC], split_acts[:, DC:2 * DC]
        ring_raw = sb("ring_raw", [P, (2 * FH + DC) * P])
        ring_hi = sb("ring_hi", [P, (2 * FH + DC) * P], F32R)
        ring_lo = sb("ring_lo", [P, (2 * FH + DC) * P], F32R)

        def ring(t, s, a, b):
            return t[:, s * FH * P + a:s * FH * P + b]
        fa_raw = sb("fa_raw", [P, DC * 8])
        fa_h = sb("fa_h", [P, DC * 8], F32R)
        fa_l = sb("fa_l", [P, DC * 8], F32R)
        work = sb("work", [P, 24, SEQ])
        rstd = sb("rstd", [P, SEQ])
        mean = sb("mean", [P, SEQ])
        newton = sb("newton", [P, SEQ])
        sq = sb("sq", [P, SEQ])
        sq_last = work[:, 1]
        sacc = sb("sacc", [P, SEQ])
        sm = sb("sm", [P, NSMALL])
        ident = sb("ident", [P, P])[:]
        level_mask = sb("level_mask", [P, NLEV * P], mybir.dt.uint8)
        not_first = sb("not_first", [P, SEQ])
        score_acc = sb("score_acc", [P, SEQ])
        cstb = sb("cstb", [P, C_LEV], BF16)
        identb = cstb[:, C_ID:C_ID + P]
        ones = sb("ones", [P, P])
        meanw = sb("meanw", [P, P])
        tiny = sb("tiny", [P, 128])

        bank = [ctx.enter_context(nc.psum_tensor(f"bank{i}", [P, SEQ], F32)) for i in range(8)]
        acc = bank[0:3]
        S = bank[3:5]
        PTP = bank[5:7]
        OP = bank[7]

        raw_in, hi_ready, lo_ready = sems("raw_in", 3), sems("hi_ready", 3), sems("lo_ready", 3)
        unit_done, acc_read = sems("unit_done", 3), sems("acc_read", 3)
        x_in, x_sq = sems("x_in", DC // 2), sems("x_sq", 2)
        small_in, const_in, fa_in = sem("small_in"), sem("const_in"), sem("fa_in")
        const_b = sem("const_b")
        xh_ready, xl_ready = sem("xh_ready"), sem("xl_ready")
        sq_ready, sacc_ready, sacc_zero = sem("sq_ready"), sem("sacc_ready"), sem("sacc_zero")
        stat_ready, mean_ready, ln_ready, y_ready = sem("stat_ready"), sem("mean_ready"), sem("ln_ready"), sem("y_ready")
        nt_ready, rstd_ready = sem("nt_ready"), sem("rstd_ready")
        ones_ready, last_sq = sem("ones_ready"), sem("last_sq")

        block = ctx.enter_context(nc.Block())

        UNIT8 = DC * P
        Q0 = GROUPS + 2
        QO = {0: GROUPS, 1: Q0 + 6}
        PH = {}
        r = GROUPS
        for l in range(layers):
            if l % 2:
                PH["odd_in", l] = r
                r += 8
            PH["mix_out", l] = r
            r += 3
            for half in range(2):
                PH["gu", l, half] = r
                r += FH
                PH["dn", l, half] = r
                r += 4

        def act_table(act, func):
            act.activation(table_warm, ones[:, 0:1], func)

        def sp_load(sp, s, r, src, n):
            if not (isinstance(r, int) and r == 0):
                sp.wait_ge(lo_ready[s], r)
            sp.dma_start(ring(ring_raw, s, 0, n), src).then_inc(raw_in[s], 16)

        def act_hi(act, s, r, n=UNIT8):
            if not (isinstance(r, int) and r == 0):
                act.wait_ge(unit_done[s], r)
            act.wait_ge(raw_in[s], 16 * (r + 1))
            act.activation(ring(ring_hi, s, 0, n), ring(ring_raw, s, 0, n), ACT.Copy).then_inc(hi_ready[s], 1)

        def dve_lo(v, s, r, n=UNIT8):
            v.wait_ge(hi_ready[s], r + 1)
            v.tensor_tensor(ring(ring_lo, s, 0, n), ring(ring_raw, s, 0, n), ring(ring_hi, s, 0, n).bitcast(F32),
                            ALU.subtract).then_inc(lo_ready[s], 1)

        def pe_chunk(pe, s, c, n, rh, rl, b):
            w0, w1 = ring(ring_hi, s, c * P, (c + 1) * P), ring(ring_lo, s, c * P, (c + 1) * P)
            pe.matmul(b, w0, rh[:, c], start=(c == 0), stop=False)
            pe.matmul(b, w0, rl[:, c], start=False, stop=False)
            return pe.matmul(b, w1, rh[:, c], start=False, stop=(c == n - 1))

        def pe_unit_wait(pe, s, r):
            pe.wait_ge(lo_ready[s], r + 1)
            if not (isinstance(r, int) and r == 0):
                pe.wait_ge(acc_read[s], r)

        def pe_unit(pe, s, r, n, rh, rl):
            pe_unit_wait(pe, s, r)
            for c in range(n):
                mm = pe_chunk(pe, s, c, n, rh, rl, acc[s][:])
            mm.then_inc(unit_done[s], 1)

        def pe_chunks(pe, s, c0, c1, n, rh, rl):
            for c in range(c0, c1):
                mm = pe_chunk(pe, s, c, n, rh, rl, acc[s][:])
            if c1 == n:
                mm.then_inc(unit_done[s], 1)

        def pe_unit_first(pe, s, r, k):
            pe_unit_wait(pe, s, r)
            for c in range(DC):
                pe.wait_ge(xl_ready, DC * k + c + 1)
                if c == 3:
                    pe_stat(pe, k)
                pe_chunks(pe, s, c, c + 1, DC, xh, xl)

        def out_units(l):
            r0, q0 = PH["mix_out", l], QO[l]
            return [(0, r0), (1, r0), (2, q0), (0, r0 + 1), (1, r0 + 1), (0, r0 + 2), (1, r0 + 2), (2, q0 + 1)]

        def out_early(pe, l, c0, c1):
            if c0 == 0:
                pe_unit_wait(pe, 0, PH["mix_out", l])
            pe_chunks(pe, 0, c0, c1, DC, oh, ol)

        def pe_stat(pe, k):
            pe.wait_ge(sacc_ready, (DC - 1) * (k + 1))
            pe.wait_ge(mean_ready, k)
            pe.matmul(OP[:], meanw[:], sacc[:], start=True, stop=False)
            pe.wait_ge(last_sq, k)
            pe.matmul(OP[:], meanw[:], sq_last, start=False, stop=True).then_inc(stat_ready, 1)

        def act_last_square(act, s, r):
            act.wait_ge(acc_read[s], r + 1)
            act.activation(sq_last, x[:, DC - 1], ACT.Square).then_inc(last_sq, 1)

        def x_square(c):
            return work[:, (0, 1, 2, 3, 8, 9, 10, 20)[c]]

        def pe_stat_first(pe, c):
            pe.wait_ge(x_sq[c % 2], c // 2 + 1)
            mm = pe.matmul(OP[:], meanw[:], x_square(c), start=(c == 0), stop=(c == DC - 1))
            if c == DC - 1:
                mm.then_inc(stat_ready, 1)

        def dve_mean(v, k):
            v.wait_ge(ln_ready, k + 1)
            v.tensor_scalar(mean[:], OP[:], EPS, None, ALU.add).then_inc(mean_ready, 1)

        def act_rsqrt(act, k):
            act.wait_ge(stat_ready, k + 1)
            act.activation(newton[:], OP[:], ACT.Ln, bias=eps).then_inc(ln_ready, 1)
            act.wait_ge(ln_ready, k + 1)
            act.activation(rstd[:], newton[:], ACT.Exp, scale=-0.5).then_inc(y_ready, 1)

        def dve_newton(v, k):
            v.wait_ge(mean_ready, k + 1)
            v.wait_ge(y_ready, k + 1)
            v.scalar_tensor_tensor(newton[:], mean[:], -0.5, rstd[:], ALU.mult, ALU.mult).then_inc(nt_ready, 1)
            v.wait_ge(nt_ready, 2 * k + 1)
            v.tensor_tensor(newton[:], newton[:], rstd[:], ALU.mult).then_inc(nt_ready, 1)
            v.wait_ge(nt_ready, 2 * k + 2)
            v.scalar_tensor_tensor(rstd[:], newton[:], 1.5, rstd[:], ALU.add, ALU.mult).then_inc(rstd_ready, 1)

        def act_xh(act, j, gcol, gate):
            act.wait_ge(*gate)
            act.activation(xh[:, j], x[:, j], ACT.Copy, scale=sm[:, gcol:gcol + 1] if isinstance(j, int)
                           else sm[:, bass.ds(gcol, 1)]).then_inc(xh_ready, 1)

        def dve_xl(v, j, gcol, n):
            v.wait_ge(xh_ready, n + 1)
            v.scalar_tensor_tensor(xl[:, j], x[:, j], sm[:, gcol:gcol + 1] if isinstance(j, int) else sm[:, bass.ds(gcol, 1)],
                                   xh[:, j].bitcast(F32), ALU.mult, ALU.subtract).then_inc(xl_ready, 1)

        def square_tile(g, s, j, r, n):
            g.wait_ge(acc_read[s], r + 1)
            g.wait_ge(sacc_ready, n)
            g.tensor_tensor(sq[:], x[:, j], x[:, j], ALU.mult).then_inc(sq_ready, 1)
            g.wait_ge(sq_ready, n + 1)
            g.tensor_tensor(sacc[:], sacc[:], sq[:], ALU.add).then_inc(sacc_ready, 1)

        def pool_zero(g, k):
            g.wait_ge(stat_ready, k)
            g.memset(sacc[:], 0.0).then_inc(sacc_zero, 1)
            g.wait_ge(sacc_zero, k)

        q_cur, k_cur, vT, Vn = work[:, 0], work[:, 1], work[:, 2], work[:, 3]
        PB = [work[:, 4 + i] for i in range(4)]
        PTS = [work[:, 8 + i] for i in range(2)]
        on = work[:, 10]
        CQ = work[:, 11:15].bitcast(BF16).rearrange("p a b -> p (a b)").rearrange("p (h t) -> p h t", h=8)
        CK = work[:, 15:19].bitcast(BF16).rearrange("p a b -> p (a b)").rearrange("p (h t) -> p h t", h=8)
        cq_cur = work[:, 19].bitcast(BF16).rearrange("p (h t) -> p h t", h=2)
        const_stage = work[:, 4:8].rearrange("p a b -> p (a b)")
        z = work[0:8, 20]
        za = work[0:8, 21]
        cum = work[0:8, 22]
        cpart = work[0:8, 23].bitcast(BF16).rearrange("p (a t) -> p a t", a=2)
        cpart2 = work[0:8, 10].bitcast(BF16).rearrange("p (a t) -> p a t", a=2)
        cpartn = [work[0:8, 8 + i].bitcast(BF16).rearrange("p (a t) -> p a t", a=2) for i in range(2)]
        nmax = tiny[:, 0:8]
        rsum = tiny[:, 8:16]
        rinv = tiny[:, 16:24]
        lamt = tiny[:, 24:32]
        dss = tiny[:, 32:36]
        dn = tiny[:, 36:48]
        dscale = tiny[:, 48:49]
        table_warm = tiny[:, 121:122]
        eps = tiny[:, 122:123]

        fa_hi, fa_lo, fa_done, fa_read = sem("fa_hi"), sem("fa_lo"), sem("fa_done"), sem("fa_read")
        gate_step, gate_act = sem("gate_step"), sem("gate_act")
        cq_in, cq_ones, cq_staged = sem("cq_in"), sem("cq_ones"), sem("cq_staged")
        lam_prod, lam_sum, lam_exp, lam_ready = sem("lam_prod"), sem("lam_sum"), sem("lam_exp"), sem("lam_ready")
        v_turned, v_nat = sem("v_turned"), sem("v_nat")
        f_scores, f_max, f_exp, f_turned, f_pv = (sem(n) for n in (
            "f_scores", "f_max", "f_exp", "f_turned", "f_pv"))
        f_pts = sems("f_pts", 2)
        d_scores, d_max, d_exp, d_mix, d_turned, d_pts, d_pv = (sem(n) for n in (
            "d_scores", "d_max", "d_exp", "d_mix", "d_turned", "d_pts", "d_pv"))
        rinv_ready, d_step = sem("rinv_ready"), sem("d_step")
        d_sq, d_ln, d_act = sem("d_sq"), sem("d_ln"), sem("d_act")
        on_ready, o_turned, oh_ready, ol_ready = sem("on_ready"), sem("o_turned"), sem("oh_ready"), sem("ol_ready")

        def pe_v_turn(pe, g):
            pe.wait_ge(acc_read[2], g + 1)
            for i in range(TB):
                mm = pe.transpose(acc[2][:, i * P:(i + 1) * P], vT[:, i * P:(i + 1) * P], ident)
            mm.then_inc(v_turned, 1)

        def act_v_nat(act, g, pv, n):
            act.wait_ge(v_turned, g + 1)
            if n is not None:
                act.wait_ge(pv, n)
            act.activation(Vn, acc[2][:], ACT.Copy).then_inc(v_nat, 1)

        def out_turn_pe(pe, n, src):
            pe.wait_ge(on_ready, n + 2)
            for i in range(TB):
                mm = pe.transpose(S[0][:, i * P:(i + 1) * P], src[:, i * P:(i + 1) * P], ident)
            mm.then_inc(o_turned, 1)

        QA = [split_acts[:, 2 * DC + i] for i in range(2)]
        KA = [split_acts[:, 2 * DC + 2 + i] for i in range(2)]
        QL = split_acts[:, 2 * DC + 4]
        HALF = [slice(0, HD), slice(HD, P)]
        qh_ready, ql_ready, kh_ready, kl_ready = sem("qh_ready"), sem("ql_ready"), sem("kh_ready"), sem("kl_ready")

        def q_split_act(act, G):
            act.wait_ge(acc_read[0], G + 1)
            for m in range(2):
                for half in range(2):
                    act.activation(QA[m][HALF[half]], q_cur[HALF[m]], ACT.Copy).then_inc(qh_ready, 1)

        def q_split_pool(g, G):
            g.wait_ge(qh_ready, 4 * G + 4)
            for m in range(2):
                h = HALF[m]
                g.wait_ge(ql_ready, 2 * G + m + 1)
                g.tensor_tensor(QL[h], q_cur[h], QA[m][h].bitcast(F32), ALU.subtract).then_inc(ql_ready, 1)

        def k_split_act(act, G):
            act.wait_ge(acc_read[1], G + 1)
            for m in range(2):
                act.activation(KA[m][HALF[m]], k_cur[HALF[m]], ACT.Copy).then_inc(kh_ready, 1)

        def k_split_dve(v, G):
            v.wait_ge(kh_ready, 2 * G + 2)
            v.wait_ge(acc_read[1], G + 1)
            for m in range(2):
                h = HALF[m]
                v.tensor_tensor(KA[m][HALF[1 - m]], k_cur[h], KA[m][h].bitcast(F32), ALU.subtract).then_inc(kl_ready, 1)

        def pe_split_wait(pe, G):
            pe.wait_ge(ql_ready, 2 * G + 3)
            pe.wait_ge(kl_ready, 2 * G + 2)

        def pe_scores(pe, b, m, i, w):
            t = slice(i * P, (i + 1) * P)
            pe.matmul(b[:, 0:w], QA[m][:, t], KA[m][:, 0:w], start=True, stop=False)
            pe.matmul(b[:, 0:w], QL[HALF[m], t], KA[m][HALF[m], 0:w], start=False, stop=False)

        CR = 2

        def fox_scores(pe, g, n):
            k, m, i = 8 * g + n, n % 2, n // 2
            pe.wait_ge(f_exp, k + 1)
            if n == 0:
                pe_split_wait(pe, g)
                pe.wait_ge(cq_staged, g + 1)
                pe.wait_ge(ol_ready, g + 1)
            b, w = S[n % 2], P * (i + 1)
            pe_scores(pe, b, m, i, w)
            pe.matmul(b[:, 0:w], cq_cur[0:6, m, i * P:(i + 1) * P],
                      CK[0:6, bass.ds(2 * g + m, 1), 0:w].rearrange("p a t -> p (a t)"), start=False, stop=False)
            pe.matmul(b[:, w - P:w], identb, cstb[:, C_FOX:C_FOX + P], start=False, stop=True).then_inc(f_scores, 1)

        def fox_max(v, g, n):
            v.wait_ge(f_scores, 8 * g + n + 1)
            v.tensor_reduce(nmax[:, n:n + 1], S[n % 2][:, 0:P * (n // 2 + 1)], AX, ALU.max, negate=True).then_inc(f_max, 1)

        def fox_exp(act, g, n):
            k, w = 8 * g + n, P * (n // 2 + 1)
            act.wait_ge(f_max, k + 1)
            act.wait_ge(f_turned, k + 1)
            if n == 0:
                act.wait_ge(rinv_ready, g + 1)
            act.activation(PB[n % 2][:, 0:w], S[n % 2][:, 0:w], ACT.Exp, bias=nmax[:, n:n + 1],
                           accum_out=rsum[:, n:n + 1]).then_inc(f_exp, 1)

        def fox_turn(pe, g, n):
            k = 8 * g + n
            pe.wait_ge(f_exp, k + 1 + CR)
            pe.wait_ge(f_pts[n % 2], 4 * g + n // 2 + 1)
            for j in range(n // 2 + 1):
                mm = pe.transpose(PTP[n % 2][:, j * P:(j + 1) * P], PB[n % 2][:, j * P:(j + 1) * P], ident)
            mm.then_inc(f_turned, 1)

        def fox_pts_wait(e, g, n):
            k = 8 * g + n
            e.wait_ge(f_turned, k + 1 + CR)
            e.wait_ge(f_pv, k + 1)

        def fox_pts_dve(v, g, n):
            fox_pts_wait(v, g, n)
            w = P * (n // 2 + 1)
            v.tensor_copy(PTS[n % 2][:, 0:w], PTP[n % 2][:, 0:w]).then_inc(f_pts[n % 2], 1)

        def fox_pts_act(act, g, n):
            fox_pts_wait(act, g, n)
            w = P * (n // 2 + 1)
            act.activation(PTS[n % 2][:, 0:w], PTP[n % 2][:, 0:w], ACT.Copy).then_inc(f_pts[n % 2], 1)

        def fox_pv(pe, g, n):
            k, m, i = 8 * g + n, n % 2, n // 2
            pe.wait_ge(f_pts[n % 2], 4 * g + n // 2 + 2)
            if n == 0:
                pe.wait_ge(v_nat, g + 1)
                pe.wait_ge(on_ready, g + 1)
            for j in range(i + 1):
                mm = pe.matmul(OP[:, i * P + m * HD:i * P + m * HD + HD], PTS[n % 2][:, j * P:(j + 1) * P],
                               Vn[:, j * P + m * HD:j * P + m * HD + HD], start=(j == 0), stop=(j == i))
            mm.then_inc(f_pv, 1)

        def proj_wait(pe, s, G):
            pe.wait_ge(lo_ready[s], G + 1)
            pe.wait_ge(acc_read[s], G)
            if s == 2:
                pe.wait_ge(v_nat, G)

        def proj_chunks(pe, s, G, c0, c1):
            if c0 == 0:
                proj_wait(pe, s, G)
            for c in range(c0, c1):
                mm = pe_chunk(pe, s, c, DC, xh, xl, acc[s][:])
            if c1 == DC:
                mm.then_inc(unit_done[s], 1)

        def dve_q(v, G):
            v.wait_ge(unit_done[0], G + 1)
            v.scalar_tensor_tensor(q_cur, acc[0][:], QSCALE, rstd[:], ALU.mult, ALU.mult).then_inc(acc_read[0], 1)

        def dve_k(v, G):
            v.wait_ge(unit_done[1], G + 1)
            v.tensor_tensor(k_cur, acc[1][:], rstd[:], ALU.mult).then_inc(acc_read[1], 1)

        def dve_v(v, G):
            v.wait_ge(unit_done[2], G + 1)
            v.tensor_tensor(vT, acc[2][:], rstd[:], ALU.mult).then_inc(acc_read[2], 1)

        def fox_group_pe(pe, g):
            proj_chunks(pe, 0, g + 1, 0, 1)
            for n in range(8):
                fox_scores(pe, g, n)
                if n == 1:
                    pe_v_turn(pe, g)
                if n < 6:
                    proj_chunks(pe, 0, g + 1, *((1, 2), (2, 4), (4, 5), (5, 6), (6, 7), (7, 8))[n])
                else:
                    proj_chunks(pe, 1, g + 1, n - 6, n - 5)
                if n >= 1:
                    fox_turn(pe, g, n - 1)
                if n >= 2:
                    fox_pv(pe, g, n - 2)
            proj_chunks(pe, 1, g + 1, 2, 3)
            fox_turn(pe, g, 7)
            fox_pv(pe, g, 6)
            proj_chunks(pe, 1, g + 1, 3, 5)
            fox_pv(pe, g, 7)
            proj_chunks(pe, 1, g + 1, 5, 8)
            proj_chunks(pe, 2, g + 1, 0, 1)
            out_turn_pe(pe, g, on)
            proj_chunks(pe, 2, g + 1, 1, 8)

        def fox_group_act(act, g):
            for n in range(8):
                fox_exp(act, g, n)
                if n == 0:
                    act_hi(act, 1, g + 1)
                if n == 1:
                    act_v_nat(act, g, f_pv, 8 * g + CR)
                if n >= 2 and n % 2 == 0:
                    fox_pts_act(act, g, n - 1)
            fox_pts_act(act, g, 7)
            act_hi(act, 2, g + 1)
            act_hi(act, 0, g + 2)
            q_split_act(act, g + 1)
            k_split_act(act, g + 1)
            act_oh(act, g)

        def act_oh(act, g):
            act.wait_ge(o_turned, g + 1)
            act.activation(oh[:, g], S[0][:], ACT.Copy).then_inc(oh_ready, 1)

        def fox_group_dve(v, g):
            fox_max(v, g, 0)
            dve_lo(v, 1, g + 1)
            for n in range(1, 8):
                fox_max(v, g, n)
                if n % 2 == 1:
                    fox_pts_dve(v, g, n - 1)
            v.wait_ge(f_exp, 8 * g + 8 + CR)
            v.reciprocal(rinv, rsum).then_inc(rinv_ready, 1)
            dve_q(v, g + 1)
            dve_lo(v, 2, g + 1)
            v.wait_ge(f_pv, 8 * g + 8 + CR)
            v.wait_ge(rinv_ready, g + 2)
            v.tensor_tensor(on.rearrange("p (n d) -> p n d", d=HD), OP[:].rearrange("p (n d) -> p n d", d=HD),
                            rinv.unsqueeze(2).to_broadcast([P, 8, HD]), ALU.mult).then_inc(on_ready, 1)
            dve_k(v, g + 1)
            dve_lo(v, 0, g + 2)
            k_split_dve(v, g + 1)
            v.wait_ge(oh_ready, g + 1)
            v.tensor_tensor(ol[:, g], S[0][:], oh[:, g].bitcast(F32), ALU.subtract).then_inc(ol_ready, 1)
            dve_v(v, g + 1)

        def diff_scores(pe, g, i):
            for m in range(2):
                k = 8 * g + 2 * i + m
                pe.wait_ge(d_exp, k + 1)
                if i == 0 and m == 0:
                    pe_split_wait(pe, FOX_G + g)
                    pe.wait_ge(ol_ready, FOX_G + g + 1)
                w = P * (i + 1)
                pe_scores(pe, S[m], m, i, w)
                pe.matmul(S[m][:, w - P:w], identb, cstb[:, C_DIFF:C_DIFF + P], start=False,
                          stop=True).then_inc(d_scores, 1)

        def diff_max(v, g, i):
            for m in range(2):
                n = 2 * i + m
                v.wait_ge(d_scores, 8 * g + n + 1)
                v.tensor_reduce(nmax[:, n:n + 1], S[m][:, 0:P * (i + 1)], AX, ALU.max, negate=True).then_inc(d_max, 1)

        def diff_exp(act, g, i):
            for m in range(2):
                n = 2 * i + m
                act.wait_ge(d_max, 8 * g + n + 1)
                act.wait_ge(d_mix, 2 * (4 * g + i) + 1 + m)
                w = P * (i + 1)
                act.activation(PB[m][:, 0:w], S[m][:, 0:w], ACT.Exp, bias=nmax[:, n:n + 1],
                               accum_out=rsum[:, n:n + 1]).then_inc(d_exp, 1)

        def diff_mix(v, g, i):
            t, w, pm = 4 * g + i, P * (i + 1), PB[2 + i % 2]
            v.wait_ge(d_exp, 2 * t + 2 + CR)
            v.reciprocal(rinv[:, 0:2], rsum[:, 2 * i:2 * i + 2]).then_inc(d_step, 1)
            v.wait_ge(d_step, 2 * t + 1)
            v.tensor_scalar(rinv[:, 2:3], rinv[:, 1:2], lamt[:, 7:8], None, ALU.mult).then_inc(d_step, 1)
            v.wait_ge(d_turned, t + 1)
            v.tensor_scalar(pm[:, 0:w], PB[0][:, 0:w], rinv[:, 0:1], None, ALU.mult).then_inc(d_mix, 1)
            v.wait_ge(d_step, 2 * t + 2)
            v.wait_ge(d_mix, 2 * t + 1 + CR)
            v.scalar_tensor_tensor(pm[:, 0:w], PB[1][:, 0:w], rinv[:, 2:3], pm[:, 0:w], ALU.mult,
                                   ALU.add).then_inc(d_mix, 1)

        def diff_turn(pe, g, i):
            t = 4 * g + i
            pe.wait_ge(d_mix, 2 * t + 2 + CR)
            pe.wait_ge(d_pts, t + 1)
            for j in range(i + 1):
                mm = pe.transpose(PTP[i % 2][:, j * P:(j + 1) * P], PB[2 + i % 2][:, j * P:(j + 1) * P], ident)
            mm.then_inc(d_turned, 1)

        def diff_pts(act, g, i):
            t, w = 4 * g + i, P * (i + 1)
            act.wait_ge(d_turned, t + 1 + CR)
            act.wait_ge(d_pv, t + 1)
            act.activation(PTS[i % 2][:, 0:w], PTP[i % 2][:, 0:w], ACT.Copy).then_inc(d_pts, 1)

        def diff_pv(pe, g, i):
            t = 4 * g + i
            pe.wait_ge(d_pts, t + 1 + CR)
            if i == 0:
                pe.wait_ge(v_nat, FOX_G + g + 1)
                pe.wait_ge(on_ready, FOX_G + g + 1)
            for j in range(i + 1):
                mm = pe.matmul(OP[:, i * P:(i + 1) * P], PTS[i % 2][:, j * P:(j + 1) * P],
                               Vn[:, j * P:(j + 1) * P], start=(j == 0), stop=(j == i))
            mm.then_inc(d_pv, 1)

        def diff_group_pe(pe, g, last=False):
            G = FOX_G + g

            def chunks(s, c0, c1, early=None):
                if not last:
                    proj_chunks(pe, s, G + 1, c0, c1)
                elif early:
                    out_early(pe, 0, *early)
            chunks(0, 0, 1)
            for i in range(4):
                diff_scores(pe, g, i)
                if i == 1:
                    pe_v_turn(pe, G)
                if i < 3:
                    chunks(0, *((1, 3), (3, 5), (5, 8))[i], early=((0, 1), (1, 3), (3, 5))[i])
                else:
                    chunks(1, 0, 2, early=(5, 6))
                if i >= 1:
                    diff_turn(pe, g, i - 1)
                if i >= 2:
                    diff_pv(pe, g, i - 2)
            chunks(1, 2, 5, early=(6, 7))
            diff_turn(pe, g, 3)
            diff_pv(pe, g, 2)
            chunks(1, 5, 7)
            diff_pv(pe, g, 3)
            chunks(1, 7, 8)
            if not last:
                chunks(2, 0, 6)
                out_turn_pe(pe, G, on)
                chunks(2, 6, 8)

        def row_rms_act(act, g, scratch):
            for i in range(4):
                act.activation(scratch[:, i * P:(i + 1) * P], OP[:, i * P:(i + 1) * P], ACT.Square,
                               accum_out=dss[:, i:i + 1]).then_inc(d_sq, 1)
            act.wait_ge(d_ln, g + 1)
            act.activation(dn[:, 4:8], dn[:, 0:4], ACT.Ln).then_inc(d_act, 1)
            act.wait_ge(d_act, 2 * g + 1)
            act.activation(dn[:, 4:8], dn[:, 4:8], ACT.Exp, scale=-0.5).then_inc(d_act, 1)

        def row_mean_dve(v, g):
            v.wait_ge(d_sq, 4 * g + 4)
            v.tensor_scalar(dn[:, 0:4], dss, 1.0 / P, EPS, ALU.mult, ALU.add).then_inc(d_ln, 1)

        def row_rms_dve(v, g, on):
            v.wait_ge(d_act, 2 * g + 2)
            v.wait_ge(d_ln, g + 1)
            v.scalar_tensor_tensor(dn[:, 8:12], dn[:, 4:8], -0.5, dn[:, 4:8], ALU.mult, ALU.mult).then_inc(d_newton, 1)
            v.wait_ge(d_newton, 3 * g + 1)
            v.tensor_tensor(dn[:, 8:12], dn[:, 8:12], dn[:, 0:4], ALU.mult).then_inc(d_newton, 1)
            v.wait_ge(d_newton, 3 * g + 2)
            v.scalar_tensor_tensor(dn[:, 8:12], dn[:, 8:12], 1.5, dn[:, 4:8], ALU.add, ALU.mult).then_inc(d_newton, 1)
            v.wait_ge(d_newton, 3 * g + 3)
            v.tensor_tensor(on.rearrange("p (n d) -> p n d", d=P), OP[:].rearrange("p (n d) -> p n d", d=P),
                            dn[:, 8:12].unsqueeze(2).to_broadcast([P, 4, P]), ALU.mult).then_inc(on_ready, 1)

        def diff_group_act(act, g, last=False):
            G = FOX_G + g
            for i in range(4):
                diff_exp(act, g, i)
                if i == 1:
                    act_v_nat(act, G, d_pv, 4 * g + CR)
                    act_hi(act, 1, G + 1)
                if i >= 1:
                    diff_pts(act, g, i - 1)
            act_hi(act, 2, G + 1)
            diff_pts(act, g, 3)
            if not last:
                q_split_act(act, G + 1)
            act_table(act, ACT.Ln)
            act.wait_ge(d_pv, 4 * g + 4 + CR)
            row_rms_act(act, g, PB[0])
            if not last:
                act_hi(act, 0, G + 2)
                k_split_act(act, G + 1)
            act.wait_ge(o_turned, G + 1)
            act.activation(oh[:, G], S[0][:], ACT.Copy, scale=dscale).then_inc(oh_ready, 1)

        def diff_group_dve(v, g, last=False):
            G = FOX_G + g
            for i in range(4):
                diff_max(v, g, i)
                diff_mix(v, g, i)
                if i == 1:
                    dve_lo(v, 1, G + 1)
            if not last:
                dve_q(v, G + 1)
            dve_lo(v, 2, G + 1)
            row_mean_dve(v, g)
            if not last:
                dve_k(v, G + 1)
            row_rms_dve(v, g, on)
            if not last:
                dve_lo(v, 0, G + 2)
                k_split_dve(v, G + 1)
            v.wait_ge(oh_ready, G + 1)
            v.scalar_tensor_tensor(ol[:, G], S[0][:], dscale, oh[:, G].bitcast(F32), ALU.mult,
                                   ALU.subtract).then_inc(ol_ready, 1)
            if not last:
                dve_v(v, G + 1)

        d_newton = sem("d_newton")

        R0 = PH.get(("odd_in", 1), 0)
        KV = [work[:, 1], work[:, 2]]
        o_state, o_vT, o_Vn = work[:, 3], work[:, 3], work[:, 4]
        oP, oPT, o_on, o_kN = [work[:, 5], work[:, 6]], [work[:, 7], work[:, 8]], work[:, 9], work[:, 9]
        qr, fr, ir, gr = (work[:, 10 + i] for i in range(4))
        hq, sgate, hb, hk = (work[:, 14 + i] for i in range(4))
        dif, zz = [work[:, 18], work[:, 19]], [work[:, 20], work[:, 21]]
        qe, hVn = work[:, 22], work[:, 23]
        sigq = mean[:]
        LB = [S[1], PTP[1]]
        nsink, sinkx, sinke = tiny[:, 49:57], tiny[:, 57:65], tiny[:, 65:73]
        gmx, gd, ge = tiny[:, 73:77], tiny[:, 77:85], tiny[:, 85:93]
        gsum, grec, gsm, glb, goml, ebl = (tiny[:, 93:97], tiny[:, 97:101], tiny[:, 101:109], tiny[:, 109:113],
                                           tiny[:, 113:117], tiny[:, 117:121])
        s_scores, s_raw_max, s_max, s_exp, s_turned, s_pts, s_pv = (sem(n) for n in (
            "s_scores", "s_raw_max", "s_max", "s_exp", "s_turned", "s_pts", "s_pv"))
        s_sinkx, s_sinke, s_sum, s_rinv = sem("s_sinkx"), sem("s_sinke"), sem("s_sum"), sem("s_rinv")
        k_made, nsink_ready, sv_turned, sv_nat = sem("k_made"), sem("nsink_ready"), sem("sv_turned"), sem("sv_nat")
        lb_step, lb_exp = sem("lb_step"), sem("lb_exp")
        h_sigf, h_sigq, h_sigg, h_gate, h_f, h_k, h_q, h_lnf, h_b = (sem(n) for n in (
            "h_sigf", "h_sigq", "h_sigg", "h_gate", "h_f", "h_k", "h_q", "h_lnf", "h_b"))
        h_eb, h_qe, h_ebl, h_kexp, h_dif, h_e, h_z, h_zread = (sem(n) for n in (
            "h_eb", "h_qe", "h_ebl", "h_kexp", "h_dif", "h_e", "h_z", "h_zread"))
        h_takes = sem("h_takes")
        h_zhalf, h_sc, h_cp, h_vturned, h_vnat, h_kn, h_u, h_state, h_o, h_gated = (sem(n) for n in (
            "h_zhalf", "h_sc", "h_cp", "h_vturned", "h_vnat", "h_kn", "h_u", "h_state", "h_o", "h_gated"))

        def odd_chunks(pe, s, r, c0, c1):
            if c0 == 0:
                pe_unit_wait(pe, s, r)
            for c in range(c0, c1):
                mm = pe_chunk(pe, s, c, DC, xh, xl, acc[s][:])
            if c1 == DC:
                mm.then_inc(unit_done[s], 1)

        def span(n):
            return (0, P) if n // 2 == 0 else (P * (n // 2 - 1), 2 * P)

        def swa_scores(pe, p, n, kv):
            k, m, i = 8 * p + n, n % 2, n // 2
            pe.wait_ge(s_exp, k + 1)
            if n == 0:
                pe.wait_ge(acc_read[0], R0 + 2 * p + 1)
                pe.wait_ge(h_gated, p + 1)
            rows, (k0, w) = slice(HD * m, HD * m + HD), span(n)
            b = S[n % 2]
            pe.matmul(b[:, 0:w], work[rows, 0, i * P:(i + 1) * P], KV[kv][rows, k0:k0 + w],
                      start=True, stop=False)
            pe.matmul(b[:, 0:w], identb, cstb[:, C_SWA + 2 * P - w:C_SWA + 2 * P], start=False,
                      stop=True).then_inc(s_scores, 1)

        def swa_max(v, p, n):
            v.wait_ge(s_scores, 8 * p + n + 1)
            v.tensor_reduce(nmax[:, n:n + 1], S[n % 2][:, 0:span(n)[1]], AX, ALU.max, negate=True).then_inc(s_raw_max, 1)
            v.wait_ge(s_raw_max, 8 * p + n + 1)
            v.tensor_tensor(nmax[:, n:n + 1], nmax[:, n:n + 1], nsink[:, bass.ds(2 * p + n % 2, 1)],
                            ALU.min).then_inc(s_max, 1)

        def swa_exp(act, p, n):
            k, w = 8 * p + n, span(n)[1]
            act.wait_ge(s_max, k + 1)
            act.wait_ge(s_turned, k + 1)
            if n == 0:
                act.wait_ge(s_rinv, p + 1)
            act.activation(oP[n % 2][:, 0:w], S[n % 2][:, 0:w], ACT.Exp, bias=nmax[:, n:n + 1],
                           accum_out=rsum[:, n:n + 1]).then_inc(s_exp, 1)

        def swa_turn(pe, p, n):
            k = 8 * p + n
            pe.wait_ge(s_exp, k + 1 + CR)
            pe.wait_ge(s_pts, k + 1)
            if n == 0:
                pe.wait_ge(h_state, 3 * p + 1)
            if n == 1:
                pe.wait_ge(h_cp, 8 * p + CR)
            for j in range(span(n)[1] // P):
                mm = pe.transpose(PTP[n % 2][:, j * P:(j + 1) * P], oP[n % 2][:, j * P:(j + 1) * P], ident)
            mm.then_inc(s_turned, 1)

        def swa_pts(act, p, n):
            k, w = 8 * p + n, span(n)[1]
            act.wait_ge(s_turned, k + 1 + CR)
            act.wait_ge(s_pv, k + 1)
            act.activation(oPT[n % 2][:, 0:w], PTP[n % 2][:, 0:w], ACT.Copy).then_inc(s_pts, 1)

        def swa_pv(pe, p, n, kv):
            k, m, i = 8 * p + n, n % 2, n // 2
            k0, w = span(n)
            pe.wait_ge(s_pts, k + 1 + CR)
            if n == 0:
                pe.wait_ge(on_ready, 2 * p + GROUPS + 1)
            for j in range(w // P):
                mm = pe.matmul(OP[:, i * P + m * HD:i * P + m * HD + HD], oPT[n % 2][:, j * P:(j + 1) * P],
                               o_Vn[:, k0 + j * P + HD * kv:k0 + j * P + HD * kv + HD],
                               start=(j == 0), stop=(j == w // P - 1))
            mm.then_inc(s_pv, 1)

        def piece(a, L):
            return a.rearrange("p (n h m) -> p n h m", h=2, m=64 >> L)

        def head_sigmoids_act(act, h):
            act.wait_ge(acc_read[1], R0 + 2 * h + 1)
            act.activation(fr, fr, ACT.Sigmoid).then_inc(h_sigf, 1)
            act.wait_ge(acc_read[2], Q0 + 2 + h + 1)
            act.activation(sigq, qr, ACT.Sigmoid).then_inc(h_sigq, 1)
            act.wait_ge(acc_read[0], R0 + 2 * h + 2)
            act.activation(gr, gr, ACT.Sigmoid).then_inc(h_sigg, 1)

        def head_f_dve(v, h):
            v.wait_ge(h_sigf, h + 1)
            v.tensor_scalar(fr, fr, goml[:, bass.ds(h, 1)], glb[:, bass.ds(h, 1)], ALU.mult, ALU.add).then_inc(h_f, 1)

        def head_ln_act(act, h):
            act.wait_ge(h_f, h + 1)
            act.activation(newton[:], fr, ACT.Ln).then_inc(h_lnf, 1)

        def head_q_dve(v, h):
            v.wait_ge(h_sigq, h + 1)
            v.tensor_tensor(hq, qr, sigq, ALU.mult).then_inc(h_q, 1)

        def head_gate_dve(v, h):
            v.wait_ge(h_sigg, h + 1)
            v.wait_ge(h_gated, h + 1)
            v.tensor_copy(sgate, gr).then_inc(h_gate, 1)

        def head_k_dve(v, p):
            v.wait_ge(h_f, p + 1)
            v.tensor_scalar(hk, fr, -1.0, 1.0, ALU.mult, ALU.add).then_inc(h_k, 1)

        def head_scan_dve(v, p):
            v.wait_ge(h_lnf, p + 1)
            v.tensor_tensor_scan(hb, not_first[:], newton[:], 0.0, ALU.mult, ALU.add).then_inc(h_b, 1)

        def head_decays_act(act, p):
            act.wait_ge(h_b, p + 1)
            act.wait_ge(h_o, p + 1)
            act.activation(qe, hb, ACT.Exp).then_inc(h_eb, 1)
            act.activation(ebl, hb[:, P - 1::P], ACT.Exp).then_inc(h_ebl, 1)
            act.wait_ge(h_z, 8 * p + 1)
            for i in range(TB):
                act.activation(dif[1][:, i * P:(i + 1) * P], hb[:, i * P:(i + 1) * P], ACT.Exp, scale=-1.0,
                               bias=hb[:, (i + 1) * P - 1:(i + 1) * P]).then_inc(h_kexp, 1)

        def head_kdec_pool(g, p):
            g.wait_ge(h_kexp, TB * p + TB)
            g.wait_ge(h_zread, 8 * p + 1)
            g.tensor_tensor(zz[1], hk, dif[1], ALU.mult).then_inc(h_z, 1)

        def level_dif_dve(v, p, L):
            b, o = piece(hb, L), piece(dif[L % 2], L)
            n, m = SEQ // (128 >> L), 64 >> L
            ref = b[:, :, 0, m - 1:m].to_broadcast([P, n, m])
            v.wait_ge(h_z, 8 * p + L + 2)
            v.wait_ge(h_b, p + 1)
            v.tensor_tensor(o[:, :, 0], ref, b[:, :, 0], ALU.subtract).then_inc(h_dif, 1)
            v.tensor_tensor(o[:, :, 1], b[:, :, 1], ref, ALU.subtract).then_inc(h_dif, 1)

        def level_exp_act(act, p, L):
            act.wait_ge(h_dif, 14 * p + 2 * L + 2)
            act.activation(dif[L % 2], dif[L % 2], ACT.Exp).then_inc(h_e, 1)

        def level_z_pool(g, p, L):
            e, o = piece(dif[L % 2], L), piece(zz[L % 2], L)
            g.wait_ge(h_e, 7 * p + L + 1)
            g.wait_ge(h_q, p + 1)
            g.wait_ge(h_zread, 8 * p + L + 2)
            g.tensor_tensor(o[:, :, 0], piece(hk, L)[:, :, 0], e[:, :, 0], ALU.mult).then_inc(h_zhalf, 1)
            g.wait_ge(h_zhalf, 7 * p + L + 1)
            g.tensor_tensor(o[:, :, 1], piece(hq, L)[:, :, 1], e[:, :, 1], ALU.mult).then_inc(h_z, 1)

        def level_scores_pe(pe, p, L):
            pe.wait_ge(h_cp, 8 * p + L + 1)
            if L < NLEV - 1:
                pe.wait_ge(h_z, 8 * p + L + 2 + CR)
                a = c = zz[L % 2]
            else:
                pe.wait_ge(h_k, p + 1)
                pe.wait_ge(h_q, p + 1)
                a, c = hk, hq
            for i in range(TB):
                mm = pe.matmul(LB[L % 2][:, i * P:(i + 1) * P], a[:, i * P:(i + 1) * P], c[:, i * P:(i + 1) * P],
                               start=True, stop=True)
            mm.then_inc(h_sc if L == NLEV - 1 else h_zread, 1)

        def level_take_dve(v, p, L):
            if L < NLEV - 1:
                v.wait_ge(h_zread, 8 * p + L + 2 + CR)
            else:
                v.wait_ge(h_sc, p + 1)
            if L == 0:
                v.wait_ge(h_o, p + 1)
            else:
                v.wait_ge(h_cp, 8 * p + L + CR)
            v.sem_inc(h_takes, 1)
            v.copy_predicated(score_acc[:].rearrange("p (n t) -> p n t", t=P),
                              level_mask[:, L * P:(L + 1) * P].unsqueeze(1).to_broadcast([P, TB, P]),
                              LB[L % 2][:].rearrange("p (n t) -> p n t", t=P)).then_inc(h_cp, 1)

        def head_turns_pe(pe, p):
            pe.wait_ge(acc_read[1], R0 + 2 * p + 2)
            pe.wait_ge(s_pts, 8 * p + 8 + CR)
            for i in range(TB):
                mm = pe.transpose(PTP[0][:, i * P:(i + 1) * P], ir[:, i * P:(i + 1) * P], ident)
            mm.then_inc(h_vturned, 1)
            pe.wait_ge(h_z, 8 * p + 1 + CR)
            for i in range(TB):
                mm = pe.transpose(PTP[1][:, i * P:(i + 1) * P], zz[1][:, i * P:(i + 1) * P], ident)
            mm.then_inc(h_zread, 1)

        def head_state_pe(pe, p):
            pe.wait_ge(h_vnat, p + 1)
            pe.wait_ge(h_kn, p + 1)
            for i in range(TB - 1):
                mm = pe.matmul(PTP[0][:, i * P:(i + 1) * P], o_kN[:, i * P:(i + 1) * P], hVn[:, i * P:(i + 1) * P],
                               start=True, stop=True)
            mm.then_inc(h_u, 1)

        def head_state_dve(v, p):
            v.wait_ge(h_u, p + 1)
            v.wait_ge(h_ebl, p + 1)
            v.wait_ge(h_o, p + 1)
            v.tensor_copy(o_state[:, 0:P], PTP[0][:, 0:P]).then_inc(h_state, 1)
            for i in range(1, TB - 1):
                v.wait_ge(h_state, 3 * p + i + 1)
                v.scalar_tensor_tensor(o_state[:, i * P:(i + 1) * P], o_state[:, (i - 1) * P:i * P], ebl[:, i:i + 1],
                                       PTP[0][:, i * P:(i + 1) * P], ALU.mult, ALU.add).then_inc(h_state, 1)

        def head_out_pe(pe, p):
            pe.wait_ge(h_cp, 8 * p + 8 + CR)
            pe.wait_ge(h_state, 3 * p + 4)
            pe.wait_ge(h_qe, p + 1)
            pe.wait_ge(on_ready, 2 * p + GROUPS + 2)
            for i in range(TB):
                t = slice(i * P, (i + 1) * P)
                if i:
                    pe.matmul(OP[:, t], qe[:, t], o_state[:, (i - 1) * P:i * P], start=True, stop=False)
                mm = pe.matmul(OP[:, t], score_acc[:, t], hVn[:, t], start=(i == 0), stop=True)
            mm.then_inc(h_o, 1)

        def body_pe(pe, p, kv, last=False):
            def chunks(s, r, c0, c1, early=None):
                if not last:
                    odd_chunks(pe, s, r, c0, c1)
                elif early:
                    out_early(pe, 1, *early)
            rq, ri, rf = R0 + 2 + 2 * p, R0 + 2 + 2 * p, Q0 + 3 + p
            for n in range(8):
                if n == 0:
                    chunks(0, rq, 0, 1, early=(0, 1))
                swa_scores(pe, p, n, kv)
                if n == 1:
                    chunks(0, rq, 2, 4, early=(1, 2))
                elif n < 6:
                    chunks(0, rq, *((1, 2), (), (4, 5), (5, 6), (6, 7), (7, 8))[n])
                else:
                    chunks(1, ri, n - 6, n - 5)
                if n >= 1:
                    swa_turn(pe, p, n - 1)
                if n >= 2:
                    swa_pv(pe, p, n - 2, kv)
            chunks(1, ri, 2, 3)
            swa_turn(pe, p, 7)
            swa_pv(pe, p, 6, kv)
            chunks(1, ri, 3, 5)
            swa_pv(pe, p, 7, kv)
            head_turns_pe(pe, p)
            chunks(1, ri, 5, 8)
            out_turn_pe(pe, GROUPS + 2 * p, o_on)
            chunks(2, rf, 0, 2, early=(2, 3))
            head_state_pe(pe, p)
            plan = [(2, rf, 2, 4), (2, rf, 4, 6), (2, rf, 6, 8), (0, rq + 1, 0, 3), (0, rq + 1, 3, 6), (0, rq + 1, 6, 8),
                    (1, ri + 1, 0, 1), (1, ri + 1, 1, 2)]
            for L in range(NLEV):
                level_scores_pe(pe, p, L)
                if last and L == 2:
                    pe.wait_ge(ol_ready, GROUPS + 2 * p + 2)
                chunks(*plan[L], early=(L + 1, L + 2) if 2 <= L <= 5 else None)
            head_out_pe(pe, p)
            chunks(1, ri + 1, 2, 8)
            if not last:
                out_turn_pe(pe, GROUPS + 2 * p + 1, o_on)

        def body_act(act, p, last=False):
            def hi(s, r):
                if not last:
                    act_hi(act, s, r)
            rq, ri, rf = R0 + 2 + 2 * p, R0 + 2 + 2 * p, Q0 + 3 + p
            swa_exp(act, p, 0)
            act_hi(act, 1, ri)
            swa_exp(act, p, 1)
            swa_pts(act, p, 0)
            for n in range(2, 8):
                swa_exp(act, p, n)
                swa_pts(act, p, n - 1)
                if n == 3:
                    head_decays_act(act, p)
            level_exp_act(act, p, 0)
            swa_pts(act, p, 7)
            act.wait_ge(s_sinkx, p + 1)
            act.activation(sinke, sinkx, ACT.Exp).then_inc(s_sinke, 1)
            act_hi(act, 2, rf)
            act.wait_ge(h_vturned, p + 1)
            act.activation(hVn, PTP[0][:], ACT.Copy).then_inc(h_vnat, 1)
            act.wait_ge(o_turned, GROUPS + 2 * p + 1)
            act.activation(oh[:, p], S[0][:], ACT.Copy).then_inc(oh_ready, 1)
            act.wait_ge(h_zread, 8 * p + 1 + CR)
            act.activation(o_kN, PTP[1][:], ACT.Copy).then_inc(h_kn, 1)
            for L in range(1, NLEV - 1):
                level_exp_act(act, p, L)
                if L == 1:
                    hi(0, rq + 1)
                if L == 4:
                    hi(1, ri + 1)
            if not last:
                head_sigmoids_act(act, p + 1)
                head_ln_act(act, p + 1)
                hi(0, rq + 2)
            else:
                act_table(act, ACT.Ln)
            act.wait_ge(h_o, p + 2)
            row_rms_act(act, DIFF_G + p, oPT[0])
            act.wait_ge(h_gated, p + 2)
            act.activation(oh[:, p + 4], oPT[1], ACT.Copy).then_inc(oh_ready, 1)

        def body_dve(v, p, last=False):
            def lo(s, r):
                if not last:
                    dve_lo(v, s, r)

            def take(dst, s, r, scale=None, waits=()):
                if last:
                    return
                v.wait_ge(unit_done[s], r + 1)
                for w in waits:
                    v.wait_ge(*w)
                if scale is None:
                    v.tensor_tensor(dst, acc[s][:], rstd[:], ALU.mult).then_inc(acc_read[s], 1)
                else:
                    v.scalar_tensor_tensor(dst, acc[s][:], scale, rstd[:], ALU.mult, ALU.mult).then_inc(acc_read[s], 1)
            rq, ri, rf = R0 + 2 + 2 * p, R0 + 2 + 2 * p, Q0 + 3 + p
            swa_max(v, p, 0)
            swa_max(v, p, 1)
            head_k_dve(v, p)
            head_scan_dve(v, p)
            dve_lo(v, 1, ri)
            for n in range(2, 8):
                swa_max(v, p, n)
                if n == 5:
                    level_dif_dve(v, p, 0)
            v.wait_ge(s_max, 8 * p + 8)
            v.tensor_tensor(sinkx.rearrange("p (i m) -> p i m", m=2), nmax.rearrange("p (i m) -> p i m", m=2),
                            sm[:, bass.ds(SINK + 2 * p, 2)].unsqueeze(1).to_broadcast([P, 4, 2]), ALU.add).then_inc(s_sinkx, 1)
            take(work[:, 0], 0, rq, QSCALE)
            v.wait_ge(h_eb, p + 1)
            v.wait_ge(h_q, p + 1)
            v.tensor_tensor(qe, qe, hq, ALU.mult).then_inc(h_qe, 1)
            v.wait_ge(s_sinke, p + 1)
            v.wait_ge(s_exp, 8 * p + 8 + CR)
            v.tensor_tensor(rsum, rsum, sinke, ALU.add).then_inc(s_sum, 1)
            v.wait_ge(s_sum, p + 1)
            v.reciprocal(rinv, rsum).then_inc(s_rinv, 1)
            v.wait_ge(s_pv, 8 * p + 8 + CR)
            v.wait_ge(s_rinv, p + 2)
            v.wait_ge(o_turned, GROUPS + 2 * p)
            v.tensor_tensor(o_on.rearrange("p (n d) -> p n d", d=HD), OP[:].rearrange("p (n d) -> p n d", d=HD),
                            rinv.unsqueeze(2).to_broadcast([P, 8, HD]), ALU.mult).then_inc(on_ready, 1)
            dve_lo(v, 2, rf)
            level_dif_dve(v, p, 1)
            take(fr, 1, ri)
            v.wait_ge(oh_ready, GROUPS + 2 * p + 1)
            v.tensor_tensor(ol[:, p], S[0][:], oh[:, p].bitcast(F32), ALU.subtract).then_inc(ol_ready, 1)
            head_state_dve(v, p)
            for L in range(NLEV):
                if L + 2 < NLEV - 1:
                    level_dif_dve(v, p, L + 2)
                level_take_dve(v, p, L)
                if L == 1:
                    lo(0, rq + 1)
                if L == 2:
                    take(qr, 2, rf)
                if L == 4:
                    lo(1, ri + 1)
                if L == 5:
                    take(gr, 0, rq + 1)
            if not last:
                head_f_dve(v, p + 1)
                head_q_dve(v, p + 1)
            lo(0, rq + 2)
            row_mean_dve(v, DIFF_G + p)
            row_rms_dve(v, DIFF_G + p, o_on)
            v.wait_ge(o_turned, GROUPS + 2 * p + 2)
            v.wait_ge(h_gate, p + 1)
            v.scalar_tensor_tensor(oPT[1], S[0][:], sm[:, HGRNN:HGRNN + 1], sgate, ALU.mult, ALU.mult).then_inc(h_gated, 1)
            if not last:
                head_gate_dve(v, p + 1)
            take(ir, 1, ri + 1, waits=[(h_vturned, p + 1)])
            v.wait_ge(oh_ready, GROUPS + 2 * p + 2)
            v.wait_ge(h_gated, p + 2)
            v.tensor_tensor(ol[:, p + 4], oPT[1], oh[:, p + 4].bitcast(F32), ALU.subtract).then_inc(ol_ready, 1)

        def body_pool(g, p):
            head_kdec_pool(g, p)
            for L in range(NLEV - 1):
                level_z_pool(g, p, L)

        ODD_FIRST = ((2, Q0), (0, R0), (2, Q0 + 1), (1, R0), (2, Q0 + 2), (0, R0 + 1), (1, R0 + 1))

        def odd_pe(pe, l):
            for n, (s, r) in enumerate(ODD_FIRST):
                if n == 0:
                    pe_unit_first(pe, s, r, 2 * l)
                else:
                    pe_unit(pe, s, r, DC, xh, xl)
                if n == 3:
                    pe.wait_ge(acc_read[2], Q0 + 2)
                    for i in range(TB):
                        mm = pe.transpose(PTP[0][:, i * P:(i + 1) * P], o_vT[:, i * P:(i + 1) * P], ident)
                    mm.then_inc(sv_turned, 1)
            pe.wait_ge(sv_nat, 1)
            with pe.Fori(0, 2) as p:
                body_pe(pe, p, 0)
            body_pe(pe, 2, 1)
            body_pe(pe, 3, 1, last=True)

        def odd_act(act, l):
            for n, (s, r) in enumerate(ODD_FIRST):
                if n >= 2:
                    act_hi(act, s, r)
                if n == 4:
                    act.wait_ge(sv_turned, 1)
                    act.activation(o_Vn, PTP[0][:], ACT.Copy).then_inc(sv_nat, 1)
            act.wait_ge(lb_step, 3)
            act.activation(ge, gd, ACT.Exp).then_inc(lb_exp, 1)
            head_sigmoids_act(act, 0)
            head_ln_act(act, 0)
            act_hi(act, 0, R0 + 2)
            act_table(act, ACT.Exp)
            with act.Fori(0, 3) as p:
                body_act(act, p)
            body_act(act, 3, last=True)

        def odd_dve(v, l):
            def take(dst, s, r, scale=None):
                v.wait_ge(unit_done[s], r + 1)
                if scale is None:
                    v.tensor_tensor(dst, acc[s][:], rstd[:], ALU.mult).then_inc(acc_read[s], 1)
                else:
                    v.scalar_tensor_tensor(dst, acc[s][:], scale, rstd[:], ALU.mult, ALU.mult).then_inc(acc_read[s], 1)
            v.tensor_scalar(nsink, sm[:, SINK:SINK + 8], -1.0, None, ALU.mult).then_inc(nsink_ready, 1)
            g0, g1 = sm[:, GAM:GAM + 4], sm[:, GAM + 4:GAM + 8]
            v.tensor_tensor(gmx, g0, g1, ALU.max).then_inc(lb_step, 1)
            v.wait_ge(lb_step, 1)
            v.tensor_tensor(gd[:, 0:4], g0, gmx, ALU.subtract).then_inc(lb_step, 1)
            v.tensor_tensor(gd[:, 4:8], g1, gmx, ALU.subtract).then_inc(lb_step, 1)
            v.wait_ge(unit_done[2], Q0 + 1)
            for n, (h, half) in enumerate(((0, 0), (0, 1), (1, 0), (1, 1))):
                src, dst = slice(HD * h, HD * h + HD), slice(HD * half, HD * half + HD)
                v.tensor_tensor(KV[h][dst, :], acc[2][src, :], rstd[src, :], ALU.mult).then_inc(
                    acc_read[2] if n == 3 else k_made, 1)
            dve_lo(v, 2, Q0 + 1)
            take(work[:, 0], 0, R0, QSCALE)
            dve_lo(v, 1, R0)
            take(o_vT, 2, Q0 + 1)
            dve_lo(v, 2, Q0 + 2)
            take(fr, 1, R0)
            dve_lo(v, 0, R0 + 1)
            take(qr, 2, Q0 + 2)
            dve_lo(v, 1, R0 + 1)
            v.wait_ge(lb_exp, 1)
            v.tensor_tensor(gsum, ge[:, 0:4], ge[:, 4:8], ALU.add).then_inc(lb_step, 1)
            v.wait_ge(lb_step, 4)
            v.reciprocal(grec, gsum).then_inc(lb_step, 1)
            v.wait_ge(lb_step, 5)
            v.tensor_tensor(gsm[:, 0:4], ge[:, 0:4], grec, ALU.mult).then_inc(lb_step, 1)
            v.tensor_tensor(gsm[:, 4:8], ge[:, 4:8], grec, ALU.mult).then_inc(lb_step, 1)
            v.wait_ge(lb_step, 7)
            v.tensor_tensor(glb, gsm[:, 0:4], gsm[:, 4:8], ALU.add).then_inc(lb_step, 1)
            v.wait_ge(lb_step, 8)
            v.tensor_tensor(glb, glb, gsm[:, 0:4], ALU.subtract).then_inc(lb_step, 1)
            v.wait_ge(lb_step, 9)
            v.tensor_scalar(goml, glb, -1.0, 1.0, ALU.mult, ALU.add).then_inc(lb_step, 1)
            v.wait_ge(lb_step, 10)
            v.wait_ge(nsink_ready, 1)
            v.wait_ge(ones_ready, 4)
            take(gr, 0, R0 + 1)
            head_f_dve(v, 0)
            dve_lo(v, 0, R0 + 2)
            head_q_dve(v, 0)
            head_gate_dve(v, 0)
            take(ir, 1, R0 + 1)
            with v.Fori(0, 3) as p:
                body_dve(v, p)
            body_dve(v, 3, last=True)

        def odd_pool(g, l):
            with g.Fori(0, 4) as p:
                body_pool(g, p)

        gs, us, sg, gg = (work[:, i] for i in range(4))
        silu_ready, g_ready, gh_ready, gl_ready = sem("silu_ready"), sem("g_ready"), sem("gh_ready"), sem("gl_ready")
        YD = 5
        xg = [work[:, 4 + i] for i in range(DC - YD)]
        out_sent, y_out, xg_ready, yg_out = sem("out_sent"), sem("y_out"), sem("xg_ready"), sem("yg_out")

        def F_act(act):
            for l in range(layers):
                if l % 2:
                    odd_act(act, l)
                k = 2 * l + 1
                for j, (s, r) in enumerate(out_units(l)):
                    if j < DC - 1:
                        act_hi(act, s, r + 1)
                    else:
                        act_table(act, ACT.Ln)
                        act_last_square(act, s, r)
                    act_xh(act, j, LN_FFN + DC * l + j, (acc_read[s], r + 1))
                act_rsqrt(act, k)
                for half in range(2):
                    r0 = PH["gu", l, half]
                    n0 = FT * l + FH * half
                    act_table(act, ACT.Silu)
                    with act.Fori(0, FH - 1) as i:
                        gu_silu_act(act, r0 + i)
                        act_hi(act, 0, r0 + i + 1)
                        act_hi(act, 1, r0 + i + 1)
                        gu_gh_act(act, i, n0 + i)
                    rd = PH["dn", l, half]
                    gu_silu_act(act, r0 + FH - 1)
                    act_hi(act, 0, rd, FH * P)
                    act_hi(act, 1, rd, FH * P)
                    gu_gh_act(act, FH - 1, n0 + FH - 1)
                    if half == 0 or l == layers - 1:
                        with act.Fori(0, 3) as i:
                            act_hi(act, 0, rd + i + 1, FH * P)
                            act_hi(act, 1, rd + i + 1, FH * P)
                    if half == 0:
                        act_hi(act, 0, rd + 4)
                        act_hi(act, 1, rd + 4)
                    elif l == layers - 1:
                        act_table(act, ACT.Ln)
                        for j, (s, r) in ((5, (1, rd + 2)), (6, (0, rd + 3)), (7, (1, rd + 3))):
                            if j == 7:
                                act_last_square(act, s, r)
                            act.wait_ge(acc_read[s], r + 1)
                            act.activation(xg[j - YD], x[:, j], ACT.Copy,
                                           scale=sm[:, LN_FIN + j:LN_FIN + j + 1]).then_inc(xg_ready, 1)
                        act_rsqrt(act, 2 * layers)
                    else:
                        gcol = LN_MIX + DC * (l + 1)
                        out_pairs_act(act, rd, FH * P, gcol)
                        act_hi(act, 2, Q0)
                        act_table(act, ACT.Ln)
                        act_last_square(act, 1, rd + 3)
                        act_xh(act, 7, gcol + 7, (acc_read[1], rd + 4))
                        act_hi(act, 0, R0)
                        act_rsqrt(act, 2 * l + 2)

        def out_pairs_act(act, r, n, gcol):
            with act.Fori(0, 3) as i:
                act_hi(act, 0, r + i + 1, n)
                act_xh(act, 2 * i, gcol + 2 * i, (acc_read[0], r + i + 1))
                act_hi(act, 1, r + i + 1, n)
                act_xh(act, 2 * i + 1, gcol + 2 * i + 1, (acc_read[1], r + i + 1))
            act_xh(act, 6, gcol + 6, (acc_read[0], r + 4))

        def gu_silu_act(act, r):
            act.wait_ge(acc_read[0], r + 1)
            act.activation(sg, gs, ACT.Silu).then_inc(silu_ready, 1)

        def gu_gh_act(act, t, n):
            act.wait_ge(g_ready, n + 1)
            act.activation(gh[:, t], gg, ACT.Copy).then_inc(gh_ready, 1)

        def x_add(v, s, j, r):
            v.wait_ge(unit_done[s], r + 1)
            v.tensor_tensor(x[:, j], acc[s][:], x[:, j], ALU.add).then_inc(acc_read[s], 1)

        def x_tile_split(v, s, j, r, gcol, n):
            x_add(v, s, j, r)
            v.wait_ge(acc_read[s], r + 1)
            dve_xl(v, j, gcol + j, n)

        def gate_up_dve(v, t, r, n, width):
            v.wait_ge(unit_done[0], r + 1)
            v.tensor_tensor(gs, acc[0][:], rstd[:], ALU.mult).then_inc(acc_read[0], 1)
            dve_lo(v, 0, r + 1, width)
            v.wait_ge(unit_done[1], r + 1)
            v.tensor_tensor(us, acc[1][:], rstd[:], ALU.mult).then_inc(acc_read[1], 1)
            v.wait_ge(silu_ready, n + 1)
            v.wait_ge(acc_read[1], r + 1)
            v.tensor_tensor(gg, sg, us, ALU.mult).then_inc(g_ready, 1)
            dve_lo(v, 1, r + 1, width)
            v.wait_ge(gh_ready, n + 1)
            v.wait_ge(g_ready, n + 1)
            v.tensor_tensor(gl[:, t], gg, gh[:, t].bitcast(F32), ALU.subtract).then_inc(gl_ready, 1)

        def out_pairs_dve(v, r, n, gcol, k):
            with v.Fori(0, 3) as i:
                for s in range(2):
                    x_add(v, s, 2 * i + s, r + i)
                    dve_lo(v, s, r + i + 1, n)
                    v.wait_ge(acc_read[s], r + i + 1)
                    dve_xl(v, 2 * i + s, gcol + 2 * i + s, DC * k + 2 * i + s)
            x_tile_split(v, 0, 6, r + 3, gcol, DC * k + 6)

        def F_dve(v):
            for l in range(layers):
                if l % 2:
                    odd_dve(v, l)
                k = 2 * l + 1
                gcol = LN_FFN + DC * l
                for j, (s, r) in enumerate(out_units(l)):
                    x_add(v, s, j, r)
                    if j < DC - 1:
                        dve_lo(v, s, r + 1)
                    v.wait_ge(acc_read[s], r + 1)
                    dve_xl(v, j, gcol + j, DC * k + j)
                dve_mean(v, k)
                dve_newton(v, k)
                v.wait_ge(rstd_ready, k + 1)
                for half in range(2):
                    r0 = PH["gu", l, half]
                    n0 = FT * l + FH * half
                    with v.Fori(0, FH - 1) as i:
                        gate_up_dve(v, i, r0 + i, n0 + i, UNIT8)
                    gate_up_dve(v, FH - 1, r0 + FH - 1, n0 + FH - 1, FH * P)
                    rd = PH["dn", l, half]
                    if half == 0 or l == layers - 1:
                        with v.Fori(0, 3) as i:
                            x_add(v, 0, 2 * i, rd + i)
                            dve_lo(v, 0, rd + i + 1, FH * P)
                            x_add(v, 1, 2 * i + 1, rd + i)
                            dve_lo(v, 1, rd + i + 1, FH * P)
                        x_add(v, 0, 6, rd + 3)
                        if half == 0:
                            dve_lo(v, 0, rd + 4)
                        x_add(v, 1, 7, rd + 3)
                        if half == 0:
                            dve_lo(v, 1, rd + 4)
                    else:
                        gcol = LN_MIX + DC * (l + 1)
                        kn = 2 * l + 2
                        out_pairs_dve(v, rd, FH * P, gcol, kn)
                        dve_lo(v, 2, Q0)
                        x_tile_split(v, 1, 7, rd + 3, gcol, DC * kn + 7)
                        dve_lo(v, 0, R0)
                        dve_mean(v, kn)
                        dve_newton(v, kn)
                        v.wait_ge(rstd_ready, kn + 1)

        def F_pe(pe):
            for l in range(layers):
                if l % 2:
                    odd_pe(pe, l)
                k = 2 * l + 1
                heads = DC * (l + 1)
                units = out_units(l)
                pe.wait_ge(ol_ready, heads)
                pe_unit_wait(pe, *units[1])
                pe_chunks(pe, 1, 0, DC - 1, DC, oh, ol)
                out_turn_pe(pe, heads - 1, o_on if l % 2 else on)
                pe_unit_wait(pe, *units[2])
                pe_chunks(pe, 2, 0, 3, DC, oh, ol)
                pe.wait_ge(ol_ready, heads + 1)
                pe_chunks(pe, 0, DC - 1, DC, DC, oh, ol)
                pe_chunks(pe, 1, DC - 1, DC, DC, oh, ol)
                pe_chunks(pe, 2, 3, DC, DC, oh, ol)
                for s, r in units[3:]:
                    pe_unit(pe, s, r, DC, oh, ol)
                for half in range(2):
                    r0 = PH["gu", l, half]
                    n0 = FT * l + FH * half
                    if half == 0:
                        pe_unit_first(pe, 0, r0, k)
                    else:
                        pe_unit(pe, 0, r0, DC, xh, xl)
                    pe_unit(pe, 1, r0, DC, xh, xl)
                    with pe.Fori(1, FH) as i:
                        for s in range(2):
                            pe_unit(pe, s, r0 + i, DC, xh, xl)
                    r0 = PH["dn", l, half]
                    pe.wait_ge(gl_ready, n0 + FH - 1)
                    pe_unit_wait(pe, 0, r0)
                    pe_chunks(pe, 0, 0, FH - 1, FH, gh, gl)
                    pe.wait_ge(gl_ready, n0 + FH)
                    pe_chunks(pe, 0, FH - 1, FH, FH, gh, gl)
                    pe_unit(pe, 1, r0, FH, gh, gl)
                    with pe.Fori(1, 4) as i:
                        for s in range(2):
                            pe_unit(pe, s, r0 + i, FH, gh, gl)
            pe_stat(pe, 2 * layers)

        def F_sp(sp):
            for l in range(layers):
                if l % 2:
                    r0 = PH["odd_in", l]
                    for n, (s, r) in enumerate(ODD_FIRST):
                        sp_load(sp, s, r, w_odd[n], UNIT8)
                    with sp.Fori(0, 3) as p:
                        for n, (s, r) in enumerate(((0, r0 + 2 + 2 * p), (1, r0 + 2 + 2 * p), (2, Q0 + 3 + p),
                                                    (0, r0 + 3 + 2 * p), (1, r0 + 3 + 2 * p))):
                            sp_load(sp, s, r, w_odd[7 + 5 * p + n], UNIT8)
                r0 = PH["mix_out", l]
                w = w_out_o if l % 2 else w_out_e
                for j, (s, r) in enumerate(out_units(l)):
                    sp_load(sp, s, r, w[j], UNIT8)
                for half in range(2):
                    r0 = PH["gu", l, half]
                    with sp.Fori(0, FH) as i:
                        for s in range(2):
                            sp_load(sp, s, r0 + i, w_gu[l, FH * half + i, s], UNIT8)
                    r0 = PH["dn", l, half]
                    with sp.Fori(0, 4) as i:
                        for s in range(2):
                            sp_load(sp, s, r0 + i, w_dn[l, half, 2 * i + s], FH * P)

        def F_pool(g):
            for l in range(layers):
                if l % 2:
                    odd_pool(g, l)
                k = 2 * l + 1
                pool_zero(g, k)
                for j, (s, r) in enumerate(out_units(l)[:-1]):
                    square_tile(g, s, j, r, (DC - 1) * k + j)
                k, r0 = k + 1, PH["dn", l, 1]
                pool_zero(g, k)
                with g.Fori(0, 3) as i:
                    for s in range(2):
                        square_tile(g, s, 2 * i + s, r0 + i, (DC - 1) * k + 2 * i + s)
                square_tile(g, 0, 6, r0 + 3, (DC - 1) * k + 6)

        @block.sync
        def _(sp):
            sp.dma_start(sm[:], small).then_inc(small_in, 16)
            sp.dma_start(fa_raw[:], w_fa).then_inc(fa_in, 16)
            sp.dma_start(x[:, 0:2], xT[:, 0:2]).then_inc(x_in[0], 16)
            sp_load(sp, 0, 0, w_even[0], UNIT8)
            for j in range(1, DC // 2):
                sp.dma_start(x[:, 2 * j:2 * j + 2], xT[:, 2 * j:2 * j + 2]).then_inc(x_in[j], 16)
            sp_load(sp, 1, 0, w_even[1], UNIT8)
            sp_load(sp, 2, 0, w_even[2], UNIT8)
            sp.dma_start(const_stage[:, 0:NCONST], const).then_inc(const_in, 16)
            sp.dma_start(ident, const[:, C_ID:C_ID + P]).then_inc(const_in, 16)
            for s in range(3):
                sp_load(sp, s, 1, w_even[3 + s], UNIT8)
            sp.wait_ge(cq_ones, 1)
            for a, (part, minus) in enumerate(((cpart[:, 0], cpartn[0][:, 0]), (cpart[:, 1], cpartn[0][:, 1]),
                                               (cpart2[:, 0], cpartn[1][:, 0]))):
                sp.wait_ge(gate_step, (5, 8, 10)[a])
                sp.dma_start(CQ[a:a + 1], part).then_inc(cq_in, 16)
                sp.wait_ge(gate_step, (6, 9, 11)[a])
                sp.dma_start(CK[3 + a:4 + a], minus).then_inc(cq_in, 16)
            with sp.Fori(2, GROUPS) as G:
                for s in range(3):
                    sp_load(sp, s, G, w_even[3 * G + s], UNIT8)
            F_sp(sp)
            for j in (0, 1, 5, 2, 3, 6, 4, 7):
                if j < YD:
                    sp.wait_ge(y_out, j + 1)
                    sp.dma_start(out[:, j], x[:, j]).then_inc(out_sent, 16)
                else:
                    sp.wait_ge(yg_out, j - YD + 1)
                    sp.dma_start(out[:, j], xg[j - YD]).then_inc(out_sent, 16)
            sp.wait_ge(out_sent, 16 * DC)

        @block.gpsimd
        def _(g):
            g.memset(ones[:], 1.0).then_inc(ones_ready, 1)
            g.memset(meanw[:], 1.0 / D).then_inc(ones_ready, 1)
            g.memset(eps, EPS).then_inc(ones_ready, 1)
            for j in range(0, DC, 2):
                g.wait_ge(x_in[j // 2], 16)
                g.tensor_tensor(x_square(j), x[:, j], x[:, j], ALU.mult).then_inc(x_sq[0], 1)
            g.memset(score_acc[:], 0.0).then_inc(ones_ready, 1)
            g.memset(work[0:6, 11:19].bitcast(BF16), 1.0).then_inc(cq_ones, 1)
            g.sem_inc(sq_ready, DC - 1)
            g.sem_inc(sacc_ready, DC - 1)
            g.sem_inc(ql_ready, 1)
            g.wait_ge(ones_ready, 4)
            g.wait_ge(cq_ones, 1)
            q_split_pool(g, 0)
            with g.Fori(1, FOX_G) as G:
                g.wait_ge(f_scores, 8 * G)
                g.wait_ge(ql_ready, 2 * G + 1)
                g.tensor_copy(cq_cur[0:6], CQ[0:6, bass.ds(2 * G, 2)]).then_inc(cq_staged, 1)
                g.wait_ge(cq_staged, G + 1)
                q_split_pool(g, G)
            with g.Fori(FOX_G, GROUPS) as G:
                q_split_pool(g, G)
            g.wait_ge(ql_ready, 2 * GROUPS + 1)
            F_pool(g)
            g.wait_ge(rstd_ready, 2 * layers + 1)
            for i in range(DC - YD):
                g.wait_ge(xg_ready, i + 1)
                g.tensor_tensor(xg[i], xg[i], rstd[:], ALU.mult).then_inc(yg_out, 1)

        @block.scalar
        def _(act):
            act.wait_ge(fa_in, 16)
            act.activation(fa_h[:], fa_raw[:], ACT.Copy).then_inc(fa_hi, 1)
            act.wait_ge(small_in, 16)
            for j in range(DC):
                act_xh(act, j, LN_MIX + j, (x_in[j // 2], 16))
                if j % 2:
                    act.activation(x_square(j), x[:, j], ACT.Square).then_inc(x_sq[1], 1)
                if j == 1:
                    act_hi(act, 0, 0)
            act_hi(act, 1, 0)
            act_hi(act, 2, 0)
            act.wait_ge(ones_ready, 3)
            act_rsqrt(act, 0)
            act.wait_ge(const_in, 32)
            act.activation(cstb[:], const_stage[:, 0:C_LEV], ACT.Copy).then_inc(const_b, 1)
            act.activation(level_mask[:], const_stage[:, C_LEV:C_FIRST], ACT.Copy).then_inc(const_b, 1)
            for i in range(TB):
                act.activation(not_first[:, i * P:(i + 1) * P], const_stage[:, C_FIRST:NCONST], ACT.Copy).then_inc(const_b, 1)
            act.wait_ge(gate_step, 1)
            act.activation(za, z, ACT.Abs, bias=sm[0:8, BFG:BFG + 1]).then_inc(gate_act, 1)
            act.wait_ge(gate_act, 1)
            act.activation(za, za, ACT.Exp, scale=-1.0).then_inc(gate_act, 1)
            act.wait_ge(gate_act, 2)
            act.activation(za, za, ACT.Ln, bias=1.0).then_inc(gate_act, 1)
            act_hi(act, 0, 1)
            q_split_act(act, 0)
            k_split_act(act, 0)
            act.wait_ge(lam_sum, 1)
            act.activation(lamt[:, 2:4], OP[:, 0:2], ACT.Exp).then_inc(lam_exp, 1)
            with act.Fori(0, FOX_G) as g:
                fox_group_act(act, g)
            with act.Fori(0, DIFF_G - 1) as g:
                diff_group_act(act, g)
            diff_group_act(act, DIFF_G - 1, last=True)
            F_act(act)

        @block.vector
        def _(v):
            for s in (f_exp, f_turned, f_pv, d_exp, d_mix, d_turned, d_pts, d_pv):
                v.sem_inc(s, CR)
            for s in (s_exp, s_turned, s_pts, s_pv, h_cp, h_z, h_zread):
                v.sem_inc(s, CR)
            for s in (ol_ready, on_ready, rinv_ready, *f_pts, s_rinv, h_o, h_state, h_gated):
                v.sem_inc(s, 1)
            v.wait_ge(fa_hi, 1)
            v.tensor_tensor(fa_l[:], fa_raw[:], fa_h[:].bitcast(F32), ALU.subtract).then_inc(fa_lo, 1)
            v.wait_ge(small_in, 16)
            for j in range(DC):
                v.wait_ge(x_in[j // 2], 16)
                dve_xl(v, j, LN_MIX + j, j)
                if j == 1:
                    dve_lo(v, 0, 0)
            v.tensor_tensor(lamt[0:HD, 0:2], sm[0:HD, LAMB:LAMB + 2], sm[0:HD, LAMB + 2:LAMB + 4],
                            ALU.mult).then_inc(lam_prod, 1)
            dve_lo(v, 1, 0)
            dve_mean(v, 0)
            dve_lo(v, 2, 0)
            dve_newton(v, 0)
            v.wait_ge(rstd_ready, 1)
            v.wait_ge(fa_done, 1)
            v.tensor_tensor(z, acc[2][0:8, :], rstd[0:8, :], ALU.mult).then_inc(gate_step, 1)
            v.wait_ge(gate_step, 1)
            v.tensor_scalar(cum, z, sm[0:8, BFG:BFG + 1], 0.0, ALU.add, ALU.min).then_inc(gate_step, 1)
            dve_q(v, 0)
            dve_k(v, 0)
            v.wait_ge(gate_act, 3)
            v.wait_ge(gate_step, 2)
            v.tensor_tensor(z, cum, za, ALU.subtract).then_inc(gate_step, 1)
            v.wait_ge(gate_step, 3)
            v.tensor_tensor_scan(cum, z, z, 0.0, ALU.add, ALU.bypass).then_inc(gate_step, 1)
            v.wait_ge(gate_step, 4)
            v.tensor_copy(cpart[:, 0], cum).then_inc(gate_step, 1)
            v.wait_ge(gate_step, 5)
            v.tensor_scalar(cpartn[0][:, 0], cpart[:, 0], -1.0, None, ALU.mult).then_inc(gate_step, 1)
            v.tensor_tensor(z, cum, cpart[:, 0], ALU.subtract).then_inc(gate_step, 1)
            v.wait_ge(gate_step, 7)
            v.tensor_copy(cpart[:, 1], z).then_inc(gate_step, 1)
            v.wait_ge(gate_step, 8)
            v.tensor_scalar(cpartn[0][:, 1], cpart[:, 1], -1.0, None, ALU.mult).then_inc(gate_step, 1)
            v.tensor_tensor(cpart2[:, 0], z, cpart[:, 1], ALU.subtract).then_inc(gate_step, 1)
            v.wait_ge(gate_step, 10)
            v.tensor_scalar(cpartn[1][:, 0], cpart2[:, 0], -1.0, None, ALU.mult).then_inc(gate_step, 1)
            dve_lo(v, 0, 1)
            k_split_dve(v, 0)
            dve_v(v, 0)
            v.wait_ge(lam_exp, 1)
            v.tensor_tensor(lamt[:, 4:5], lamt[:, 3:4], lamt[:, 2:3], ALU.subtract).then_inc(lam_ready, 1)
            v.wait_ge(lam_ready, 1)
            v.tensor_scalar(lamt[:, 7:8], lamt[:, 4:5], -LAMBDA_INIT, None, ALU.add).then_inc(lam_ready, 1)
            v.tensor_scalar(dscale, sm[:, DIFFN:DIFFN + 1], 1.0 - LAMBDA_INIT, None, ALU.mult).then_inc(lam_ready, 1)
            v.wait_ge(cq_in, 16 * 6)
            v.tensor_copy(cq_cur[0:6], CQ[0:6, 0:2]).then_inc(cq_staged, 1)
            with v.Fori(0, FOX_G) as g:
                fox_group_dve(v, g)
            v.wait_ge(lam_ready, 3)
            with v.Fori(0, DIFF_G - 1) as g:
                diff_group_dve(v, g)
            diff_group_dve(v, DIFF_G - 1, last=True)
            F_dve(v)
            k = 2 * layers
            dve_mean(v, k)
            dve_newton(v, k)
            v.wait_ge(rstd_ready, k + 1)
            for j in range(YD):
                v.scalar_tensor_tensor(x[:, j], x[:, j], sm[:, LN_FIN + j:LN_FIN + j + 1], rstd[:],
                                       ALU.mult, ALU.mult).then_inc(y_out, 1)

        @block.tensor
        def _(pe):
            pe.wait_ge(ones_ready, 2)
            pe_stat_first(pe, 0)
            pe_stat_first(pe, 1)
            pe.wait_ge(fa_lo, 1)
            for c in range(DC):
                if c + 2 < DC:
                    pe_stat_first(pe, c + 2)
                pe.wait_ge(xl_ready, c + 1)
                a, b = fa_h[:, 8 * c:8 * c + 8], fa_l[:, 8 * c:8 * c + 8]
                pe.matmul(acc[2][0:8, :], a, xh[:, c], start=(c == 0), stop=False)
                pe.matmul(acc[2][0:8, :], a, xl[:, c], start=False, stop=False)
                mm = pe.matmul(acc[2][0:8, :], b, xh[:, c], start=False, stop=(c == DC - 1))
            mm.then_inc(fa_done, 1)
            pe_unit(pe, 0, 0, DC, xh, xl)
            pe_unit(pe, 1, 0, DC, xh, xl)
            pe.wait_ge(lam_prod, 1)
            pe.wait_ge(mean_ready, 1)
            pe.matmul(OP[:, 0:2], ones[0:HD, :], lamt[0:HD, 0:2], start=True, stop=True).then_inc(lam_sum, 1)
            pe.wait_ge(gate_step, 1)
            pe_unit(pe, 2, 0, DC, xh, xl)
            pe.wait_ge(const_b, 2 + TB)
            pe.wait_ge(cq_in, 16 * 6)
            with pe.Fori(0, FOX_G) as g:
                fox_group_pe(pe, g)
            with pe.Fori(0, DIFF_G - 1) as g:
                diff_group_pe(pe, g)
            diff_group_pe(pe, DIFF_G - 1, last=True)
            F_pe(pe)


def kernel(**inputs):
    import numpy as np
    import concourse.bacc as _bacc
    from concourse import mybir as _mybir
    from concourse.bass_utils import run_bass_kernel_spmd as _run
    layers = LAYERS

    a = {n: np.asarray(v) for n, v in inputs.items()}

    def tiles(w, cols, width=P):
        k = w.shape[0] // P
        return np.ascontiguousarray(np.stack([
            w[:, c:c + width].reshape(k, P, width).transpose(1, 0, 2).reshape(P, k * width) for c in cols]))

    def cols(v):
        return v.reshape(-1, P).T

    w = a["w_in_even"][0]
    starts = []
    for g in range(FOX_G):
        starts += [g * P, 512 + g * P, 1024 + g * P]
    for g in range(DIFF_G):
        starts += [1544 + g * P, 2056 + g * P, 2568 + g * P]
    small = np.zeros((P, NSMALL), np.float32)
    small[:, LN_MIX:LN_MIX + 16] = cols(a["ln_mix"])
    small[:, LN_FFN:LN_FFN + 16] = cols(a["ln_ffn"])
    small[:, LN_FIN:LN_FIN + 8] = cols(a["ln_final"])
    small[:, DIFFN:DIFFN + 1] = cols(a["diff_norm"])
    small[:, HGRNN:HGRNN + 1] = cols(a["hgrn_norm"])
    small[0:8, BFG] = a["b_forget"][0]
    for n, name in enumerate(("lambda_q1", "lambda_q2", "lambda_k1", "lambda_k2")):
        small[0:HD, LAMB + n] = a[name][0]
    small[:, SINK:SINK + 8] = a["sinks"]
    small[:, GAM:GAM + 8] = cols(a["hgrn_gamma"])
    def hgrn(h):
        return [768 + 512 * b + P * h for b in (1, 0, 3, 2)]
    odd_cols = [512, 0, 640, *hgrn(0)]
    for p in range(3):
        odd_cols += [P * (p + 1), *hgrn(p + 1)]
    gate, up, down = a["w_gate"], a["w_up"], a["w_down"]
    fcols = [t * P for t in range(FT)]
    ocols = [j * P for j in range(DC)]
    arrays = {
        "xT": np.ascontiguousarray(a["x"][0].T.reshape(DC, P, SEQ).transpose(1, 0, 2)),
        "small": small,
        "const": constants(),
        "w_even": tiles(w, starts),
        "w_fa": tiles(w, [1536], 8)[0],
        "w_out_e": tiles(a["w_out_even"][0], ocols),
        "w_odd": tiles(a["w_in_odd"][0], odd_cols),
        "w_out_o": tiles(a["w_out_odd"][0], ocols),
        "w_gu": np.stack([np.stack([tiles(gate[l], fcols), tiles(up[l], fcols)], 1) for l in range(2)]),
        "w_dn": np.stack([np.stack([tiles(down[l, h * FH * P:(h + 1) * FH * P], ocols) for h in range(2)])
                          for l in range(2)]),
    }
    nc = _bacc.Bacc("TRN2", target_bir_lowering=False, num_devices=1)
    args = [nc.dram_tensor(f"in_{n}", v.shape, _mybir.dt.from_np(v.dtype), kind="ExternalInput").ap()
            for n, v in arrays.items()]
    out = nc.dram_tensor("out", (P, DC, SEQ), F32, kind="ExternalOutput").ap()
    build(nc, layers, *args, out)
    r = _run(nc, [{f"in_{n}": v for n, v in arrays.items()}], core_ids=[0])
    y = r.results[0]["out"]
    return np.ascontiguousarray(y.transpose(2, 1, 0).reshape(1, SEQ, D))


LAYERS = 2
```
